# Optimizing a Trainium2 kernel written in Bass

```python
import math
import jax, jax.numpy as jnp
from jax import lax
import numpy as np

D_MODEL = 1024
BATCH = 1
SEQ = 1024
DEPTH = 1

ATT_HEADS = 12
ATT_HEAD_DIM = 64
ATT_WIDTH = ATT_HEADS * ATT_HEAD_DIM
DILATED_PATTERNS = ((128, 1), (512, 4), (2048, 16))
ATT_BLOCK = 128
ROPE_THETA = 10000.0

DN_HEADS = 6
DN_HEAD_DIM = 128
DN_WIDTH = DN_HEADS * DN_HEAD_DIM
CONV_WIDTH = 4
DN_CHUNK = 64

N_BRANCHES = 2

SPLIT_SIZES = (ATT_WIDTH, ATT_WIDTH, ATT_WIDTH,
               3 * DN_WIDTH,
               DN_HEADS,
               DN_HEADS,
               DN_WIDTH,
               N_BRANCHES * D_MODEL)
IN_COLS = sum(SPLIT_SIZES)

PEER_HEADS = 8
N_KEYS = 128
N_EXPERTS = N_KEYS * N_KEYS
PEER_QUERY_DIM = 256
PEER_HALF = PEER_QUERY_DIM // 2
PEER_TOPK = 16
PEER_TOKEN_BLOCK = 128

ALPHA = (2.0 * DEPTH) ** 0.25
BETA = (8.0 * DEPTH) ** -0.25
LN_EPS = 1e-5
RMS_EPS = 1e-6
NEG = -1e30

kernel_name = "hybrid_dilated_attn_gated_deltanet_peer_deepnorm"

f32 = jnp.float32

def layer_norm(x, gain, bias):
    xf = x.astype(f32)
    mu = jnp.mean(xf, axis=-1, keepdims=True)
    var = jnp.mean(jnp.square(xf - mu), axis=-1, keepdims=True)
    return ((xf - mu) * lax.rsqrt(var + LN_EPS) * gain.astype(f32) + bias.astype(f32)).astype(x.dtype)

def rope(x):
    S, d = x.shape[1], x.shape[-1]
    inv_freq = ROPE_THETA ** (-jnp.arange(0, d, 2, dtype=f32) / d)
    ang = jnp.arange(S, dtype=f32)[:, None] * inv_freq[None, :]
    cos = jnp.cos(ang)[None, :, None, :]
    sin = jnp.sin(ang)[None, :, None, :]
    x1, x2 = x[..., : d // 2], x[..., d // 2:]
    return jnp.concatenate([x1 * cos - x2 * sin, x1 * sin + x2 * cos], axis=-1)

def dilated_band_attention(q, k, v, dilation, band):
    B, S, H, d = q.shape
    L = S // dilation
    nb = -(-L // ATT_BLOCK)
    Lp = nb * ATT_BLOCK

    def to_sub(t, front):
        t = t.reshape(B, L, dilation, H, d).transpose(0, 2, 1, 3, 4)
        return jnp.pad(t, ((0, 0), (0, 0), (front, Lp - L), (0, 0), (0, 0)))

    qs = to_sub(q, 0).reshape(B, dilation, nb, ATT_BLOCK, H, d)

    def band_keys(t):
        tp = to_sub(t, ATT_BLOCK)
        prev = tp[:, :, :Lp].reshape(B, dilation, nb, ATT_BLOCK, H, d)
        cur = tp[:, :, ATT_BLOCK:].reshape(B, dilation, nb, ATT_BLOCK, H, d)
        return jnp.concatenate([prev, cur], axis=3)

    kb, vb = band_keys(k), band_keys(v)
    s = jnp.einsum('brnqhd,brnkhd->brnhqk', qs, kb) * (d ** -0.5)
    qi = jnp.arange(ATT_BLOCK)[:, None]
    kj = jnp.arange(2 * ATT_BLOCK)[None, :]
    dist = ATT_BLOCK + qi - kj
    key_pos = jnp.arange(nb)[:, None, None] * ATT_BLOCK + kj[None] - ATT_BLOCK
    mask = (dist >= 0) & (dist <= band) & (key_pos >= 0)
    s = jnp.where(mask[:, None], s, NEG)
    m = jnp.max(s, axis=-1, keepdims=True)
    lse = m[..., 0] + jnp.log(jnp.sum(jnp.exp(s - m), axis=-1))
    p = jnp.exp(s - lse[..., None])
    o = jnp.einsum('brnhqk,brnkhd->brnqhd', p, vb)
    o = o.reshape(B, dilation, Lp, H, d)[:, :, :L].transpose(0, 2, 1, 3, 4).reshape(B, S, H, d)
    lse = lse.transpose(0, 1, 2, 4, 3).reshape(B, dilation, Lp, H)[:, :, :L]
    lse = lse.transpose(0, 2, 1, 3).reshape(B, S, H)
    return o, lse

def dilated_attention(q, k, v):
    outs, lses = [], []
    for window, dilation in DILATED_PATTERNS:
        o, l = dilated_band_attention(q, k, v, dilation, window // dilation)
        outs.append(o)
        lses.append(l)
    outs = jnp.stack(outs, axis=3)
    wts = jax.nn.softmax(jnp.stack(lses, axis=-1), axis=-1)
    return jnp.einsum('bshg,bshgd->bshd', wts, outs)

def causal_depthwise_conv(x, w):
    return lax.conv_general_dilated(x, w[:, None, :], window_strides=(1,),
                                    padding=[(CONV_WIDTH - 1, 0)],
                                    dimension_numbers=('NWC', 'WIO', 'NWC'),
                                    feature_group_count=x.shape[-1])

def l2norm(x):
    return x * lax.rsqrt(jnp.sum(jnp.square(x), axis=-1, keepdims=True) + RMS_EPS)

def gated_delta_rule(q, k, v, g, beta):
    B, S, H, dk = q.shape
    dv = v.shape[-1]
    C = DN_CHUNK
    n = S // C

    def chunks(t):
        return jnp.swapaxes(t.reshape((B, n, C, H) + t.shape[3:]), 2, 3)

    qc, kc, vc, gc, bc = chunks(q), chunks(k), chunks(v), chunks(g), chunks(beta)
    G = jnp.cumsum(gc, axis=-1)
    idx = jnp.arange(C)
    lower = idx[:, None] >= idx[None, :]
    strict = idx[:, None] > idx[None, :]
    decay_mat = jnp.exp(jnp.where(lower, G[..., :, None] - G[..., None, :], NEG))
    kk = jnp.einsum('bnhid,bnhjd->bnhij', kc, kc)
    M = jnp.where(strict, bc[..., None] * kk * decay_mat, 0.0)
    eye = jnp.eye(C, dtype=f32)
    T = lax.linalg.triangular_solve(eye + M, jnp.broadcast_to(eye, M.shape), left_side=True,
                                    lower=True, unit_diagonal=True)
    u = T @ (bc[..., None] * vc)
    w = T @ (bc[..., None] * kc * jnp.exp(G)[..., None])
    qk = jnp.einsum('bnhid,bnhjd->bnhij', qc, kc) * decay_mat
    q_dec = qc * jnp.exp(G)[..., None]
    k_dec = kc * jnp.exp(G[..., -1:] - G)[..., None]
    g_last = jnp.exp(G[..., -1])

    def step(state, inp):
        u_i, w_i, qk_i, qd_i, kd_i, gl_i = inp
        v_new = u_i - jnp.einsum('bhcd,bhde->bhce', w_i, state)
        o_i = jnp.einsum('bhcd,bhde->bhce', qd_i, state) + jnp.einsum('bhij,bhje->bhie', qk_i, v_new)
        state = gl_i[..., None, None] * state + jnp.einsum('bhcd,bhce->bhde', kd_i, v_new)
        return state, o_i

    xs = (u, w, qk, q_dec, k_dec, g_last)
    xs = tuple(jnp.moveaxis(t, 1, 0) for t in xs)
    _, o = lax.scan(step, jnp.zeros((B, H, dk, dv), f32), xs)
    o = jnp.moveaxis(o, 0, 1)
    return jnp.swapaxes(o, 2, 3).reshape(B, S, H, dv)

def mixing_sublayer(x, w_in, dn_conv, dn_A_log, dn_dt_bias, dn_norm_gain,
                    w_branch_attn, w_branch_delta, w_out):
    B, S, _ = x.shape
    h = x @ w_in
    points, acc = [], 0
    for sz in SPLIT_SIZES[:-1]:
        acc += sz
        points.append(acc)
    q_a, k_a, v_a, qkv_b, beta_in, a_in, gate_b, br_gate = jnp.split(h, points, axis=-1)

    qa = rope(q_a.astype(f32).reshape(B, S, ATT_HEADS, ATT_HEAD_DIM))
    ka = rope(k_a.astype(f32).reshape(B, S, ATT_HEADS, ATT_HEAD_DIM))
    va = v_a.astype(f32).reshape(B, S, ATT_HEADS, ATT_HEAD_DIM)
    y_a = dilated_attention(qa, ka, va).reshape(B, S, ATT_WIDTH).astype(x.dtype)

    qkv = jax.nn.silu(causal_depthwise_conv(qkv_b, dn_conv)).astype(f32)
    qb, kb, vb = jnp.split(qkv, 3, axis=-1)
    qb = l2norm(qb.reshape(B, S, DN_HEADS, DN_HEAD_DIM)) * (DN_HEAD_DIM ** -0.5)
    kb = l2norm(kb.reshape(B, S, DN_HEADS, DN_HEAD_DIM))
    vb = vb.reshape(B, S, DN_HEADS, DN_HEAD_DIM)
    beta = jax.nn.sigmoid(beta_in.astype(f32))
    g = -jnp.exp(dn_A_log.astype(f32)) * jax.nn.softplus(a_in.astype(f32) + dn_dt_bias.astype(f32))
    ob = gated_delta_rule(qb, kb, vb, g, beta)
    ob = ob * lax.rsqrt(jnp.mean(jnp.square(ob), axis=-1, keepdims=True) + RMS_EPS) * dn_norm_gain.astype(f32)
    ob = ob.reshape(B, S, DN_WIDTH) * jax.nn.silu(gate_b.astype(f32))
    y_b = ob.astype(x.dtype)

    gates = jax.nn.sigmoid(br_gate.astype(f32)).reshape(B, S, N_BRANCHES, D_MODEL)
    merged = gates[:, :, 0] * (y_a @ w_branch_attn).astype(f32) + gates[:, :, 1] * (y_b @ w_branch_delta).astype(f32)
    return merged.astype(x.dtype) @ w_out

def peer_sublayer(x, w_query, sub_keys, expert_down, expert_up):
    B, S, D = x.shape
    T = B * S
    t = x.reshape(T, D)
    q = (t @ w_query).reshape(T, PEER_HEADS, 2, PEER_HALF)
    s = jnp.einsum('thpc,hpkc->thpk', q, sub_keys).astype(f32)
    top_s, top_i = lax.top_k(s, PEER_TOPK)
    cand_s = (top_s[:, :, 0, :, None] + top_s[:, :, 1, None, :]).reshape(T, PEER_HEADS, PEER_TOPK * PEER_TOPK)
    cand_i = (top_i[:, :, 0, :, None] * N_KEYS + top_i[:, :, 1, None, :]).reshape(T, PEER_HEADS, PEER_TOPK * PEER_TOPK)
    best_s, best_j = lax.top_k(cand_s, PEER_TOPK)
    experts = jnp.take_along_axis(cand_i, best_j, axis=-1)
    gate = jax.nn.softmax(best_s, axis=-1)

    def token_block(args):
        xb, eb, gb = args
        act = jax.nn.gelu(jnp.einsum('pd,phkd->phk', xb, expert_down[eb]).astype(f32), approximate=False)
        return jnp.einsum('phk,phkd->pd', (gb * act).astype(x.dtype), expert_up[eb])

    nblk = T // PEER_TOKEN_BLOCK
    y = lax.map(token_block, (t.reshape(nblk, PEER_TOKEN_BLOCK, D),
                              experts.reshape(nblk, PEER_TOKEN_BLOCK, PEER_HEADS, PEER_TOPK),
                              gate.reshape(nblk, PEER_TOKEN_BLOCK, PEER_HEADS, PEER_TOPK)))
    return y.reshape(B, S, D)

def setup_inputs(seed: int = 0) -> dict:
    key = jax.random.key(seed)
    ks = jax.random.split(key, 18)
    nrm = jax.random.normal
    dt = jnp.exp(jax.random.uniform(ks[4], (DEPTH, DN_HEADS), f32) * (math.log(0.1) - math.log(0.001)) + math.log(0.001))
    return {
        "x": nrm(ks[0], (BATCH, SEQ, D_MODEL), f32),
        "w_in": nrm(ks[1], (DEPTH, D_MODEL, IN_COLS), f32) * D_MODEL ** -0.5,
        "dn_conv": nrm(ks[2], (DEPTH, CONV_WIDTH, 3 * DN_WIDTH), f32) * CONV_WIDTH ** -0.5,
        "dn_A_log": jnp.log(jax.random.uniform(ks[3], (DEPTH, DN_HEADS), f32, 1.0, 16.0)),
        "dn_dt_bias": dt + jnp.log(-jnp.expm1(-dt)),
        "dn_norm_gain": 1.0 + 0.02 * nrm(ks[5], (DEPTH, DN_HEAD_DIM), f32),
        "w_branch_attn": nrm(ks[6], (DEPTH, ATT_WIDTH, D_MODEL), f32) * ATT_WIDTH ** -0.5,
        "w_branch_delta": nrm(ks[7], (DEPTH, DN_WIDTH, D_MODEL), f32) * DN_WIDTH ** -0.5,
        "w_out": nrm(ks[8], (DEPTH, D_MODEL, D_MODEL), f32) * (D_MODEL ** -0.5) * BETA,
        "ln1_gain": 1.0 + 0.02 * nrm(ks[9], (DEPTH, D_MODEL), f32),
        "ln1_bias": 0.02 * nrm(ks[10], (DEPTH, D_MODEL), f32),
        "peer_w_query": nrm(ks[11], (DEPTH, D_MODEL, PEER_HEADS * PEER_QUERY_DIM), f32) * D_MODEL ** -0.5,
        "peer_sub_keys": nrm(ks[12], (DEPTH, PEER_HEADS, 2, N_KEYS, PEER_HALF), f32) * PEER_HALF ** -0.5,
        "peer_expert_down": nrm(ks[13], (DEPTH, N_EXPERTS, D_MODEL), f32) * D_MODEL ** -0.5,
        "peer_expert_up": nrm(ks[14], (DEPTH, N_EXPERTS, D_MODEL), f32) * BETA,
        "ln2_gain": 1.0 + 0.02 * nrm(ks[15], (DEPTH, D_MODEL), f32),
        "ln2_bias": 0.02 * nrm(ks[16], (DEPTH, D_MODEL), f32),
    }

def reference(x, w_in, dn_conv, dn_A_log, dn_dt_bias, dn_norm_gain, w_branch_attn, w_branch_delta,
              w_out, ln1_gain, ln1_bias, peer_w_query, peer_sub_keys, peer_expert_down, peer_expert_up,
              ln2_gain, ln2_bias):
    for layer in range(DEPTH):
        mix = mixing_sublayer(x, w_in[layer], dn_conv[layer], dn_A_log[layer], dn_dt_bias[layer],
                              dn_norm_gain[layer], w_branch_attn[layer], w_branch_delta[layer], w_out[layer])
        x = layer_norm(ALPHA * x + mix, ln1_gain[layer], ln1_bias[layer])
        ffn = peer_sublayer(x, peer_w_query[layer], peer_sub_keys[layer], peer_expert_down[layer],
                            peer_expert_up[layer])
        x = layer_norm(ALPHA * x + ffn, ln2_gain[layer], ln2_bias[layer])
    return x


_drawn_inputs = setup_inputs


def setup_inputs(seed=0):
    import zlib

    import numpy as np

    out = dict(_drawn_inputs(seed))
    spreads = {}
    factors = {'dn_norm_gain': 3.44, 'ln2_gain': 2.862, 'ln2_bias': 2.858}
    for name, (base, spread) in spreads.items():
        noise = np.random.default_rng([zlib.crc32(name.encode()), seed]).standard_normal(out[name].shape)
        drawn = base * np.exp(spread * noise) if base else spread * noise
        out[name] = __import__('jax').numpy.asarray(drawn.astype(out[name].dtype))
    for name, factor in factors.items():
        out[name] = (out[name] * factor).astype(out[name].dtype)
    return out
```

```python
import math

import numpy as np

import concourse.bass as bass
from concourse import mybir
from contextlib import ExitStack, contextmanager

F32 = mybir.dt.float32
F32R = mybir.dt.float32r
U32 = mybir.dt.uint32
ALU = mybir.AluOpType
ACT = mybir.ActivationFunctionType
AX = mybir.AxisListType

P = 128
D = 1024
T = 1024
KD = D // P
TT = T // P
HALF = 512
AH, AD = 12, 64
AW = AH * AD
AT = AW // P
DH, DD = 6, 128
DW = DH * DD
CONV = 4
N_ATT = 3 * AT
N_DN = 3 * DH
N_GB = DH
N_BR = 2 * KD
N_IN = N_ATT + N_DN + N_GB + N_BR
PH, PK, TOP = 8, 128, 16
ALPHA = 2.0 ** 0.25
NEG = -1e30


class Step:

    def __init__(self, sem, base=0):
        self.sem, self.base, self.n = sem, base, 0

    def inc(self, ins, by=1):
        self.n += by
        ins.then_inc(self.sem, by)
        return self.at()

    def at(self, back=0):
        return self.base + (self.n - back)

    def wait(self, eng, back=0):
        eng.wait_ge(self.sem, self.at(back))


@contextmanager
def stage_semaphores(nc, prefix):
    held = {}

    def sem(name):
        if name not in held:
            held[name] = nc.alloc_semaphore(f"{prefix}_{name}")
        return held[name]

    yield sem
    nc.clear_and_free_semaphores(list(held.values()))
    nc.all_engine_barrier()


def wait_alone(eng, sem, value, passed):
    eng.wait_ge(sem, value)
    eng.sem_inc(passed, 1)


def stage_project(nc, g):
    with ExitStack() as ctx:
        def sb(name, shape, dt=F32):
            return ctx.enter_context(nc.sbuf_tensor(name, shape, dt))

        sem = ctx.enter_context(stage_semaphores(nc, "p"))

        xh, xl = sb("p_xh", [P, KD, T], F32R), sb("p_xl", [P, KD, T], F32R)
        xraw = [sb(f"p_xraw{u}", [P, T]) for u in range(2)]
        wraw = [sb(f"p_wraw{u}", [P, KD, P]) for u in range(2)]
        wh = [sb(f"p_wh{u}", [P, KD, P], F32R) for u in range(2)]
        wl = [sb(f"p_wl{u}", [P, KD, P], F32R) for u in range(2)]
        cin = [sb(f"p_cin{u}", [P, CONV - 1 + T]) for u in range(2)]
        cout = [sb(f"p_cout{u}", [P, T]) for u in range(2)]
        out = [sb(f"p_out{u}", [P, T]) for u in range(2)]
        cw = sb("p_cw", [P, N_DN, CONV])
        wba = sb("p_wba", [P, KD, 2 * DH])
        ba = sb("p_ba", [P, TT, 2 * DH])
        xba = sb("p_xba", [P, KD, T])
        ps = [ctx.enter_context(nc.psum_tensor(f"p_ps{u}", [P, T], F32)) for u in range(2)]
        psb = ctx.enter_context(nc.psum_tensor("p_psb", [P, HALF], F32))

        ld_x = [sem(f"ld_x{u}") for u in range(2)]
        ld_w = [sem(f"ld_w{u}") for u in range(2)]
        ld_c = sem("ld_c")
        x_hi, x_lo = sem("x_hi"), sem("x_lo")
        w_hi, w_lo = sem("w_hi"), sem("w_lo")
        mm_done = sem("mm_done")
        ba_done, ba_out, ba_st = sem("ba_done"), sem("ba_out"), sem("ba_st")
        out_ready = sem("out_ready")
        cin_ready, cout_ready, conv_step = sem("cin_ready"), sem("cout_ready"), sem("conv_step")
        zeroed = sem("zeroed")
        stored = [sem(f"stored{u}") for u in range(2)]
        block = ctx.enter_context(nc.Block())
        pairs = N_IN // 2
        att, dn, gb = N_ATT // 2, N_DN // 2, N_GB // 2

        @block.sync
        def _(sp):
            for k in range(KD):
                if k >= 2:
                    sp.wait_ge(x_lo, k - 1)
                sp.dma_start(xraw[k % 2][:], g.xT[k * P:(k + 1) * P, :]).then_inc(ld_x[k % 2], 16)
                if k < 2:
                    sp.dma_start(wraw[k][:], g.w_in[k]).then_inc(ld_w[k], 16)
            sp.dma_start(wba[:], g.w_ba.rearrange("(k p) c -> p k c", p=P)).then_inc(ld_c, 16)
            sp.dma_start(cw[:], g.conv).then_inc(ld_c, 16)
            sp.dma_start(xba[:], g.xT.rearrange("(k p) t -> p k t", p=P)).then_inc(ld_c, 16)
            with sp.Fori(0, pairs - 1) as i:
                for u in range(2):
                    sp.wait_ge(w_lo, 2 * i + (u + 1))
                    sp.dma_start(wraw[u][:], g.w_in[bass.ds(2 * i + (2 + u), 1)].rearrange("o p k c -> (o p) k c")).then_inc(ld_w[u], 16)

        @block.scalar
        def _(act):
            for k in range(KD):
                act.wait_ge(ld_x[k % 2], 16 * (k // 2 + 1))
                nc.scalar.copy(xh[:, k, :], xraw[k % 2][:]).then_inc(x_hi, 1)

            def split(u, n):
                act.wait_ge(ld_w[u], n)
                nc.scalar.copy(wh[u][:], wraw[u][:]).then_inc(w_hi, 1)

            split(0, 16)
            split(1, 16)

            def body(i, kind, last=False):
                for u in range(2):
                    act.wait_ge(mm_done, 2 * i + (u + 1))
                    if kind == "conv":
                        j = i - att
                        act.wait_ge(cout_ready, 2 * j + u)
                        nc.scalar.copy(cin[u][:, CONV - 1:], ps[u][:]).then_inc(cin_ready, 1)
                    else:
                        act.wait_ge(stored[u], 16 * i)
                        f = {"att": ACT.Copy, "gb": ACT.Silu, "br": ACT.Sigmoid}[kind]
                        nc.scalar.activation(out[u][:], ps[u][:], f).then_inc(out_ready, 1)
                    if not last:
                        split(u, 16 * i + 32)
                    if kind == "conv":
                        act.wait_ge(cout_ready, 2 * j + (u + 1))
                        act.wait_ge(stored[u], 16 * i)
                        nc.scalar.activation(out[u][:], cout[u][:], ACT.Silu).then_inc(out_ready, 1)

            act.wait_ge(zeroed, 2)
            with act.Fori(0, att) as i:
                body(i, "att")
            with act.Fori(att, att + dn) as i:
                body(i, "conv")
            with act.Fori(att + dn, att + dn + gb) as i:
                body(i, "gb")
            with act.Fori(att + dn + gb, pairs - 1) as i:
                body(i, "br")
            body(pairs - 1, "br", last=True)

        @block.vector
        def _(dve):
            nc.vector.memset(cin[0][:, 0:CONV - 1], 0.0).then_inc(zeroed, 1)
            nc.vector.memset(cin[1][:, 0:CONV - 1], 0.0).then_inc(zeroed, 1)
            for k in range(KD):
                dve.wait_ge(x_hi, k + 1)
                nc.vector.tensor_tensor(xl[:, k, :], xraw[k % 2][:], xh[:, k, :].bitcast(F32), ALU.subtract).then_inc(x_lo, 1)

            def split(u, n):
                dve.wait_ge(w_hi, n)
                nc.vector.tensor_tensor(wl[u][:], wraw[u][:], wh[u][:].bitcast(F32), ALU.subtract).then_inc(w_lo, 1)

            split(0, 1)
            split(1, 2)
            dve.wait_ge(ba_done, 1)
            nc.vector.tensor_copy(ba[:], psb[:, 0:TT * 2 * DH].rearrange("p (t c) -> p t c", t=TT)).then_inc(ba_out, 1)
            dve.wait_ge(ld_c, 48)

            def body(i, conv):
                for u in range(2):
                    if conv:
                        j = i - att
                        step = Step(conv_step, 6 * j + 3 * u)
                        dve.wait_ge(cin_ready, 2 * j + (u + 1))
                        dve.wait_ge(out_ready, 2 * i + u)
                        w = [cw[:, bass.ds(2 * j + u, 1), t:t + 1].rearrange("p a b -> p (a b)") for t in range(CONV)]
                        step.inc(nc.vector.tensor_scalar(cout[u][:], cin[u][:, 0:T], w[0], None, ALU.mult))
                        for t in range(1, CONV):
                            step.wait(dve)
                            ins = nc.vector.scalar_tensor_tensor(cout[u][:], cin[u][:, t:t + T], w[t], cout[u][:],
                                                                 ALU.mult, ALU.add)
                            if t < CONV - 1:
                                step.inc(ins)
                        ins.then_inc(cout_ready, 1)
                    split(u, 2 * i + (u + 3))

            with dve.Fori(0, att) as i:
                body(i, False)
            with dve.Fori(att, att + dn) as i:
                body(i, True)
            with dve.Fori(att + dn, pairs - 1) as i:
                body(i, False)

        @block.tensor
        def _(pe):
            pe.wait_ge(ld_c, 48)
            for t in range(TT):
                for k in range(KD):
                    ins = nc.tensor.matmul(psb[:, t * 2 * DH:(t + 1) * 2 * DH], xba[:, k, t * P:(t + 1) * P],
                                           wba[:, k, :], start=(k == 0), stop=(k == KD - 1))
            ins.then_inc(ba_done, 1)
            pe.wait_ge(x_lo, KD)
            with pe.Fori(0, pairs) as i:
                for u in range(2):
                    pe.wait_ge(w_lo, 2 * i + (u + 1))
                    for h in range(2):
                        o = ps[u][:, h * HALF:(h + 1) * HALF]
                        for k in range(KD):
                            for n, (a, b) in enumerate(((wh, xh), (wh, xl), (wl, xh))):
                                ins = nc.tensor.matmul(o, a[u][:, k, :], b[:, k, h * HALF:(h + 1) * HALF],
                                                       start=(k == 0 and n == 0), stop=(k == KD - 1 and n == 2))
                    ins.then_inc(mm_done, 1)

        @block.gpsimd
        def _(pool):
            pool.wait_ge(ba_out, 1)
            pool.dma_start(g.ba, ba[:]).then_inc(ba_st, 16)
            with pool.Fori(0, pairs) as i:
                for u in range(2):
                    pool.wait_ge(out_ready, 2 * i + (u + 1))
                    pool.dma_start(g.hT[bass.ds(2 * i + u, 1)].rearrange("o p t -> (o p) t"), out[u][:]).then_inc(stored[u], 16)
            pool.wait_ge(ba_st, 16)
            for u in range(2):
                pool.wait_ge(stored[u], 16 * pairs)


def stage_attention(nc, g):
    HPT = P // AD
    ITEMS = HPT * TT
    groups = [1 + qt // 4 for qt in range(TT)] * HPT
    through = [sum(groups[:n + 1]) for n in range(ITEMS)]
    G = sum(groups)
    with ExitStack() as ctx:
        def sb(name, shape, dt=F32):
            return ctx.enter_context(nc.sbuf_tensor(name, shape, dt))

        sem = ctx.enter_context(stage_semaphores(nc, "a"))

        cos, sin = sb("a_cos", [P, T]), sb("a_sin", [P, T])
        bias, ident = sb("a_bias", [P, T]), sb("a_ident", [P, P])
        vT, V = sb("a_vT", [P, AT, T]), sb("a_V", [P, TT, AW])
        raw = [sb(f"a_raw{n}", [P, T]) for n in range(4)]
        q, k = sb("a_q", [P, T]), sb("a_k", [P, T])
        sc = [sb(f"a_sc{u}", [P, T]) for u in range(2)]
        pb = [sb(f"a_pb{u}", [P, T]) for u in range(2)]
        pT = [sb(f"a_pT{u}", [P, TT, P]) for u in range(2)]
        ya, yaT = sb("a_ya", [P, TT, AW]), sb("a_yaT", [P, AT, T])
        mx, nm = sb("a_mx", [P, ITEMS]), sb("a_nm", [P, ITEMS])
        rs, ri = sb("a_rs", [P, ITEMS]), sb("a_ri", [P, ITEMS])
        psS = [ctx.enter_context(nc.psum_tensor(f"a_psS{u}", [P, T], F32)) for u in range(2)]
        psT = [ctx.enter_context(nc.psum_tensor(f"a_psT{u}", [P, HALF], F32)) for u in range(2)]
        psO = [ctx.enter_context(nc.psum_tensor(f"a_psO{u}", [P, HALF], F32)) for u in range(2)]

        ld_c, ld_v, ld_q = sem("ld_c"), sem("ld_v"), sem("ld_q")
        v_tr, v_out = sem("v_tr"), sem("v_out")
        rope_step, rope_done = sem("rope_step"), sem("rope_done")
        s_done, masked, max_ready = sem("s_done"), sem("masked"), sem("max_ready")
        exp_done, tr_done, pT_ready = sem("exp_done"), sem("tr_done"), sem("pT_ready")
        pv_done, recip_done, o_out = sem("pv_done"), sem("recip_done"), sem("o_out")
        y_tr, y_out, passed, stored = sem("y_tr"), sem("y_out"), sem("passed"), sem("stored")
        block = ctx.enter_context(nc.Block())

        def evac(act, i, n, grp):
            qt = n % TT
            for b in range(groups[n]):
                act.wait_ge(tr_done, G * i + (grp + 1))
                act.wait_ge(pv_done, ITEMS * i + max(n - 1, 0))
                w = min(4, qt + 1 - 4 * b)
                nc.scalar.copy(pT[n % 2][:, 4 * b:4 * b + w, :],
                               psT[grp % 2][:, 0:w * P].rearrange("p (a t) -> p a t", t=P)).then_inc(pT_ready, 1)
                grp += 1
            return grp

        @block.sync
        def _(sp):
            sp.dma_start(vT[:], g.hT[2 * AT:3 * AT].rearrange("n p t -> p n t")).then_inc(ld_v, 16)
            for d, s in ((ident, g.ident), (cos, g.cos), (sin, g.sin), (bias, g.bias)):
                sp.dma_start(d[:], s).then_inc(ld_c, 16)
            with sp.Fori(0, AT) as i:
                sp.wait_ge(rope_done, i * 2)
                for n, first in ((0, 0), (2, AT)):
                    src = g.hT[bass.ds(i + first, 1)].rearrange("o p t -> (o p) t")
                    sp.dma_start(raw[n][:], src).then_inc(ld_q, 16)
                    for r in range(4):
                        s = r ^ 1
                        sp.dma_start(raw[n + 1][32 * r:32 * r + 32, :], src[32 * s:32 * s + 32, :]).then_inc(ld_q, 16)
            sp.wait_ge(y_out, 2 * TT)
            sp.dma_start(g.y[0:AT].rearrange("n p t -> p n t"), yaT[:]).then_inc(stored, 16)
            sp.wait_ge(stored, 16)

        @block.scalar
        def _(act):
            with act.Fori(0, AT) as i:
                grp = 0
                for n in range(ITEMS):
                    N = (n % TT + 1) * P
                    act.wait_ge(max_ready, ITEMS * i + (n + 1))
                    act.wait_ge(tr_done, G * i + (through[n - 2] if n >= 2 else 0))
                    nc.scalar.activation(pb[n % 2][:, 0:N], sc[n % 2][:, 0:N], ACT.Exp, bias=nm[:, n:n + 1],
                                         accum_out=rs[:, n:n + 1]).then_inc(exp_done, 1)
                    if n >= 1:
                        grp = evac(act, i, n - 1, grp)
                grp = evac(act, i, ITEMS - 1, grp)

        @block.vector
        def _(dve):
            for kb in range(TT):
                for h in range(2):
                    n = 2 * kb + h
                    dve.wait_ge(v_tr, n + 1)
                    nc.vector.tensor_copy(V[:, kb, h * 384:(h + 1) * 384], psT[h][:, 0:384]).then_inc(v_out, 1)
            dve.wait_ge(ld_c, 64)
            with dve.Fori(0, AT) as i:
                dve.wait_ge(ld_q, 160 * (i + 1))
                step = Step(rope_step, 4 * i)
                for n, o in ((0, q), (2, k)):
                    nc.vector.tensor_tensor(o[:], raw[n][:], cos[:], ALU.mult)
                    step.inc(nc.vector.tensor_tensor(raw[n + 1][:], raw[n + 1][:], sin[:], ALU.mult), 2)
                    step.wait(dve)
                    nc.vector.tensor_tensor(o[:], o[:], raw[n + 1][:], ALU.add).then_inc(rope_done, 1)

                def out(n):
                    h, qt = n // TT, n % TT
                    dve.wait_ge(exp_done, ITEMS * i + (n + 1))
                    nc.vector.reciprocal(ri[:, n:n + 1], rs[:, n:n + 1]).then_inc(recip_done, 1)
                    dve.wait_ge(recip_done, ITEMS * i + (n + 1))
                    dve.wait_ge(pv_done, ITEMS * i + (n + 1))
                    nc.vector.tensor_scalar(ya[:, qt, bass.ds(i * P + h * AD, AD)], psO[n % 2][:, 0:AD],
                                            ri[:, n:n + 1], None, ALU.mult).then_inc(o_out, 1)

                for n in range(ITEMS):
                    qt = n % TT
                    N = (qt + 1) * P
                    dve.wait_ge(exp_done, ITEMS * i + max(n - 1, 0))
                    wait_alone(dve, s_done, ITEMS * i + (n + 1), passed)
                    nc.vector.tensor_tensor_reduce(out=sc[n % 2][:, 0:N], in0=psS[n % 2][:, 0:N],
                                                   in1=bias[:, T - N:T], scale=AD ** -0.5, scalar=NEG,
                                                   op0=ALU.add, op1=ALU.max,
                                                   accum_out=mx[:, n:n + 1]).then_inc(masked, 1)
                    dve.wait_ge(masked, ITEMS * i + (n + 1))
                    nc.vector.tensor_scalar(nm[:, n:n + 1], mx[:, n:n + 1], -1.0, None, ALU.mult).then_inc(max_ready, 1)
                    if n >= 2:
                        out(n - 2)
                out(ITEMS - 2)
                out(ITEMS - 1)
            for kb in range(TT):
                for h in range(2):
                    n = 2 * kb + h
                    dve.wait_ge(y_tr, n + 1)
                    nc.vector.tensor_copy(yaT[:, 3 * h:3 * h + 3, kb * P:(kb + 1) * P],
                                          psT[h][:, 0:384].rearrange("p (a t) -> p a t", t=P)).then_inc(y_out, 1)

        @block.tensor
        def _(pe):
            pe.wait_ge(ld_c, 64)
            pe.wait_ge(ld_v, 16)
            for kb in range(TT):
                for h in range(2):
                    n = 2 * kb + h
                    if n >= 2:
                        pe.wait_ge(v_out, n - 1)
                    for a in range(3):
                        ins = nc.tensor.transpose(psT[h][:, a * P:(a + 1) * P], vT[:, 3 * h + a, kb * P:(kb + 1) * P], ident[:])
                    ins.then_inc(v_tr, 1)
            pe.wait_ge(v_out, 2 * TT)

            with pe.Fori(0, AT) as i:
                def scores(n):
                    h, qt = n // TT, n % TT
                    N = (qt + 1) * P
                    pe.wait_ge(masked, ITEMS * i + max(n - 1, 0))
                    for a in range(0, N, HALF):
                        b = min(a + HALF, N)
                        ins = nc.tensor.matmul(psS[n % 2][:, a:b], q[h * AD:(h + 1) * AD, qt * P:(qt + 1) * P],
                                               k[h * AD:(h + 1) * AD, a:b], start=True, stop=True)
                    ins.then_inc(s_done, 1)

                def values(n):
                    h, qt = n // TT, n % TT
                    pe.wait_ge(pT_ready, G * i + through[n])
                    pe.wait_ge(o_out, ITEMS * i + max(n - 1, 0))
                    for kb in range(qt + 1):
                        ins = nc.tensor.matmul(psO[n % 2][:, 0:AD], pT[n % 2][:, kb, :],
                                               V[:, kb, bass.ds(i * P + h * AD, AD)], start=(kb == 0), stop=(kb == qt))
                    ins.then_inc(pv_done, 1)

                pe.wait_ge(rope_done, 2 * i + 2)
                scores(0)
                grp = 0
                for n in range(ITEMS):
                    if n + 1 < ITEMS:
                        scores(n + 1)
                    pe.wait_ge(exp_done, ITEMS * i + (n + 1))
                    for b in range(groups[n]):
                        pe.wait_ge(pT_ready, G * i + max(grp - 1, 0))
                        for kb in range(4 * b, min(4 * b + 4, n % TT + 1)):
                            ins = nc.tensor.transpose(psT[grp % 2][:, kb % 4 * P:(kb % 4 + 1) * P],
                                                      pb[n % 2][:, kb * P:(kb + 1) * P], ident[:])
                        ins.then_inc(tr_done, 1)
                        grp += 1
                    if n >= 1:
                        values(n - 1)
                values(ITEMS - 1)
            pe.wait_ge(o_out, ITEMS * AT)
            for kb in range(TT):
                for h in range(2):
                    n = 2 * kb + h
                    if n >= 2:
                        pe.wait_ge(y_out, n - 1)
                    for a in range(3):
                        ins = nc.tensor.transpose(psT[h][:, a * P:(a + 1) * P], ya[:, kb, (3 * h + a) * P:(3 * h + a + 1) * P], ident[:])
                    ins.then_inc(y_tr, 1)


def stage_deltanet(nc, g):
    C = P
    NC = T // C
    HH = DH // 2
    W = HH * P
    LEVELS = 7
    with ExitStack() as ctx:
        def sb(name, shape, dt=F32):
            return ctx.enter_context(nc.sbuf_tensor(name, shape, dt))

        def full(name):
            return sb(name, [P, 2, HH, P])

        sem = ctx.enter_context(stage_semaphores(nc, "d"))

        ident, upto, later = sb("d_ident", [P, P]), sb("d_upto", [P, P]), sb("d_later", [P, P])
        level = sb("d_level", [P, LEVELS, P])
        ones, half_power = sb("d_ones", [P, P]), sb("d_half_power", [P, 2 * DH])
        ba, z = sb("d_ba", [P, NC, 2 * DH]), sb("d_z", [P, NC, DH])
        neg_a, dtb, gain = sb("d_neg_a", [P, DH]), sb("d_dtb", [P, DH]), sb("d_gain", [P, 1])
        ez, gg = sb("d_ez", [P, NC, DH]), sb("d_gg", [P, NC, DH])
        beta, eG, eK, gl = (sb(f"d_{n}", [P, NC, DH]) for n in ("beta", "eG", "eK", "gl"))
        Gs = sb("d_Gs", [P, NC, DH])
        gB = full("d_gB")
        cbeta, ceG, ceK, cgl, cG = (sb(f"d_c{n}", [P, DH]) for n in ("beta", "eG", "eK", "gl", "G"))
        raw = [sb(f"d_raw{n}", [P, DH, P]) for n in range(3)]
        gate = sb("d_gate", [P, DH, P])
        sq = sb("d_sq", [P, 2, 2, HH, P])
        ss, rn = sb("d_ss", [P, 2 * DH]), sb("d_rn", [P, 2 * DH])
        tq, tqd, tk, tkb, kd, kg, vb = (full(f"d_{n}") for n in ("tq", "tqd", "tk", "tkb", "kd", "kg", "vb"))
        qT, kT, kbT, qdT = (full(f"d_{n}T") for n in ("q", "k", "kb", "qd"))
        dec, MT, qk = full("d_dec"), full("d_MT"), full("d_qk")
        LT = [full(f"d_LT{u}") for u in range(2)]
        Tm, TT_, X = full("d_Tm"), full("d_TT"), full("d_X")
        nwT, vn, S, S2 = full("d_nwT"), full("d_vn"), full("d_S"), full("d_S2")
        sqo, so, ro, on = full("d_sqo"), sb("d_so", [P, DH]), sb("d_ro", [P, DH]), full("d_on")
        ybT = sb("d_ybT", [P, DH, T])
        ps = {n: ctx.enter_context(nc.psum_tensor(f"d_ps{n}", [P, 2, HALF], F32)) for n in "ABCD"}

        def pw(n, h=None):
            v = ps[n][:, :, 0:W].rearrange("p a (b t) -> p a b t", t=P)
            return v if h is None else v[:, h]

        def cast(v, h=None):
            v = v.rearrange("p (a b) -> p a b", a=2)
            if h is None:
                return v.unsqueeze(3).broadcast_to([P, 2, HH, P])
            return v[:, h].unsqueeze(2).broadcast_to([P, HH, P])

        def heads(v, h):
            return v.unsqueeze(1).broadcast_to([P, HH, P])

        def at(v, h):
            return v[:, h // HH, h % HH, :]

        block = ctx.enter_context(nc.Block())

        @block.sync
        def _(sp):
            srcs = [(ident, g.ident), (upto, g.upto), (later, g.notlater), (level, g.level), (ba, g.ba),
                    (neg_a, g.a_log.partition_broadcast(P)), (dtb, g.dt_bias.partition_broadcast(P)),
                    (gain, g.norm_gain)]
            for d, s in srcs:
                sp.dma_start(d[:], s).then_inc(sem("ld_c"), 16)
            with sp.Fori(0, NC) as i:
                sp.wait_ge(sem("tr1"), 3 * i)
                for n in range(3):
                    src = g.hT[N_ATT + n * DH:N_ATT + (n + 1) * DH, :, bass.ds(i * C, C)]
                    sp.dma_start(raw[n][:], src.rearrange("n p t -> p n t")).then_inc(sem("ld_qkv"), 16)
                sp.wait_ge(sem("y_out"), 2 * i)
                src = g.hT[N_ATT + N_DN:N_ATT + N_DN + N_GB, :, bass.ds(i * C, C)]
                sp.dma_start(gate[:], src.rearrange("n p t -> p n t")).then_inc(sem("ld_gate"), 16)
            sp.wait_ge(sem("y_out"), 2 * NC)
            sp.dma_start(g.y[AT:AT + DH].rearrange("n p t -> p n t"), ybT[:]).then_inc(sem("stored"), 16)
            sp.wait_ge(sem("stored"), 16)

        @block.gpsimd
        def _(pool):
            nc.gpsimd.memset(ones[:], 1.0).then_inc(sem("ones"), 1)
            nc.gpsimd.memset(half_power[:], -0.5).then_inc(sem("ones"), 1)
            nc.gpsimd.memset(S[:], 0.0).then_inc(sem("ones"), 1)
            pool.wait_ge(sem("ones"), 3)
            with pool.Fori(0, NC) as i:
                pool.wait_ge(sem("sumsq"), i + 1)
                pool.wait_ge(sem("tk"), 2 * i)
                nc.gpsimd.tensor_tensor(rn[:], ss[:], half_power[:], ALU.pow).then_inc(sem("rnorm"), 1)
                pool.wait_ge(sem("tk"), 2 * i + 2)
                pool.wait_ge(sem("chunk_factors"), i + 1)
                pool.wait_ge(sem("w_mm"), 2 * i)
                nc.gpsimd.tensor_tensor(tkb[:], tk[:], cast(cbeta[:]), ALU.mult).then_inc(sem("tkb"), 1)
                pool.wait_ge(sem("tq"), i + 1)
                nc.gpsimd.tensor_tensor(tqd[:], tq[:], cast(ceG[:]), ALU.mult).then_inc(sem("tqd"), 1)
                pool.wait_ge(sem("state_mm"), i)
                nc.gpsimd.tensor_tensor(kd[:], tk[:], cast(ceK[:]), ALU.mult).then_inc(sem("kd"), 1)
                pool.wait_ge(sem("tkb"), i + 1)
                nc.gpsimd.tensor_tensor(kg[:], tkb[:], cast(ceG[:]), ALU.mult).then_inc(sem("kg"), 1)
                for v in range(1, LEVELS):
                    u = v % 2
                    for h in range(2):
                        pool.wait_ge(sem("M"), 2 * i + 1 + h)
                        pool.wait_ge(sem("X_mm"), 12 * i + max(2 * (v - 3) + h + 1, 0))
                        nc.gpsimd.tensor_tensor(LT[u][:, h], MT[:, h], heads(level[:, v, :], h), ALU.mult).then_inc(sem("LT"), 1)
                pool.wait_ge(sem("state"), i)
                nc.gpsimd.tensor_tensor(S2[:], S[:], cast(cgl[:]), ALU.mult).then_inc(sem("decayed"), 1)
                pool.wait_ge(sem("out_sumsq"), i + 1)
                nc.gpsimd.tensor_tensor(ro[:], so[:], half_power[:, 0:DH], ALU.pow).then_inc(sem("out_rnorm"), 1)

        @block.scalar
        def _(act):
            act.wait_ge(sem("ld_c"), 16 * 8)
            nc.scalar.activation(beta[:], ba[:, :, 0:DH], ACT.Sigmoid).then_inc(sem("beta"), 1)
            nc.scalar.activation(neg_a[:], neg_a[:], ACT.Exp).then_inc(sem("exp"), 1)
            act.wait_ge(sem("z_abs"), 1)
            nc.scalar.activation(ez[:], ez[:], ACT.Exp, scale=-1.0).then_inc(sem("ez"), 1)
            act.wait_ge(sem("ez"), 1)
            nc.scalar.activation(ez[:], ez[:], ACT.Ln, bias=1.0).then_inc(sem("ez"), 1)
            act.wait_ge(sem("G_ready"), 1)
            nc.scalar.activation(eG[:], Gs[:], ACT.Exp).then_inc(sem("exps"), 1)
            nc.scalar.activation(gl[:], gl[:], ACT.Exp).then_inc(sem("exps"), 1)
            nc.scalar.activation(eK[:], eK[:], ACT.Exp).then_inc(sem("exps"), 1)
            with act.Fori(0, NC) as i:
                for n, name in ((0, "A"), (1, "B")):
                    act.wait_ge(sem("tr1"), 3 * i + n + 1)
                    act.wait_ge(sem("sumsq"), i)
                    nc.scalar.activation(sq[:, n], pw(name), ACT.Square).then_inc(sem("squares"), 1)
                act.wait_ge(sem("tr2"), 4 * i + 1)
                nc.scalar.copy(qT[:], pw("A")).then_inc(sem("qT"), 1)
                act.wait_ge(sem("tr2"), 4 * i + 3)
                nc.scalar.copy(kbT[:], pw("C")).then_inc(sem("kbT"), 1)
                act.wait_ge(sem("decay"), i + 1)
                nc.scalar.activation(dec[:], dec[:], ACT.Exp).then_inc(sem("decay_exp"), 1)
                for h in range(2):
                    act.wait_ge(sem("T_tr"), 2 * i + h + 1)
                    nc.scalar.copy(Tm[:, h], pw("A", h)).then_inc(sem("T_first"), 1)
                for v in range(1, LEVELS):
                    for h in range(2):
                        act.wait_ge(sem("X_mm"), 12 * i + 2 * (v - 1) + h + 1)
                        nc.scalar.copy(X[:, h], pw("B", h)).then_inc(sem("X"), 1)
                for h in range(2):
                    act.wait_ge(sem("w_mm"), 2 * i + h + 1)
                    nc.scalar.mul(nwT[:, h], pw("A", h), -1.0).then_inc(sem("w"), 1)
                for h in range(2):
                    act.wait_ge(sem("vn_mm"), 2 * i + h + 1)
                    nc.scalar.copy(vn[:, h], pw("B", h)).then_inc(sem("vn"), 1)
                act.wait_ge(sem("o_mm"), i + 1)
                nc.scalar.activation(sqo[:], pw("C"), ACT.Square).then_inc(sem("out_squares"), 1)

        @block.vector
        def _(dve):
            dve.wait_ge(sem("ld_c"), 16 * 8)
            nc.vector.tensor_tensor(z[:], ba[:, :, DH:], dtb[:].unsqueeze(1).broadcast_to([P, NC, DH]), ALU.add).then_inc(sem("z"), 1)
            dve.wait_ge(sem("z"), 1)
            nc.vector.tensor_scalar(ez[:], z[:], -1.0, None, ALU.mult).then_inc(sem("z"), 1)
            dve.wait_ge(sem("z"), 2)
            nc.vector.tensor_tensor(ez[:], ez[:], z[:], ALU.max).then_inc(sem("z_abs"), 1)
            nc.vector.tensor_scalar(z[:], z[:], 0.0, None, ALU.max).then_inc(sem("z"), 1)
            dve.wait_ge(sem("z"), 3)
            dve.wait_ge(sem("ez"), 2)
            nc.vector.tensor_tensor(z[:], z[:], ez[:], ALU.add).then_inc(sem("z"), 1)
            dve.wait_ge(sem("exp"), 1)
            dve.wait_ge(sem("z"), 4)
            nc.vector.tensor_scalar(z[:], z[:], -1.0, None, ALU.mult).then_inc(sem("z"), 1)
            dve.wait_ge(sem("z"), 5)
            nc.vector.tensor_tensor(gg[:], z[:], neg_a[:].unsqueeze(1).broadcast_to([P, NC, DH]), ALU.mult).then_inc(sem("g"), 1)
            dve.wait_ge(sem("G_mm"), 2)
            G2 = NC * DH
            nc.vector.tensor_copy(Gs[:].rearrange("p a b -> p (a b)"), ps["A"][:, 0, 0:G2])
            nc.vector.tensor_copy(gl[:].rearrange("p a b -> p (a b)"), ps["B"][:, 0, 0:G2]).then_inc(sem("g_copied"), 1)
            dve.wait_ge(sem("g_copied"), 1)
            nc.vector.tensor_tensor(eK[:], gl[:], Gs[:], ALU.subtract).then_inc(sem("G_ready"), 1)
            dve.wait_ge(sem("exps"), 3)
            dve.wait_ge(sem("beta"), 1)
            with dve.Fori(0, NC) as i:
                dve.wait_ge(sem("decayed"), i)
                dve.wait_ge(sem("kg"), i)
                dve.wait_ge(sem("rowG"), i)
                dve.wait_ge(sem("g"), 1)
                for d, s in ((cbeta, beta), (ceG, eG), (ceK, eK), (cgl, gl), (cG, Gs)):
                    nc.vector.tensor_copy(d[:], s[:, bass.ds(i, 1), :].rearrange("p a b -> p (a b)"))
                nc.vector.tensor_copy(gB[:].rearrange("p a b t -> p (a b) t"),
                                      gg[:, bass.ds(i, 1), :].rearrange("p a b -> p (a b)").unsqueeze(2).broadcast_to([P, DH, P])).then_inc(sem("chunk_factors"), 1)
                dve.wait_ge(sem("tr1"), 3 * i + 3)
                dve.wait_ge(sem("chunk_factors"), i + 1)
                dve.wait_ge(sem("vn_mm"), 2 * i)
                nc.vector.tensor_tensor(vb[:], pw("C"), cast(cbeta[:]), ALU.mult).then_inc(sem("vb"), 1)
                dve.wait_ge(sem("squares"), 2 * i + 2)
                dve.wait_ge(sem("rnorm"), i)
                nc.vector.tensor_reduce(ss[:], sq[:].rearrange("p n a b t -> p (n a b) t"), AX.X, ALU.add).then_inc(sem("ss_raw"), 1)
                dve.wait_ge(sem("ss_raw"), 3 * i + 1)
                nc.vector.tensor_scalar(ss[:, 0:DH], ss[:, 0:DH], 1e-6, float(DD), ALU.add, ALU.mult).then_inc(sem("ss_raw"), 1)
                nc.vector.tensor_scalar(ss[:, DH:], ss[:, DH:], 1e-6, None, ALU.add).then_inc(sem("ss_raw"), 1)
                dve.wait_ge(sem("ss_raw"), 3 * i + 3)
                dve.sem_inc(sem("sumsq"), 1)
                dve.wait_ge(sem("rnorm"), i + 1)
                dve.wait_ge(sem("tr2"), 4 * i)
                dve.wait_ge(sem("kd"), i)
                for h in range(2):
                    nc.vector.tensor_tensor(tk[:, h], pw("B", h), cast(rn[:, DH:], h), ALU.mult).then_inc(sem("tk"), 1)
                nc.vector.tensor_tensor(tq[:], pw("A"), cast(rn[:, 0:DH]), ALU.mult).then_inc(sem("tq"), 1)
                dve.wait_ge(sem("tr2"), 4 * i + 2)
                nc.vector.tensor_copy(kT[:], pw("B")).then_inc(sem("kT"), 1)
                dve.wait_ge(sem("tr2"), 4 * i + 4)
                nc.vector.tensor_copy(qdT[:], pw("D")).then_inc(sem("qdT"), 1)
                dve.wait_ge(sem("rowG"), i + 1)
                nc.vector.tensor_tensor(dec[:], pw("C"), cast(cG[:]), ALU.subtract).then_inc(sem("decay_step"), 1)
                dve.wait_ge(sem("decay_step"), 2 * i + 1)
                d6 = dec[:].rearrange("p a b t -> p (a b) t")
                nc.vector.tensor_tensor(d6, d6, later[:].unsqueeze(1).broadcast_to([P, DH, P]), ALU.add).then_inc(sem("decay_step"), 1)
                dve.wait_ge(sem("decay_step"), 2 * i + 2)
                dve.sem_inc(sem("decay"), 1)
                dve.wait_ge(sem("decay_exp"), i + 1)
                dve.wait_ge(sem("kk_mm"), 2 * i + 2)
                for h in range(2):
                    nc.vector.tensor_tensor(MT[:, h], pw("A", h), dec[:, h], ALU.mult).then_inc(sem("M"), 1)
                nc.vector.tensor_tensor(qk[:], pw("D"), dec[:], ALU.mult).then_inc(sem("qk"), 1)
                for h in range(2):
                    dve.wait_ge(sem("M"), 2 * i + h + 1)
                    nc.vector.tensor_tensor(TT_[:, h], MT[:, h], heads(level[:, 0, :], h), ALU.mult).then_inc(sem("T0"), 1)
                for h in range(2):
                    dve.wait_ge(sem("T0"), 4 * i + h + 1)
                    nc.vector.tensor_tensor(TT_[:, h], heads(ident[:], h), TT_[:, h], ALU.subtract).then_inc(sem("T0"), 1)
                for v in range(1, LEVELS):
                    for h in range(2):
                        dve.wait_ge(sem("TX_mm"), 12 * i + 2 * (v - 1) + h + 1)
                        if v < LEVELS - 1:
                            nc.vector.tensor_tensor(Tm[:, h], Tm[:, h], pw("C", h), ALU.subtract).then_inc(sem("T"), 1)
                        nc.vector.tensor_tensor(TT_[:, h], TT_[:, h], pw("D", h), ALU.subtract).then_inc(sem("TT"), 1)
                dve.wait_ge(sem("decayed"), i + 1)
                dve.wait_ge(sem("state_mm"), i + 1)
                nc.vector.tensor_tensor(S[:], S2[:], pw("D"), ALU.add).then_inc(sem("state"), 1)
                dve.wait_ge(sem("out_squares"), i + 1)
                dve.wait_ge(sem("out_rnorm"), i)
                nc.vector.tensor_reduce(so[:], sqo[:].rearrange("p a b t -> p (a b) t"), AX.X, ALU.add).then_inc(sem("so_raw"), 1)
                dve.wait_ge(sem("so_raw"), 2 * i + 1)
                nc.vector.tensor_scalar(so[:], so[:], 1.0 / DD, 1e-6, ALU.mult, ALU.add).then_inc(sem("so_raw"), 1)
                dve.wait_ge(sem("so_raw"), 2 * i + 2)
                dve.sem_inc(sem("out_sumsq"), 1)
                dve.wait_ge(sem("out_rnorm"), i + 1)
                nc.vector.tensor_tensor(on[:], pw("C"), cast(ro[:]), ALU.mult).then_inc(sem("on"), 1)
                dve.wait_ge(sem("ld_gate"), 16 * (i + 1))
                for h in range(2):
                    dve.wait_ge(sem("on_tr"), 2 * i + h + 1)
                    nc.vector.scalar_tensor_tensor(ybT[:, h * HH:(h + 1) * HH, bass.ds(i * C, C)], pw("A", h), gain[:, 0:1],
                                                   gate[:, h * HH:(h + 1) * HH, :], ALU.mult, ALU.mult).then_inc(sem("y_out"), 1)

        @block.tensor
        def _(pe):
            pe.wait_ge(sem("g"), 1)
            pe.wait_ge(sem("ones"), 3)
            gf = gg[:].rearrange("p a b -> p (a b)")
            nc.tensor.matmul(ps["A"][:, 0, 0:NC * DH], upto[:], gf, start=True, stop=True).then_inc(sem("G_mm"), 1)
            nc.tensor.matmul(ps["B"][:, 0, 0:NC * DH], ones[:], gf, start=True, stop=True).then_inc(sem("G_mm"), 1)
            pe.wait_ge(sem("g_copied"), 1)
            with pe.Fori(0, NC) as i:
                pe.wait_ge(sem("ld_qkv"), 48 * (i + 1))
                pe.wait_ge(sem("y_out"), 2 * i)
                for n, name in enumerate("ABC"):
                    for h in range(DH):
                        ins = nc.tensor.transpose(at(pw(name), h), raw[n][:, h, :], ident[:])
                    ins.then_inc(sem("tr1"), 1)

                def turn(name, src, ready, count=1):
                    pe.wait_ge(sem(ready), count * i + count)
                    for h in range(DH):
                        ins = nc.tensor.transpose(at(pw(name), h), at(src, h), ident[:])
                    ins.then_inc(sem("tr2"), 1)

                turn("A", tq, "tq")
                turn("B", tk, "tk", 2)
                pe.wait_ge(sem("vb"), i + 1)
                turn("C", tkb, "tkb")
                pe.wait_ge(sem("state"), i)
                turn("D", tqd, "tqd")
                pe.wait_ge(sem("kT"), i + 1)
                pe.wait_ge(sem("kbT"), i + 1)
                pe.wait_ge(sem("qT"), i + 1)
                for h in range(DH):
                    ins = nc.tensor.matmul(at(pw("A"), h), at(kT, h), at(kbT, h), start=True, stop=True)
                ins.then_inc(sem("kk_mm"), 1)
                for h in range(DH):
                    ins = nc.tensor.matmul(at(pw("C"), h), at(gB, h), upto[:], start=True, stop=True)
                ins.then_inc(sem("rowG"), 1)
                pe.wait_ge(sem("qdT"), i + 1)
                for h in range(DH):
                    ins = nc.tensor.matmul(at(pw("D"), h), at(kT, h), at(qT, h), start=True, stop=True)
                ins.then_inc(sem("kk_mm"), 1)
                for h in range(2):
                    pe.wait_ge(sem("T0"), 4 * i + 3 + h)
                    for a in range(HH):
                        ins = nc.tensor.transpose(pw("A", h)[:, a], TT_[:, h, a, :], ident[:])
                    ins.then_inc(sem("T_tr"), 1)
                pe.wait_ge(sem("qk"), i + 1)
                for v in range(1, LEVELS):
                    for h in range(2):
                        pe.wait_ge(sem("LT"), 12 * i + 2 * (v - 1) + h + 1)
                        if v == 1:
                            pe.wait_ge(sem("T_first"), 2 * i + h + 1)
                        else:
                            pe.wait_ge(sem("T"), 10 * i + 2 * (v - 2) + h + 1)
                            pe.wait_ge(sem("TT"), 12 * i + 2 * (v - 2) + h + 1)
                        for a in range(HH):
                            ins = nc.tensor.matmul(pw("B", h)[:, a], LT[v % 2][:, h, a, :], Tm[:, h, a, :], start=True, stop=True)
                        ins.then_inc(sem("X_mm"), 1)
                    for h in range(2):
                        pe.wait_ge(sem("X"), 12 * i + 2 * (v - 1) + h + 1)
                        for a in range(HH):
                            if v < LEVELS - 1:
                                nc.tensor.matmul(pw("C", h)[:, a], TT_[:, h, a, :], X[:, h, a, :], start=True, stop=True)
                            ins = nc.tensor.matmul(pw("D", h)[:, a], X[:, h, a, :], TT_[:, h, a, :], start=True, stop=True)
                        ins.then_inc(sem("TX_mm"), 1)
                for h in range(2):
                    pe.wait_ge(sem("TT"), 12 * i + 2 * (LEVELS - 2) + h + 1)
                    pe.wait_ge(sem("kg"), i + 1)
                    for a in range(HH):
                        ins = nc.tensor.matmul(pw("A", h)[:, a], kg[:, h, a, :], TT_[:, h, a, :], start=True, stop=True)
                    ins.then_inc(sem("w_mm"), 1)
                pe.wait_ge(sem("state"), i)
                for h in range(2):
                    pe.wait_ge(sem("w"), 2 * i + h + 1)
                    for a in range(HH):
                        nc.tensor.matmul(pw("B", h)[:, a], TT_[:, h, a, :], vb[:, h, a, :], start=True, stop=False)
                        ins = nc.tensor.matmul(pw("B", h)[:, a], nwT[:, h, a, :], S[:, h, a, :], start=False, stop=True)
                    ins.then_inc(sem("vn_mm"), 1)
                for h in range(2):
                    pe.wait_ge(sem("vn"), 2 * i + h + 1)
                    for a in range(HH):
                        nc.tensor.matmul(pw("C", h)[:, a], qdT[:, h, a, :], S[:, h, a, :], start=True, stop=False)
                        ins = nc.tensor.matmul(pw("C", h)[:, a], qk[:, h, a, :], vn[:, h, a, :], start=False, stop=True)
                ins.then_inc(sem("o_mm"), 1)
                pe.wait_ge(sem("kd"), i + 1)
                for h in range(DH):
                    ins = nc.tensor.matmul(at(pw("D"), h), at(kd, h), at(vn, h), start=True, stop=True)
                ins.then_inc(sem("state_mm"), 1)
                pe.wait_ge(sem("on"), i + 1)
                for h in range(2):
                    for a in range(HH):
                        ins = nc.tensor.transpose(pw("A", h)[:, a], on[:, h, a, :], ident[:])
                    ins.then_inc(sem("on_tr"), 1)


def float32r_products(wh, wl, xh, xl):
    return ((wh, xh), (wh, xl), (wl, xh))


def stage_merge(nc, g):
    NK = 2 * AT
    with ExitStack() as ctx:
        def sb(name, shape, dt=F32):
            return ctx.enter_context(nc.sbuf_tensor(name, shape, dt))

        sem = ctx.enter_context(stage_semaphores(nc, "m"))

        yraw = [sb(f"m_yraw{u}", [P, T]) for u in range(2)]
        yh, yl = sb("m_yh", [P, NK, T], F32R), sb("m_yl", [P, NK, T], F32R)
        wraw = [sb(f"m_wraw{u}", [P, NK, P]) for u in range(2)]
        wh = [sb(f"m_wh{u}", [P, NK, P], F32R) for u in range(2)]
        wl = [sb(f"m_wl{u}", [P, NK, P], F32R) for u in range(2)]
        gates = [sb(f"m_gates{u}", [P, 2, T]) for u in range(2)]
        ps = [[ctx.enter_context(nc.psum_tensor(f"m_ps{u}{b}", [P, T], F32)) for b in range(2)] for u in range(2)]
        block = ctx.enter_context(nc.Block())

        @block.sync
        def _(sp):
            for k in range(NK):
                if k >= 2:
                    sp.wait_ge(sem("y_lo"), k - 1)
                sp.dma_start(yraw[k % 2][:], g.y[k]).then_inc(sem(f"ld_y{k % 2}"), 16)
                if k < 2:
                    sp.dma_start(wraw[k][:], g.w_branch[k]).then_inc(sem(f"ld_w{k}"), 16)
                    for b in range(2):
                        sp.dma_start(gates[k][:, b, :], g.hT[N_IN - N_BR + b * KD + k]).then_inc(sem(f"ld_g{k}"), 16)
            with sp.Fori(0, KD // 2 - 1) as i:
                for u in range(2):
                    sp.wait_ge(sem("w_lo"), 2 * i + (u + 1))
                    sp.dma_start(wraw[u][:], g.w_branch[bass.ds(2 * i + (2 + u), 1)].rearrange("o p k c -> (o p) k c")).then_inc(sem(f"ld_w{u}"), 16)
                    sp.wait_ge(sem("gated"), 4 * i + (2 * u + 2))
                    for b in range(2):
                        sp.dma_start(gates[u][:, b, :], g.hT[bass.ds(2 * i + (N_IN - N_BR + b * KD + 2 + u), 1)].rearrange("o p t -> (o p) t")).then_inc(sem(f"ld_g{u}"), 16)

        @block.scalar
        def _(act):
            for k in range(NK):
                act.wait_ge(sem(f"ld_y{k % 2}"), 16 * (k // 2 + 1))
                nc.scalar.copy(yh[:, k, :], yraw[k % 2][:]).then_inc(sem("y_hi"), 1)
            for u in range(2):
                act.wait_ge(sem(f"ld_w{u}"), 16)
                nc.scalar.copy(wh[u][:], wraw[u][:]).then_inc(sem("w_hi"), 1)
            with act.Fori(0, KD // 2 - 1) as i:
                for u in range(2):
                    act.wait_ge(sem("mm"), 2 * i + (u + 1))
                    act.wait_ge(sem(f"ld_w{u}"), 16 * i + 32)
                    nc.scalar.copy(wh[u][:], wraw[u][:]).then_inc(sem("w_hi"), 1)

        @block.vector
        def _(dve):
            for k in range(NK):
                dve.wait_ge(sem("y_hi"), k + 1)
                nc.vector.tensor_tensor(yl[:, k, :], yraw[k % 2][:], yh[:, k, :].bitcast(F32), ALU.subtract).then_inc(sem("y_lo"), 1)
            for u in range(2):
                dve.wait_ge(sem("w_hi"), u + 1)
                nc.vector.tensor_tensor(wl[u][:], wraw[u][:], wh[u][:].bitcast(F32), ALU.subtract).then_inc(sem("w_lo"), 1)

            def body(i, last=False):
                for u in range(2):
                    dve.wait_ge(sem("mm"), 2 * i + (u + 1))
                    if not last:
                        dve.wait_ge(sem("w_hi"), 2 * i + (u + 3))
                        nc.vector.tensor_tensor(wl[u][:], wraw[u][:], wh[u][:].bitcast(F32), ALU.subtract).then_inc(sem("w_lo"), 1)
                    dve.wait_ge(sem(f"ld_g{u}"), 32 * i + 32)
                    for b in range(2):
                        nc.vector.tensor_tensor(gates[u][:, b, :], gates[u][:, b, :], ps[u][b][:], ALU.mult).then_inc(sem("ps_read"), 1)
                    dve.wait_ge(sem("ps_read"), 4 * i + (2 * u + 2))
                    nc.vector.tensor_tensor(g.merged[:, bass.ds(2 * i + u, 1), :].rearrange("p o t -> p (o t)"),
                                            gates[u][:, 0, :], gates[u][:, 1, :], ALU.add).then_inc(sem("gated"), 2)

            with dve.Fori(0, KD // 2 - 1) as i:
                body(i)
            body(KD // 2 - 1, last=True)

        @block.tensor
        def _(pe):
            pe.wait_ge(sem("y_lo"), NK)
            with pe.Fori(0, KD // 2) as i:
                for u in range(2):
                    pe.wait_ge(sem("w_lo"), 2 * i + (u + 1))
                    pe.wait_ge(sem("ps_read"), 4 * i)
                    for b in range(2):
                        for h in range(2):
                            for k in range(AT):
                                for n, (a, x) in enumerate(float32r_products(wh, wl, yh, yl)):
                                    ins = nc.tensor.matmul(ps[u][b][:, h * HALF:(h + 1) * HALF], a[u][:, b * AT + k, :],
                                                           x[:, b * AT + k, h * HALF:(h + 1) * HALF],
                                                           start=(k == 0 and n == 0), stop=(k == AT - 1 and n == 2))
                    ins.then_inc(sem("mm"), 1)


def stage_out_norm(nc, g):
    with ExitStack() as ctx:
        def sb(name, shape, dt=F32):
            return ctx.enter_context(nc.sbuf_tensor(name, shape, dt))

        sem = ctx.enter_context(stage_semaphores(nc, "o"))

        wraw = [sb(f"o_wraw{u}", [P, D]) for u in range(2)]
        wh, wl = sb("o_wh", [P, KD, D], F32R), sb("o_wl", [P, KD, D], F32R)
        mh = [sb(f"o_mh{u}", [P, KD, P], F32R) for u in range(2)]
        ml = [sb(f"o_ml{u}", [P, KD, P], F32R) for u in range(2)]
        x = [sb(f"o_x{u}", [P, D]) for u in range(2)]
        z = [sb(f"o_z{u}", [P, D]) for u in range(2)]
        xT = [sb(f"o_xT{u}", [P, KD, P]) for u in range(2)]
        gain, bias, ident = sb("o_gain", [P, D]), sb("o_bias", [P, D]), sb("o_ident", [P, P])
        stats, mv, rstd, power = sb("o_stats", [P, 2, 6]), sb("o_mv", [P, 2]), sb("o_rstd", [P, 1]), sb("o_power", [P, 1])
        ps = [ctx.enter_context(nc.psum_tensor(f"o_ps{u}", [P, D], F32)) for u in range(2)]
        psT = ctx.enter_context(nc.psum_tensor("o_psT", [P, D], F32))
        block = ctx.enter_context(nc.Block())

        @block.sync
        def _(sp):
            for d, s in ((gain, g.ln1_gain.partition_broadcast(P)), (bias, g.ln1_bias.partition_broadcast(P)), (ident, g.ident)):
                sp.dma_start(d[:], s).then_inc(sem("ld_c"), 16)
            for k in range(KD):
                if k >= 2:
                    sp.wait_ge(sem("w_lo"), k - 1)
                sp.dma_start(wraw[k % 2][:], g.w_out[k * P:(k + 1) * P, :]).then_inc(sem(f"ld_w{k % 2}"), 16)
            with sp.Fori(0, TT // 2) as i:
                for u in range(2):
                    sp.wait_ge(sem("z"), 2 * i)
                    sp.dma_start(x[u][:], g.x[bass.ds(2 * i * P + u * P, P), :]).then_inc(sem(f"ld_x{u}"), 16)

        @block.gpsimd
        def _(pool):
            nc.gpsimd.memset(power[:], -0.5).then_inc(sem("power"), 1)
            pool.wait_ge(sem("ld_c"), 48)
            pool.wait_ge(sem("power"), 1)
            with pool.Fori(0, TT // 2) as i:
                for u in range(2):
                    pool.wait_ge(sem("var"), 2 * i + (u + 1))
                    pool.wait_ge(sem("normed"), 2 * i + u)
                    nc.gpsimd.tensor_tensor(rstd[:], mv[:, 1:2], power[:], ALU.pow).then_inc(sem("rstd"), 1)
                    pool.wait_ge(sem("normed"), 2 * i + (u + 1))
                    nc.gpsimd.tensor_tensor(z[u][:], z[u][:], gain[:], ALU.mult).then_inc(sem("scaled"), 1)
                    pool.wait_ge(sem("scaled"), 2 * i + (u + 1))
                    nc.gpsimd.tensor_tensor(z[u][:], z[u][:], bias[:], ALU.add).then_inc(sem("x1"), 1)
                    pool.wait_ge(sem("x1"), 2 * i + (u + 1))
                    pool.dma_start(g.x1[bass.ds(2 * i * P + u * P, P), :], z[u][:]).then_inc(sem(f"st_x1{u}"), 16)
                    pool.wait_ge(sem("xT"), 2 * i + (u + 1))
                    pool.dma_start(g.x1T[:, :, bass.ds(2 * i * P + u * P, P)].rearrange("k p t -> p k t"), xT[u][:]).then_inc(sem(f"st_xT{u}"), 16)
            for u in range(2):
                pool.wait_ge(sem(f"st_x1{u}"), 16 * (TT // 2))
                pool.wait_ge(sem(f"st_xT{u}"), 16 * (TT // 2))

        @block.scalar
        def _(act):
            for k in range(KD):
                act.wait_ge(sem(f"ld_w{k % 2}"), 16 * (k // 2 + 1))
                nc.scalar.copy(wh[:, k, :], wraw[k % 2][:]).then_inc(sem("w_hi"), 1)
            with act.Fori(0, TT // 2) as i:
                for u in range(2):
                    act.wait_ge(sem("mm"), 2 * i)
                    nc.scalar.copy(mh[u][:], g.merged[:, :, bass.ds(2 * i * P + u * P, P)]).then_inc(sem("m_hi"), 1)
                for u in range(2):
                    act.wait_ge(sem(f"st_xT{u}"), 16 * i)
                    act.wait_ge(sem("turned"), 2 * i + (u + 1))
                    nc.scalar.copy(xT[u][:], psT[:].rearrange("p (k t) -> p k t", t=P)).then_inc(sem("xT"), 1)

        @block.vector
        def _(dve):
            for k in range(KD):
                dve.wait_ge(sem("w_hi"), k + 1)
                nc.vector.tensor_tensor(wl[:, k, :], wraw[k % 2][:], wh[:, k, :].bitcast(F32), ALU.subtract).then_inc(sem("w_lo"), 1)
            with dve.Fori(0, TT // 2) as i:
                for u in range(2):
                    dve.wait_ge(sem("m_hi"), 2 * i + (u + 1))
                    nc.vector.tensor_tensor(ml[u][:], g.merged[:, :, bass.ds(2 * i * P + u * P, P)], mh[u][:].bitcast(F32), ALU.subtract).then_inc(sem("m_lo"), 1)
                for u in range(2):
                    dve.wait_ge(sem(f"ld_x{u}"), 16 * i + 16)
                    dve.wait_ge(sem(f"st_x1{u}"), 16 * i)
                    dve.wait_ge(sem("turned"), 2 * i)
                    dve.wait_ge(sem("mm"), 2 * i + (u + 1))
                    nc.vector.scalar_tensor_tensor(z[u][:], x[u][:], ALPHA, ps[u][:], ALU.mult, ALU.add).then_inc(sem("z"), 1)
                    dve.wait_ge(sem("z"), 2 * i + (u + 1))
                    dve.wait_ge(sem("normed"), 2 * i + u)
                    for h in range(2):
                        ins = nc.vector.bn_stats(stats[:, h, :], z[u][:, h * HALF:(h + 1) * HALF])
                    ins.then_inc(sem("stats"), 1)
                    wait_alone(dve, sem("stats"), 2 * i + (u + 1), sem("passed"))
                    nc.vector.bn_aggr(mv[:], stats[:]).then_inc(sem("aggr"), 1)
                    dve.wait_ge(sem("aggr"), 2 * i + (u + 1))
                    nc.vector.tensor_scalar(mv[:, 1:2], mv[:, 1:2], 1e-5, None, ALU.add).then_inc(sem("var"), 1)
                    dve.wait_ge(sem("rstd"), 2 * i + (u + 1))
                    nc.vector.tensor_scalar(z[u][:], z[u][:], mv[:, 0:1], rstd[:, 0:1], ALU.subtract, ALU.mult).then_inc(sem("normed"), 1)

        @block.tensor
        def _(pe):
            pe.wait_ge(sem("w_lo"), KD)
            pe.wait_ge(sem("ld_c"), 48)
            with pe.Fori(0, TT // 2) as i:
                for u in range(2):
                    pe.wait_ge(sem("m_lo"), 2 * i + (u + 1))
                    pe.wait_ge(sem("z"), 2 * i)
                    for h in range(2):
                        for k in range(KD):
                            for n, (a, b) in enumerate(float32r_products(mh, ml, wh, wl)):
                                ins = nc.tensor.matmul(ps[u][:, h * HALF:(h + 1) * HALF], a[u][:, k, :], b[:, k, h * HALF:(h + 1) * HALF],
                                                       start=(k == 0 and n == 0), stop=(k == KD - 1 and n == 2))
                    ins.then_inc(sem("mm"), 1)
                for u in range(2):
                    pe.wait_ge(sem("x1"), 2 * i + (u + 1))
                    pe.wait_ge(sem("xT"), 2 * i + u)
                    for k in range(KD):
                        ins = nc.tensor.transpose(psT[:, k * P:(k + 1) * P], z[u][:, k * P:(k + 1) * P], ident[:])
                    ins.then_inc(sem("turned"), 1)


def stage_scores(nc, g):
    N = 2 * PH
    with ExitStack() as ctx:
        def sb(name, shape, dt=F32):
            return ctx.enter_context(nc.sbuf_tensor(name, shape, dt))

        sem = ctx.enter_context(stage_semaphores(nc, "s"))

        xraw = [sb(f"s_xraw{u}", [P, T]) for u in range(2)]
        xh, xl = g.x1h, g.x1l
        wraw = [sb(f"s_wraw{u}", [P, KD, P]) for u in range(2)]
        wh = [sb(f"s_wh{u}", [P, KD, P], F32R) for u in range(2)]
        wl = [sb(f"s_wl{u}", [P, KD, P], F32R) for u in range(2)]
        keys = sb("s_keys", [P, N, PK])
        q = [sb(f"s_q{u}", [P, T]) for u in range(2)]
        sout = [sb(f"s_out{u}", [P, TT, PK]) for u in range(2)]
        psq = [ctx.enter_context(nc.psum_tensor(f"s_psq{u}", [P, T], F32)) for u in range(2)]
        pss = [ctx.enter_context(nc.psum_tensor(f"s_pss{u}", [P, T], F32)) for u in range(2)]
        block = ctx.enter_context(nc.Block())

        @block.sync
        def _(sp):
            for k in range(KD):
                if k >= 2:
                    sp.wait_ge(sem("x_lo"), k - 1)
                sp.dma_start(xraw[k % 2][:], g.x1T[k]).then_inc(sem(f"ld_x{k % 2}"), 16)
                if k < 2:
                    sp.dma_start(wraw[k][:], g.w_query[k]).then_inc(sem(f"ld_w{k}"), 16)
            sp.dma_start(keys[:], g.keys.rearrange("n c k -> c n k")).then_inc(sem("ld_k"), 16)
            with sp.Fori(0, N // 2 - 1) as i:
                for u in range(2):
                    sp.wait_ge(sem("w_lo"), 2 * i + (u + 1))
                    sp.dma_start(wraw[u][:], g.w_query[bass.ds(2 * i + (2 + u), 1)].rearrange("o p k c -> (o p) k c")).then_inc(sem(f"ld_w{u}"), 16)

        @block.scalar
        def _(act):
            for k in range(KD):
                act.wait_ge(sem(f"ld_x{k % 2}"), 16 * (k // 2 + 1))
                nc.scalar.copy(xh[:, k, :], xraw[k % 2][:]).then_inc(sem("x_hi"), 1)

            def split(u, n):
                act.wait_ge(sem(f"ld_w{u}"), n)
                nc.scalar.copy(wh[u][:], wraw[u][:]).then_inc(sem("w_hi"), 1)

            split(0, 16)
            split(1, 16)

            def body(i, last=False):
                for u in range(2):
                    act.wait_ge(sem("mm"), 2 * i + (u + 1))
                    act.wait_ge(sem("s_mm"), 2 * i)
                    nc.scalar.copy(q[u][:], psq[u][:]).then_inc(sem("q"), 1)
                    if not last:
                        split(u, 16 * i + 32)

            with act.Fori(0, N // 2 - 1) as i:
                body(i)
            body(N // 2 - 1, last=True)

        @block.vector
        def _(dve):
            for k in range(KD):
                dve.wait_ge(sem("x_hi"), k + 1)
                nc.vector.tensor_tensor(xl[:, k, :], xraw[k % 2][:], xh[:, k, :].bitcast(F32), ALU.subtract).then_inc(sem("x_lo"), 1)

            def split(u, n):
                dve.wait_ge(sem("w_hi"), n)
                nc.vector.tensor_tensor(wl[u][:], wraw[u][:], wh[u][:].bitcast(F32), ALU.subtract).then_inc(sem("w_lo"), 1)

            split(0, 1)
            split(1, 2)

            def body(i, last=False):
                for u in range(2):
                    if not last:
                        split(u, 2 * i + (u + 3))
                for u in range(2):
                    dve.wait_ge(sem(f"st_s{u}"), 16 * i)
                    dve.wait_ge(sem("s_mm"), 2 * i + (u + 1))
                    nc.vector.tensor_copy(sout[u][:], pss[u][:].rearrange("p (t k) -> p t k", t=TT)).then_inc(sem("s_out"), 1)

            with dve.Fori(0, N // 2 - 1) as i:
                body(i)
            body(N // 2 - 1, last=True)

        @block.tensor
        def _(pe):
            pe.wait_ge(sem("x_lo"), KD)
            pe.wait_ge(sem("ld_k"), 16)

            def queries(i, u):
                pe.wait_ge(sem("w_lo"), 2 * i + (u + 1))
                pe.wait_ge(sem("q"), 2 * i)
                for h in range(2):
                    for k in range(KD):
                        for n, (a, b) in enumerate(float32r_products(wh, wl, xh, xl)):
                            ins = nc.tensor.matmul(psq[u][:, h * HALF:(h + 1) * HALF], a[u][:, k, :], b[:, k, h * HALF:(h + 1) * HALF],
                                                   start=(k == 0 and n == 0), stop=(k == KD - 1 and n == 2))
                ins.then_inc(sem("mm"), 1)

            def scores(i, u):
                pe.wait_ge(sem("q"), 2 * i + (u + 1))
                pe.wait_ge(sem("s_out"), 2 * i)
                for t in range(TT):
                    ins = nc.tensor.matmul(pss[u][:, t * PK:(t + 1) * PK], q[u][:, t * P:(t + 1) * P],
                                           keys[:, bass.ds(2 * i + u, 1), :].rearrange("p o k -> p (o k)"), start=True, stop=True)
                ins.then_inc(sem("s_mm"), 1)

            with pe.Fori(0, N // 2) as i:
                queries(i, 0)
                queries(i, 1)
                scores(i, 0)
                scores(i, 1)

        @block.gpsimd
        def _(pool):
            with pool.Fori(0, N // 2) as i:
                for u in range(2):
                    pool.wait_ge(sem("s_out"), 2 * i + (u + 1))
                    pool.dma_start(g.s[:, :, bass.ds(2 * i + u, 1), :].rearrange("t p o k -> p t (o k)"), sout[u][:]).then_inc(sem(f"st_s{u}"), 16)
            for u in range(2):
                pool.wait_ge(sem(f"st_s{u}"), 16 * (N // 2))


GONE = -3e38

def stage_down_and_route(nc, g):
    SLOTS = PK // TT
    GT = 8
    NG = P // GT
    sched = [0] * 4 + [2, 1, 1] * 4
    assert sum(sched) == NG and len(sched) == SLOTS
    HB = 2 * NG
    with ExitStack() as ctx:
        def sb(name, shape, dt=F32):
            return ctx.enter_context(nc.sbuf_tensor(name, shape, dt))

        sem = ctx.enter_context(stage_semaphores(nc, "r"))
        xh, xl = g.x1h, g.x1l
        draw = [sb(f"r_draw{u}", [P, KD, P]) for u in range(2)]
        dh = [sb(f"r_dh{u}", [P, KD, P], F32R) for u in range(2)]
        dl = [sb(f"r_dl{u}", [P, KD, P], F32R) for u in range(2)]
        act_out = [sb(f"r_act{u}", [P, T]) for u in range(2)]
        ident, iota = sb("r_ident", [P, P]), sb("r_iota", [P, P])
        st = sb("r_st", [P, 2 * PH, PK])
        val, idx = sb("r_val", [P, PH, 2, TOP]), sb("r_idx", [P, PH, 2, TOP], U32)
        keyf = sb("r_keyf", [P, PH, 2, TOP])
        cand = sb("r_cand", [P, PH, TOP, TOP])
        best, flat = sb("r_best", [P, PH, TOP]), sb("r_flat", [P, PH, TOP], U32)
        rank = sb("r_rank", [P, 2, PH, TOP], U32)
        rankf = sb("r_rankf", [P, 2, PH, TOP])
        zsum = sb("r_zsum", [P, PH])
        route = sb("r_route", [P, 3, PH, TOP])
        rt = sb("r_rt", [P, 3, P])
        oi = [sb(f"r_oi{u}", [P, GT, PK]) for u in range(2)]
        oj = [sb(f"r_oj{u}", [P, GT, PK]) for u in range(2)]
        W = sb("r_W", [P, PK, P])
        psd = [ctx.enter_context(nc.psum_tensor(f"r_psd{u}", [P, T], F32)) for u in range(2)]
        psw = [ctx.enter_context(nc.psum_tensor(f"r_psw{u}", [P, HALF], F32)) for u in range(2)]
        psT = ctx.enter_context(nc.psum_tensor("r_psT", [P, HALF], F32))
        block = ctx.enter_context(nc.Block())

        def groups_at(slot):
            first = sum(sched[:slot])
            return range(first, first + sched[slot])

        PIECES = 13

        @block.sync
        def _(sp):
            def load_d(c, n):
                sp.dma_start(draw[n][:], g.down[bass.ds(c, 1)].rearrange("o p k e -> (o p) k e")).then_inc(sem(f"ld_d{n}"), 16)

            def load_st(t):
                sp.dma_start(st[:], g.s[bass.ds(t, 1)].rearrange("o p n k -> (o p) n k")).then_inc(sem("ld_st"), 16)

            for d, s in ((ident, g.ident), (iota, g.iota)):
                sp.dma_start(d[:], s).then_inc(sem("ld_c"), 16)
            load_st(0)
            load_d(0, 0)
            load_d(1, 1)

            def store_W(t):
                for q in range(4):
                    sp.dma_start(g.W[q * 32:(q + 1) * 32, :, bass.ds(t * P, P)].rearrange("j p t -> p j t"),
                                 W[:, q * 32:(q + 1) * 32, :]).then_inc(sem("st_W"), 16)

            def tile(t, last=False):
                for s in range(SLOTS):
                    c, n = SLOTS * t + s, s % 2
                    if s == 0 and not last:
                        sp.wait_ge(sem("st_used"), t + 1)
                        load_st(t + 1)
                    if not (last and s >= SLOTS - 2):
                        sp.wait_ge(sem("d_lo"), c + 1)
                        load_d(c + 2, n)
                    sp.wait_ge(sem("gelu"), c + 1)
                    sp.dma_start(g.act[bass.ds(c, 1)].rearrange("o p t -> (o p) t"), act_out[n][:]).then_inc(sem(f"st_a{n}"), 16)
                sp.wait_ge(sem("W"), HB * t + HB)
                store_W(t)

            with sp.Fori(0, TT - 1) as t:
                tile(t)
            tile(TT - 1, last=True)
            sp.wait_ge(sem("st_W"), 64 * TT)
            for n in range(2):
                sp.wait_ge(sem(f"st_a{n}"), 16 * PK // 2)

        @block.scalar
        def _(act):
            def split_d(c, n, count):
                act.wait_ge(sem(f"ld_d{n}"), count)
                nc.scalar.copy(dh[n][:], draw[n][:]).then_inc(sem("d_hi"), 1)

            def topk_exp(t):
                act.wait_ge(sem("shifted"), t + 1)
                nc.scalar.activation(route[:, 2], route[:, 2], ACT.Exp).then_inc(sem("exp"), 1)

            def topk_turn(t):
                act.wait_ge(sem("onehot"), NG * t)
                act.wait_ge(sem("turned"), t + 1)
                nc.scalar.copy(rt[:], psT[:, 0:3 * P].rearrange("p (c t) -> p c t", t=P)).then_inc(sem("rt"), 1)

            split_d(0, 0, 16)
            split_d(1, 1, 16)
            topk_exp(0)
            topk_turn(0)

            def tile(t, last=False):
                for s in range(SLOTS):
                    c, n = SLOTS * t + s, s % 2
                    act.wait_ge(sem("d_mm"), c + 1)
                    act.wait_ge(sem(f"st_a{n}"), 16 * (SLOTS // 2) * t + 16 * (s // 2))
                    nc.scalar.activation(act_out[n][:], psd[n][:], ACT.Gelu).then_inc(sem("gelu"), 1)
                    if not (last and s >= SLOTS - 2):
                        split_d(c + 2, n, 16 * (SLOTS // 2) * t + 16 * (s // 2) + 32)
                    for m in groups_at(s):
                        if m == 0:
                            act.wait_ge(sem("st_W"), 64 * t)
                        for b in range(2):
                            act.wait_ge(sem("w_mm"), HB * t + (2 * m + b + 1))
                            nc.scalar.copy(W[:, :, m * GT + 4 * b:m * GT + 4 * b + 4].rearrange("p j t -> p t j"),
                                           psw[b][:].rearrange("p (t j) -> p t j", j=PK)).then_inc(sem("W"), 1)
                    if not last and s == 10:
                        topk_exp(t + 1)
                if not last:
                    topk_turn(t + 1)

            with act.Fori(0, TT - 1) as t:
                tile(t)
            tile(TT - 1, last=True)

        @block.gpsimd
        def _(pool):
            def gate(t, m):
                u = m % 2
                pool.wait_ge(sem("onehot"), NG * t + (m + 1))
                nc.gpsimd.tensor_tensor(oi[u][:], oi[u][:], rt[:, 2, m * GT:(m + 1) * GT].unsqueeze(2).broadcast_to([P, GT, PK]),
                                        ALU.mult).then_inc(sem("gated"), 1)

            def pick(t, side):
                pool.wait_ge(sem("eq"), 2 * t + (side + 1))
                nc.gpsimd.tensor_tensor(cand[:], cand[:], keyf[:, :, side, :].unsqueeze(2).broadcast_to([P, PH, TOP, TOP]),
                                        ALU.mult).then_inc(sem("picked"), 1)

            pick(0, 0)
            pick(0, 1)

            def tile(t, last=False):
                for s in range(SLOTS):
                    for m in groups_at(s):
                        gate(t, m)
                    if not last and s == 11:
                        pick(t + 1, 0)
                    if not last and s == 12:
                        pick(t + 1, 1)

            with pool.Fori(0, TT - 1) as t:
                tile(t)
            tile(TT - 1, last=True)

        @block.vector
        def _(dve):
            def split_d(c, n):
                dve.wait_ge(sem("d_hi"), c + 1)
                nc.vector.tensor_tensor(dl[n][:], draw[n][:], dh[n][:].bitcast(F32), ALU.subtract).then_inc(sem("d_lo"), 1)

            def topk(t, piece):
                def before():
                    wait_alone(dve, sem("pieces"), PIECES * t + piece, sem("passed"))

                done = None
                pairs = [(h, p, 2 * h + p) for h in range(PH) for p in range(2)]
                if piece == 0:
                    wait_alone(dve, sem("ld_st"), 16 * t + 16, sem("passed"))
                    before()
                    for h, p, n in pairs:
                        done = nc.vector.max(val[:, h, p, 0:8], st[:, n, :])
                elif piece == 1:
                    before()
                    for h, p, n in pairs:
                        done = nc.vector.max_index(idx[:, h, p, 0:8], val[:, h, p, 0:8], st[:, n, :])
                elif piece == 2:
                    before()
                    for h, p, n in pairs:
                        done = nc.vector.match_replace(out=st[:, n, :], in_to_replace=val[:, h, p, 0:8], in_values=st[:, n, :], imm_value=GONE)
                elif piece == 3:
                    before()
                    for h, p, n in pairs:
                        done = nc.vector.max(val[:, h, p, 8:16], st[:, n, :])
                elif piece == 4:
                    before()
                    for h, p, n in pairs:
                        done = nc.vector.max_index(idx[:, h, p, 8:16], val[:, h, p, 8:16], st[:, n, :])
                elif piece == 5:
                    before()
                    dve.sem_inc(sem("st_used"), 1)
                    nc.vector.tensor_copy(keyf[:], idx[:])
                    done = nc.vector.tensor_tensor(cand[:], val[:, :, 0, :].unsqueeze(3).broadcast_to([P, PH, TOP, TOP]),
                                                   val[:, :, 1, :].unsqueeze(2).broadcast_to([P, PH, TOP, TOP]), ALU.add)
                elif piece == 6:
                    before()
                    for h in range(PH):
                        done = nc.vector.max(best[:, h, 0:8], sums[:, h])
                elif piece == 7:
                    before()
                    for h in range(PH):
                        done = nc.vector.max_index(flat[:, h, 0:8], best[:, h, 0:8], sums[:, h])
                elif piece == 8:
                    before()
                    for h in range(PH):
                        done = nc.vector.match_replace(out=sums[:, h], in_to_replace=best[:, h, 0:8], in_values=sums[:, h], imm_value=GONE)
                elif piece == 9:
                    before()
                    for h in range(PH):
                        done = nc.vector.max(best[:, h, 8:16], sums[:, h])
                elif piece == 10:
                    before()
                    for h in range(PH):
                        nc.vector.max_index(flat[:, h, 8:16], best[:, h, 8:16], sums[:, h])
                    dve.wait_ge(sem("turned"), t)
                    nc.vector.tensor_tensor(route[:, 2], best[:], best[:, :, 0:1].broadcast_to([P, PH, TOP]), ALU.subtract).then_inc(sem("shifted"), 1)
                    dve.wait_ge(sem("shifted"), t + 1)
                    dve.sem_inc(sem("pieces"), 1)
                elif piece == 11:
                    before()
                    nc.vector.tensor_scalar(rank[:, 0], flat[:], 4, None, ALU.logical_shift_right)
                    nc.vector.tensor_scalar(rank[:, 1], flat[:], 15, None, ALU.bitwise_and).then_inc(sem("ranks"), 1)
                    wait_alone(dve, sem("ranks"), 2 * t + 1, sem("passed"))
                    nc.vector.tensor_copy(rankf[:], rank[:]).then_inc(sem("ranks"), 1)
                    dve.wait_ge(sem("ranks"), 2 * t + 2)
                    nc.vector.tensor_tensor(cand[:], rankf[:, 0].unsqueeze(3).broadcast_to([P, PH, TOP, TOP]),
                                            ranks16, ALU.is_equal).then_inc(sem("eq"), 1)
                    dve.wait_ge(sem("exp"), t + 1)
                    nc.vector.tensor_reduce(zsum[:], route[:, 2], AX.X, ALU.add).then_inc(sem("zsum"), 1)
                    dve.wait_ge(sem("zsum"), 2 * t + 1)
                    nc.vector.reciprocal(zsum[:], zsum[:]).then_inc(sem("zsum"), 1)
                    dve.wait_ge(sem("zsum"), 2 * t + 2)
                    done = nc.vector.tensor_tensor(route[:, 2], route[:, 2], zsum[:].unsqueeze(2).broadcast_to([P, PH, TOP]), ALU.mult)
                elif piece == 12:
                    dve.wait_ge(sem("picked"), 2 * t + 1)
                    nc.vector.tensor_reduce(route[:, 0], cand[:], AX.X, ALU.add).then_inc(sem("summed"), 1)
                    dve.wait_ge(sem("summed"), 2 * t + 1)
                    nc.vector.tensor_tensor(cand[:], rankf[:, 1].unsqueeze(3).broadcast_to([P, PH, TOP, TOP]),
                                            ranks16, ALU.is_equal).then_inc(sem("eq"), 1)
                    dve.wait_ge(sem("picked"), 2 * t + 2)
                    nc.vector.tensor_reduce(route[:, 1], cand[:], AX.X, ALU.add).then_inc(sem("summed"), 1)
                    dve.wait_ge(sem("summed"), 2 * t + 2)
                    before()
                    dve.sem_inc(sem("pieces"), 1)
                    dve.sem_inc(sem("routed"), 1)
                if done is not None:
                    done.then_inc(sem("pieces"), 1)

            sums = cand[:].rearrange("p h a b -> p h (a b)")
            ranks16 = iota[:, 0:TOP].unsqueeze(1).unsqueeze(1).broadcast_to([P, PH, TOP, TOP])

            split_d(0, 0)
            split_d(1, 1)
            dve.wait_ge(sem("ld_c"), 32)
            for piece in range(PIECES):
                topk(0, piece)

            def tile(t, last=False):
                for s in range(SLOTS):
                    c, n = SLOTS * t + s, s % 2
                    if s == 0:
                        dve.wait_ge(sem("rt"), t + 1)
                    for m in groups_at(s):
                        u = m % 2
                        if m < 2:
                            dve.wait_ge(sem("w_mm"), HB * t)
                        else:
                            dve.wait_ge(sem("w_mm"), HB * t + 2 * (m - 1))
                        keys = iota[:].unsqueeze(1).broadcast_to([P, GT, PK])
                        nc.vector.tensor_tensor(oj[u][:], keys, rt[:, 1, m * GT:(m + 1) * GT].unsqueeze(2).broadcast_to([P, GT, PK]), ALU.is_equal)
                        nc.vector.tensor_tensor(oi[u][:], keys, rt[:, 0, m * GT:(m + 1) * GT].unsqueeze(2).broadcast_to([P, GT, PK]),
                                                ALU.is_equal).then_inc(sem("onehot"), 1)
                    if not last and s < PIECES:
                        topk(t + 1, s)
                    if not (last and s >= SLOTS - 2):
                        split_d(c + 2, n)

            with dve.Fori(0, TT - 1) as t:
                tile(t)
            tile(TT - 1, last=True)

        @block.tensor
        def _(pe):
            def turn(t):
                pe.wait_ge(sem("routed"), t + 1)
                pe.wait_ge(sem("rt"), t)
                for c in range(3):
                    ins = nc.tensor.transpose(psT[:, c * P:(c + 1) * P], route[:, c].rearrange("p h a -> p (h a)"), ident[:])
                ins.then_inc(sem("turned"), 1)

            turn(0)

            def tile(t, last=False):
                for s in range(SLOTS):
                    c, n = SLOTS * t + s, s % 2
                    pe.wait_ge(sem("d_lo"), c + 1)
                    if s >= 2:
                        pe.wait_ge(sem("gelu"), c - 1)
                    else:
                        pe.wait_ge(sem("gelu"), SLOTS * t)
                    for h in range(2):
                        for k in range(KD):
                            for m, (a, b) in enumerate(float32r_products(dh, dl, xh, xl)):
                                ins = nc.tensor.matmul(psd[n][:, h * HALF:(h + 1) * HALF], a[n][:, k, :], b[:, k, h * HALF:(h + 1) * HALF],
                                                       start=(k == 0 and m == 0), stop=(k == KD - 1 and m == 2))
                    ins.then_inc(sem("d_mm"), 1)
                    for m in groups_at(s):
                        pe.wait_ge(sem("gated"), NG * t + (m + 1))
                        for b in range(2):
                            pe.wait_ge(sem("W"), HB * t + max(2 * m + b - 1, 0))
                            for k in range(4):
                                ins = nc.tensor.matmul(psw[b][:, k * PK:(k + 1) * PK], oi[m % 2][:, 4 * b + k, :], oj[m % 2][:, 4 * b + k, :],
                                                       start=True, stop=True)
                            ins.then_inc(sem("w_mm"), 1)
                    if not last and s == SLOTS - 1:
                        turn(t + 1)

            with pe.Fori(0, TT - 1) as t:
                tile(t)
            tile(TT - 1, last=True)


def stage_up(nc, g):
    NCH = PK
    G = 4
    NR = NCH // G
    NB = 8
    with ExitStack() as ctx:
        def sb(name, shape, dt=F32):
            return ctx.enter_context(nc.sbuf_tensor(name, shape, dt))

        sem = ctx.enter_context(stage_semaphores(nc, "e"))
        y = sb("e_y", [P, TT, D])
        uraw = [sb(f"e_uraw{u}", [P, D]) for u in range(2)]
        araw = [sb(f"e_araw{u}", [P, T]) for u in range(2)]
        Wt = [sb(f"e_W{u}", [P, T]) for u in range(2)]
        uh = [sb(f"e_uh{u}", [P, D], F32R) for u in range(2 * G)]
        ul = [sb(f"e_ul{u}", [P, D], F32R) for u in range(2 * G)]
        Ch = [sb(f"e_Ch{u}", [P, T], F32R) for u in range(2 * G)]
        Cl = [sb(f"e_Cl{u}", [P, T], F32R) for u in range(2 * G)]
        stats, mv = [sb(f"e_stats{u}", [P, 2, 6]) for u in range(2)], [sb(f"e_mv{u}", [P, 2]) for u in range(2)]
        rstd, power = [sb(f"e_rstd{u}", [P, 1]) for u in range(2)], sb("e_power", [P, 1])
        psy = [ctx.enter_context(nc.psum_tensor(f"e_psy{u}", [P, HALF], F32)) for u in range(NB)]
        block = ctx.enter_context(nc.Block())

        def scale(pool, t):
            pool.wait_ge(sem("normed"), t + 1)
            nc.gpsimd.tensor_tensor(y[:, t, :], y[:, t, :], araw[0][:], ALU.mult).then_inc(sem("scaled"), 1)

        def norm(dve, t):
            u = t % 2
            dve.wait_ge(sem("y_add"), 16 * (NR - 1) + 2 * t + 2)
            if t >= 2:
                dve.wait_ge(sem("rstd"), t - 1)
                dve.wait_ge(sem("normed"), t - 1)
            for h in range(2):
                ins = nc.vector.bn_stats(stats[u][:, h, :], y[:, t, h * HALF:(h + 1) * HALF])
            ins.then_inc(sem("stats"), 1)
            dve.wait_ge(sem("stats"), t + 1)
            nc.vector.bn_aggr(mv[u][:], stats[u][:]).then_inc(sem("aggr"), 1)
            dve.wait_ge(sem("aggr"), t + 1)
            nc.vector.tensor_scalar(mv[u][:, 1:2], mv[u][:, 1:2], 1e-5, None, ALU.add).then_inc(sem("var"), 1)
            dve.wait_ge(sem("rstd"), t + 1)
            nc.vector.tensor_scalar(y[:, t, :], y[:, t, :], mv[u][:, 0:1], rstd[u][:, 0:1], ALU.subtract, ALU.mult).then_inc(sem("normed"), 1)
            if t == 0:
                dve.wait_ge(sem("ld_ln"), 32)
            dve.wait_ge(sem("scaled"), t + 1)
            nc.vector.tensor_tensor(y[:, t, :], y[:, t, :], araw[1][:], ALU.add).then_inc(sem("final"), 1)

        @block.sync
        def _(sp):
            sp.dma_start(y[:], g.x1.rearrange("(t p) d -> p t d", p=P)).then_inc(sem("ld_y"), 16)

            def load(c, n):
                for d, s, name in ((araw, g.act, "A"), (Wt, g.W, "A"), (uraw, g.up, "u")):
                    sp.dma_start(d[n][:], s[bass.ds(c, 1)].rearrange("o p k -> (o p) k")).then_inc(sem(f"ld_{name}{n}"), 16)

            load(0, 0)
            load(1, 1)
            with sp.Fori(0, NCH // 2 - 1) as i:
                for n in range(2):
                    sp.wait_ge(sem("C_lo"), 2 * i + (n + 1))
                    load(2 * i + (n + 2), n)
            sp.wait_ge(sem("C_lo"), NCH)
            for d, s in ((araw[0], g.ln2_gain), (araw[1], g.ln2_bias)):
                sp.dma_start(d[:], s.partition_broadcast(P)).then_inc(sem("ld_ln"), 16)
            for t in range(TT):
                sp.wait_ge(sem("final"), t + 1)
                sp.dma_start(g.out[t * P:(t + 1) * P, :], y[:, t, :]).then_inc(sem("st_out"), 16)
            sp.wait_ge(sem("st_out"), 16 * TT)

        @block.scalar
        def _(act):
            def prepare(r, par, pair):
                for q in range(G):
                    c, n, s = G * r + q, q % 2, par * G + q
                    act.wait_ge(sem(f"ld_u{n}"), 16 * (G // 2) * r + 16 * (q // 2 + 1))
                    if q == 0 and pair is not None:
                        act.wait_ge(sem("y_mm"), pair)
                    nc.scalar.copy(uh[s][:], uraw[n][:]).then_inc(sem("u_hi"), 1)
                    act.wait_ge(sem("weighted"), c + 1)
                    nc.scalar.copy(Ch[s][:], araw[n][:]).then_inc(sem("C_hi"), 1)

            prepare(0, 0, None)
            prepare(1, 1, None)
            with act.Fori(0, NR // 2 - 1) as i:
                for par in range(2):
                    prepare(2 * i + (2 + par), par, 32 * i + 16 * (par + 1))

        @block.gpsimd
        def _(pool):
            nc.gpsimd.memset(power[:], -0.5).then_inc(sem("power"), 1)
            with pool.Fori(0, NCH // 2) as i:
                for n in range(2):
                    pool.wait_ge(sem(f"ld_A{n}"), 32 * i + 32)
                    nc.gpsimd.tensor_tensor(araw[n][:], araw[n][:], Wt[n][:], ALU.mult).then_inc(sem("weighted"), 1)
            pool.wait_ge(sem("power"), 1)
            pool.wait_ge(sem("ld_ln"), 32)
            for t in range(TT):
                pool.wait_ge(sem("var"), t + 1)
                nc.gpsimd.tensor_tensor(rstd[t % 2][:], mv[t % 2][:, 1:2], power[:], ALU.pow).then_inc(sem("rstd"), 1)
                scale(pool, t)

        @block.vector
        def _(dve):
            dve.wait_ge(sem("ld_y"), 16)
            nc.vector.tensor_scalar(y[:], y[:], ALPHA, None, ALU.mult).then_inc(sem("y_init"), 1)
            dve.wait_ge(sem("y_init"), 1)

            def low(r, par, q):
                c, n, s = G * r + q, q % 2, par * G + q
                dve.wait_ge(sem("u_hi"), c + 1)
                nc.vector.tensor_tensor(ul[s][:], uraw[n][:], uh[s][:].bitcast(F32), ALU.subtract)
                dve.wait_ge(sem("C_hi"), c + 1)
                nc.vector.tensor_tensor(Cl[s][:], araw[n][:], Ch[s][:].bitcast(F32), ALU.subtract).then_inc(sem("C_lo"), 1)

            def add(r, b):
                dve.wait_ge(sem("y_mm"), 16 * r + (b + 1))
                o = y[:, b // 2, b % 2 * HALF:(b % 2 + 1) * HALF]
                nc.vector.tensor_tensor(o, o, psy[b % NB][:], ALU.add).then_inc(sem("y_add"), 1)

            for par in range(2):
                for q in range(G):
                    low(par, par, q)
            with dve.Fori(0, NR // 2 - 1) as i:
                for par in range(2):
                    for b in range(2 * TT):
                        add(2 * i + par, b)
                    for q in range(G):
                        low(2 * i + (2 + par), par, q)
            for r in (NR - 2, NR - 1):
                for b in range(2 * TT):
                    add(r, b)
                    if r == NR - 1 and b % 2:
                        norm(dve, b // 2)

        @block.tensor
        def _(pe):
            def up(r, par, first=False):
                pe.wait_ge(sem("C_lo"), G * r + G)
                for b in range(2 * TT):
                    t, h = b // 2, b % 2
                    if not first or b >= NB:
                        pe.wait_ge(sem("y_add"), 16 * r + (b - NB + 1))
                    for q in range(G):
                        s = G * par + q
                        for m, (a, v) in enumerate(float32r_products(Ch, Cl, uh, ul)):
                            ins = nc.tensor.matmul(psy[b % NB][:], a[s][:, t * P:(t + 1) * P], v[s][:, h * HALF:(h + 1) * HALF],
                                                   start=(q == 0 and m == 0), stop=(q == G - 1 and m == 2))
                    ins.then_inc(sem("y_mm"), 1)

            up(0, 0, first=True)
            up(1, 1)
            with pe.Fori(1, NR // 2) as i:
                for par in range(2):
                    up(2 * i + par, par)


def build_program(nc, g):
    def dram(name, shape):
        return nc.dram_tensor(name, shape, F32, kind="Internal").ap()

    g.hT = dram("hT", (N_IN, P, T))
    g.ba = dram("ba", (P, TT, 2 * DH))
    g.y = dram("y", (2 * AT, P, T))
    g.x1 = dram("x1", (T, D))
    g.x1T = dram("x1T", (KD, P, T))
    g.s = dram("s", (TT, P, 2 * PH, PK))
    g.act = dram("act", (PK, P, T))
    g.W = dram("W", (PK, P, T))
    stage_project(nc, g)
    stage_attention(nc, g)
    stage_deltanet(nc, g)
    with nc.sbuf_tensor("merged", [P, KD, T], F32) as merged:
        g.merged = merged
        stage_merge(nc, g)
        stage_out_norm(nc, g)
    with nc.sbuf_tensor("x1h", [P, KD, T], F32R) as g.x1h, nc.sbuf_tensor("x1l", [P, KD, T], F32R) as g.x1l:
        stage_scores(nc, g)
        stage_down_and_route(nc, g)
    stage_up(nc, g)


def host_constants():
    inv = (np.float32(10000.0) ** (-np.arange(0, AD, 2, dtype=np.float32) / np.float32(AD))).astype(np.float32)
    ang = (np.arange(T, dtype=np.float32)[:, None] * inv[None, :]).astype(np.float32)
    c, s = np.cos(ang).T, np.sin(ang).T
    d = np.arange(P)[:, None] - np.arange(T)[None, :] + (T - P)
    n = np.zeros(d.shape, np.float64)
    for window, r in ((128, 1), (512, 4), (2048, 16)):
        n += (d >= 0) & (d % r == 0) & (d <= window)
    bias = np.where(n > 0, np.log(np.maximum(n, 1.0)) * AD ** 0.5, NEG)
    i = np.arange(P)
    later = (i[None, :] >= i[:, None])
    level = np.zeros((P, 7, P), np.float32)
    for n in range(7):
        b = 1 << n
        same = (i[None, :] // (2 * b)) == (i[:, None] // (2 * b))
        level[:, n, :] = same & (i[:, None] // b % 2 == 0) & (i[None, :] // b % 2 == 1)
    return {
        "ident": np.eye(P, dtype=np.float32),
        "cos": np.ascontiguousarray(np.concatenate([c] * 4).astype(np.float32)),
        "sin": np.ascontiguousarray(np.concatenate([-s, s] * 2).astype(np.float32)),
        "bias": bias.astype(np.float32),
        "upto": later.astype(np.float32),
        "notlater": np.where(later, 0.0, NEG).astype(np.float32),
        "level": level,
        "iota": np.tile(np.arange(P, dtype=np.float32), (P, 1)),
    }


class Arrays:
    pass


def kernel(**inputs):
    import concourse.bacc as bacc
    from concourse.bass_utils import run_bass_kernel_spmd

    a = {k: np.asarray(v) for k, v in inputs.items()}
    w_in = a["w_in"][0]
    ba0 = 3 * AW + 3 * DW
    cols = np.r_[0:ba0, ba0 + 2 * DH:w_in.shape[1]]
    arrays = {
        "x": a["x"][0],
        "xT": a["x"][0].T,
        "w_in": w_in[:, cols].reshape(KD, P, N_IN, P).transpose(2, 1, 0, 3),
        "w_ba": w_in[:, ba0:ba0 + 2 * DH],
        "conv": a["dn_conv"][0].reshape(CONV, N_DN, P).transpose(2, 1, 0),
        "a_log": a["dn_A_log"][0],
        "dt_bias": a["dn_dt_bias"][0],
        "norm_gain": a["dn_norm_gain"][0][:, None],
        "w_branch": np.concatenate([a["w_branch_attn"][0], a["w_branch_delta"][0]]).reshape(2 * AT, P, KD, P).transpose(2, 1, 0, 3),
        "w_out": a["w_out"][0],
        "ln1_gain": a["ln1_gain"][0],
        "ln1_bias": a["ln1_bias"][0],
        "w_query": a["peer_w_query"][0].reshape(KD, P, 2 * PH, P).transpose(2, 1, 0, 3),
        "keys": a["peer_sub_keys"][0].reshape(2 * PH, PK, P).transpose(0, 2, 1),
        "down": a["peer_expert_down"][0].reshape(PK, PK, KD, P).transpose(1, 3, 2, 0),
        "up": a["peer_expert_up"][0].reshape(PK, PK, D).transpose(1, 0, 2),
        "ln2_gain": a["ln2_gain"][0],
        "ln2_bias": a["ln2_bias"][0],
        **host_constants(),
    }
    nc = bacc.Bacc("TRN2", target_bir_lowering=False, num_devices=1)
    g = Arrays()
    given = {}
    for name, v in arrays.items():
        v = np.ascontiguousarray(v)
        given[f"in_{name}"] = v
        g.__dict__[name] = nc.dram_tensor(f"in_{name}", v.shape, mybir.dt.from_np(v.dtype), kind="ExternalInput").ap()
    g.out = nc.dram_tensor("out", (T, D), F32, kind="ExternalOutput").ap()
    build_program(nc, g)
    r = run_bass_kernel_spmd(nc, [given], core_ids=[0])
    return r.results[0]["out"].reshape(1, T, D)
```

```python
import math

import numpy as np

import concourse.bass as bass
from concourse import mybir
from contextlib import ExitStack, contextmanager

F32 = mybir.dt.float32
F32R = mybir.dt.float32r
U32 = mybir.dt.uint32
ALU = mybir.AluOpType
ACT = mybir.ActivationFunctionType
AX = mybir.AxisListType

P = 128
D = 1024
T = 1024
KD = D // P
TT = T // P
HALF = 512
AH, AD = 12, 64
AW = AH * AD
AT = AW // P
DH, DD = 6, 128
DW = DH * DD
CONV = 4
N_ATT = 3 * AT
N_DN = 3 * DH
N_GB = DH
N_BR = 2 * KD
N_IN = N_ATT + N_DN + N_GB + N_BR
PH, PK, TOP = 8, 128, 16
ALPHA = 2.0 ** 0.25
NEG = -1e30


class Step:

    def __init__(self, sem, base=0):
        self.sem, self.base, self.n = sem, base, 0

    def inc(self, ins, by=1):
        self.n += by
        ins.then_inc(self.sem, by)
        return self.at()

    def at(self, back=0):
        return START + self.base + (self.n - back)

    def wait(self, eng, back=0):
        eng.wait_ge(self.sem, self.at(back))


START = 1


@contextmanager
def stage_semaphores(nc, prefix, names):
    held = {name: nc.alloc_semaphore(f"{prefix}_{name}") for name in names.split()}
    for s in held.values():
        nc.gpsimd.sem_inc(s, START)
    nc.all_engine_barrier()
    yield held.__getitem__
    nc.clear_and_free_semaphores(list(held.values()))
    nc.all_engine_barrier()


def wait_alone(eng, sem, value, passed):
    eng.wait_ge(sem, value)
    eng.sem_inc(passed, 1)


def stage_project(nc, g):
    with ExitStack() as ctx:
        def sb(name, shape, dt=F32):
            return ctx.enter_context(nc.sbuf_tensor(name, shape, dt))

        sem = ctx.enter_context(stage_semaphores(nc, "p",
            "ld_x0 ld_x1 ld_w0 ld_w1 ld_c x_hi x_lo w_hi w_lo mm_done ba_done ba_out ba_st out_ready "
            "cin_ready cout_ready conv_step zeroed stored0 stored1"))

        xh, xl = sb("p_xh", [P, KD, T], F32R), sb("p_xl", [P, KD, T], F32R)
        xraw = [sb(f"p_xraw{u}", [P, T]) for u in range(2)]
        wraw = [sb(f"p_wraw{u}", [P, KD, P]) for u in range(2)]
        wh = [sb(f"p_wh{u}", [P, KD, P], F32R) for u in range(2)]
        wl = [sb(f"p_wl{u}", [P, KD, P], F32R) for u in range(2)]
        cin = [sb(f"p_cin{u}", [P, CONV - 1 + T]) for u in range(2)]
        cout = [sb(f"p_cout{u}", [P, T]) for u in range(2)]
        out = [sb(f"p_out{u}", [P, T]) for u in range(2)]
        cw = sb("p_cw", [P, N_DN, CONV])
        wba = sb("p_wba", [P, KD, 2 * DH])
        ba = sb("p_ba", [P, TT, 2 * DH])
        xba = sb("p_xba", [P, KD, T])
        ps = [ctx.enter_context(nc.psum_tensor(f"p_ps{u}", [P, T], F32)) for u in range(2)]
        psb = ctx.enter_context(nc.psum_tensor("p_psb", [P, HALF], F32))

        ld_x = [sem(f"ld_x{u}") for u in range(2)]
        ld_w = [sem(f"ld_w{u}") for u in range(2)]
        ld_c = sem("ld_c")
        x_hi, x_lo = sem("x_hi"), sem("x_lo")
        w_hi, w_lo = sem("w_hi"), sem("w_lo")
        mm_done = sem("mm_done")
        ba_done, ba_out, ba_st = sem("ba_done"), sem("ba_out"), sem("ba_st")
        out_ready = sem("out_ready")
        cin_ready, cout_ready, conv_step = sem("cin_ready"), sem("cout_ready"), sem("conv_step")
        zeroed = sem("zeroed")
        stored = [sem(f"stored{u}") for u in range(2)]
        block = ctx.enter_context(nc.Block())
        pairs = N_IN // 2
        att, dn, gb = N_ATT // 2, N_DN // 2, N_GB // 2

        @block.sync
        def _(sp):
            for k in range(KD):
                if k >= 2:
                    sp.wait_ge(x_lo, START + k - 1)
                sp.dma_start(xraw[k % 2][:], g.xT[k * P:(k + 1) * P, :]).then_inc(ld_x[k % 2], 16)
                if k < 2:
                    sp.dma_start(wraw[k][:], g.w_in[k]).then_inc(ld_w[k], 16)
            sp.dma_start(wba[:], g.w_ba.rearrange("(k p) c -> p k c", p=P)).then_inc(ld_c, 16)
            sp.dma_start(cw[:], g.conv).then_inc(ld_c, 16)
            sp.dma_start(xba[:], g.xT.rearrange("(k p) t -> p k t", p=P)).then_inc(ld_c, 16)
            sp.wait_ge(ba_out, START + 1)
            sp.dma_start(g.ba, ba[:]).then_inc(ba_st, 16)

            def store(i, u):
                sp.wait_ge(out_ready, START + 2 * i + (u + 1))
                sp.dma_start(g.hT[bass.ds(2 * i + u, 1)].rearrange("o p t -> (o p) t"), out[u][:]).then_inc(stored[u], 16)

            with sp.Fori(0, pairs - 1) as i:
                for u in range(2):
                    sp.wait_ge(w_lo, START + 2 * i + (u + 1))
                    sp.dma_start(wraw[u][:], g.w_in[bass.ds(2 * i + (2 + u), 1)].rearrange("o p k c -> (o p) k c")).then_inc(ld_w[u], 16)
                    store(i, u)
            for u in range(2):
                store(pairs - 1, u)
            sp.wait_ge(ba_st, START + 16)
            for u in range(2):
                sp.wait_ge(stored[u], START + 16 * pairs)

        @block.scalar
        def _(act):
            for k in range(KD):
                act.wait_ge(ld_x[k % 2], START + 16 * (k // 2 + 1))
                nc.scalar.copy(xh[:, k, :], xraw[k % 2][:]).then_inc(x_hi, 1)

            def split(u, n):
                act.wait_ge(ld_w[u], START + n)
                nc.scalar.copy(wh[u][:], wraw[u][:]).then_inc(w_hi, 1)

            split(0, 16)
            split(1, 16)

            def body(i, kind, last=False):
                for u in range(2):
                    act.wait_ge(mm_done, START + 2 * i + (u + 1))
                    if kind == "conv":
                        j = i - att
                        act.wait_ge(cout_ready, START + 2 * j + u)
                        nc.scalar.copy(cin[u][:, CONV - 1:], ps[u][:]).then_inc(cin_ready, 1)
                    else:
                        act.wait_ge(stored[u], START + 16 * i)
                        f = {"att": ACT.Copy, "gb": ACT.Silu, "br": ACT.Sigmoid}[kind]
                        nc.scalar.activation(out[u][:], ps[u][:], f).then_inc(out_ready, 1)
                    if not last:
                        split(u, 16 * i + 32)
                    if kind == "conv":
                        act.wait_ge(cout_ready, START + 2 * j + (u + 1))
                        act.wait_ge(stored[u], START + 16 * i)
                        nc.scalar.activation(out[u][:], cout[u][:], ACT.Silu).then_inc(out_ready, 1)

            act.wait_ge(zeroed, START + 2)
            with act.Fori(0, att) as i:
                body(i, "att")
            with act.Fori(att, att + dn) as i:
                body(i, "conv")
            with act.Fori(att + dn, att + dn + gb) as i:
                body(i, "gb")
            with act.Fori(att + dn + gb, pairs - 1) as i:
                body(i, "br")
            body(pairs - 1, "br", last=True)

        @block.vector
        def _(dve):
            nc.vector.memset(cin[0][:, 0:CONV - 1], 0.0).then_inc(zeroed, 1)
            nc.vector.memset(cin[1][:, 0:CONV - 1], 0.0).then_inc(zeroed, 1)
            for k in range(KD):
                dve.wait_ge(x_hi, START + k + 1)
                nc.vector.tensor_tensor(xl[:, k, :], xraw[k % 2][:], xh[:, k, :].bitcast(F32), ALU.subtract).then_inc(x_lo, 1)

            def split(u, n):
                dve.wait_ge(w_hi, START + n)
                nc.vector.tensor_tensor(wl[u][:], wraw[u][:], wh[u][:].bitcast(F32), ALU.subtract).then_inc(w_lo, 1)

            split(0, 1)
            split(1, 2)
            dve.wait_ge(ba_done, START + 1)
            nc.vector.tensor_copy(ba[:], psb[:, 0:TT * 2 * DH].rearrange("p (t c) -> p t c", t=TT)).then_inc(ba_out, 1)
            dve.wait_ge(ld_c, START + 48)

            def body(i, conv):
                for u in range(2):
                    if conv:
                        j = i - att
                        step = Step(conv_step, 6 * j + 3 * u)
                        dve.wait_ge(cin_ready, START + 2 * j + (u + 1))
                        dve.wait_ge(out_ready, START + 2 * i + u)
                        w = [cw[:, bass.ds(2 * j + u, 1), t:t + 1].rearrange("p a b -> p (a b)") for t in range(CONV)]
                        step.inc(nc.vector.tensor_scalar(cout[u][:], cin[u][:, 0:T], w[0], None, ALU.mult))
                        for t in range(1, CONV):
                            step.wait(dve)
                            ins = nc.vector.scalar_tensor_tensor(cout[u][:], cin[u][:, t:t + T], w[t], cout[u][:],
                                                                 ALU.mult, ALU.add)
                            if t < CONV - 1:
                                step.inc(ins)
                        ins.then_inc(cout_ready, 1)
                    split(u, 2 * i + (u + 3))

            with dve.Fori(0, att) as i:
                body(i, False)
            with dve.Fori(att, att + dn) as i:
                body(i, True)
            with dve.Fori(att + dn, pairs - 1) as i:
                body(i, False)

        @block.tensor
        def _(pe):
            pe.wait_ge(ld_c, START + 48)
            for t in range(TT):
                for k in range(KD):
                    ins = nc.tensor.matmul(psb[:, t * 2 * DH:(t + 1) * 2 * DH], xba[:, k, t * P:(t + 1) * P],
                                           wba[:, k, :], start=(k == 0), stop=(k == KD - 1))
            ins.then_inc(ba_done, 1)
            pe.wait_ge(x_lo, START + KD)
            with pe.Fori(0, pairs) as i:
                for u in range(2):
                    pe.wait_ge(w_lo, START + 2 * i + (u + 1))
                    for h in range(2):
                        o = ps[u][:, h * HALF:(h + 1) * HALF]
                        for k in range(KD):
                            for n, (a, b) in enumerate(((wh, xh), (wh, xl), (wl, xh))):
                                ins = nc.tensor.matmul(o, a[u][:, k, :], b[:, k, h * HALF:(h + 1) * HALF],
                                                       start=(k == 0 and n == 0), stop=(k == KD - 1 and n == 2))
                    ins.then_inc(mm_done, 1)


def stage_attention(nc, g):
    HPT = P // AD
    ITEMS = HPT * TT
    groups = [1 + qt // 4 for qt in range(TT)] * HPT
    through = [sum(groups[:n + 1]) for n in range(ITEMS)]
    G = sum(groups)
    with ExitStack() as ctx:
        def sb(name, shape, dt=F32):
            return ctx.enter_context(nc.sbuf_tensor(name, shape, dt))

        sem = ctx.enter_context(stage_semaphores(nc, "a",
            "ld_c ld_v ld_q v_tr v_out rope_step rope_done s_done masked max_ready exp_done tr_done pT_ready "
            "pv_done recip_done o_out y_tr y_out passed stored"))

        cos, sin = sb("a_cos", [P, T]), sb("a_sin", [P, T])
        bias, ident = sb("a_bias", [P, T]), sb("a_ident", [P, P])
        vT, V = sb("a_vT", [P, AT, T]), sb("a_V", [P, TT, AW])
        raw = [sb(f"a_raw{n}", [P, T]) for n in range(4)]
        q, k = sb("a_q", [P, T]), sb("a_k", [P, T])
        sc = [sb(f"a_sc{u}", [P, T]) for u in range(2)]
        pb = [sb(f"a_pb{u}", [P, T]) for u in range(2)]
        pT = [sb(f"a_pT{u}", [P, TT, P]) for u in range(2)]
        ya, yaT = sb("a_ya", [P, TT, AW]), sb("a_yaT", [P, AT, T])
        mx, nm = sb("a_mx", [P, ITEMS]), sb("a_nm", [P, ITEMS])
        rs, ri = sb("a_rs", [P, ITEMS]), sb("a_ri", [P, ITEMS])
        psS = [ctx.enter_context(nc.psum_tensor(f"a_psS{u}", [P, T], F32)) for u in range(2)]
        psT = [ctx.enter_context(nc.psum_tensor(f"a_psT{u}", [P, HALF], F32)) for u in range(2)]
        psO = [ctx.enter_context(nc.psum_tensor(f"a_psO{u}", [P, HALF], F32)) for u in range(2)]

        ld_c, ld_v, ld_q = sem("ld_c"), sem("ld_v"), sem("ld_q")
        v_tr, v_out = sem("v_tr"), sem("v_out")
        rope_step, rope_done = sem("rope_step"), sem("rope_done")
        s_done, masked, max_ready = sem("s_done"), sem("masked"), sem("max_ready")
        exp_done, tr_done, pT_ready = sem("exp_done"), sem("tr_done"), sem("pT_ready")
        pv_done, recip_done, o_out = sem("pv_done"), sem("recip_done"), sem("o_out")
        y_tr, y_out, passed, stored = sem("y_tr"), sem("y_out"), sem("passed"), sem("stored")
        block = ctx.enter_context(nc.Block())

        def evac(act, i, n, grp):
            qt = n % TT
            for b in range(groups[n]):
                act.wait_ge(tr_done, START + G * i + (grp + 1))
                act.wait_ge(pv_done, START + ITEMS * i + max(n - 1, 0))
                w = min(4, qt + 1 - 4 * b)
                nc.scalar.copy(pT[n % 2][:, 4 * b:4 * b + w, :],
                               psT[grp % 2][:, 0:w * P].rearrange("p (a t) -> p a t", t=P)).then_inc(pT_ready, 1)
                grp += 1
            return grp

        @block.sync
        def _(sp):
            sp.dma_start(vT[:], g.hT[2 * AT:3 * AT].rearrange("n p t -> p n t")).then_inc(ld_v, 16)
            for d, s in ((ident, g.ident), (cos, g.cos), (sin, g.sin), (bias, g.bias)):
                sp.dma_start(d[:], s).then_inc(ld_c, 16)
            with sp.Fori(0, AT) as i:
                sp.wait_ge(rope_done, START + i * 2)
                for n, first in ((0, 0), (2, AT)):
                    src = g.hT[bass.ds(i + first, 1)].rearrange("o p t -> (o p) t")
                    sp.dma_start(raw[n][:], src).then_inc(ld_q, 16)
                    for r in range(4):
                        s = r ^ 1
                        sp.dma_start(raw[n + 1][32 * r:32 * r + 32, :], src[32 * s:32 * s + 32, :]).then_inc(ld_q, 16)
            sp.wait_ge(y_out, START + 2 * TT)
            sp.dma_start(g.y[0:AT].rearrange("n p t -> p n t"), yaT[:]).then_inc(stored, 16)
            sp.wait_ge(stored, START + 16)

        @block.scalar
        def _(act):
            with act.Fori(0, AT) as i:
                grp = 0
                for n in range(ITEMS):
                    N = (n % TT + 1) * P
                    act.wait_ge(max_ready, START + ITEMS * i + (n + 1))
                    act.wait_ge(tr_done, START + (G * i + (through[n - 2] if n >= 2 else 0)))
                    nc.scalar.activation(pb[n % 2][:, 0:N], sc[n % 2][:, 0:N], ACT.Exp, bias=nm[:, n:n + 1],
                                         accum_out=rs[:, n:n + 1]).then_inc(exp_done, 1)
                    if n >= 1:
                        grp = evac(act, i, n - 1, grp)
                grp = evac(act, i, ITEMS - 1, grp)

        @block.vector
        def _(dve):
            for kb in range(TT):
                for h in range(2):
                    n = 2 * kb + h
                    dve.wait_ge(v_tr, START + n + 1)
                    nc.vector.tensor_copy(V[:, kb, h * 384:(h + 1) * 384], psT[h][:, 0:384]).then_inc(v_out, 1)
            dve.wait_ge(ld_c, START + 64)
            with dve.Fori(0, AT) as i:
                dve.wait_ge(ld_q, START + 160 * (i + 1))
                step = Step(rope_step, 4 * i)
                for n, o in ((0, q), (2, k)):
                    nc.vector.tensor_tensor(o[:], raw[n][:], cos[:], ALU.mult)
                    step.inc(nc.vector.tensor_tensor(raw[n + 1][:], raw[n + 1][:], sin[:], ALU.mult), 2)
                    step.wait(dve)
                    nc.vector.tensor_tensor(o[:], o[:], raw[n + 1][:], ALU.add).then_inc(rope_done, 1)

                def out(n):
                    h, qt = n // TT, n % TT
                    dve.wait_ge(exp_done, START + ITEMS * i + (n + 1))
                    nc.vector.reciprocal(ri[:, n:n + 1], rs[:, n:n + 1]).then_inc(recip_done, 1)
                    dve.wait_ge(recip_done, START + ITEMS * i + (n + 1))
                    dve.wait_ge(pv_done, START + ITEMS * i + (n + 1))
                    nc.vector.tensor_scalar(ya[:, qt, bass.ds(i * P + h * AD, AD)], psO[n % 2][:, 0:AD],
                                            ri[:, n:n + 1], None, ALU.mult).then_inc(o_out, 1)

                for n in range(ITEMS):
                    qt = n % TT
                    N = (qt + 1) * P
                    dve.wait_ge(exp_done, START + ITEMS * i + max(n - 1, 0))
                    wait_alone(dve, s_done, START + ITEMS * i + (n + 1), passed)
                    nc.vector.tensor_tensor_reduce(out=sc[n % 2][:, 0:N], in0=psS[n % 2][:, 0:N],
                                                   in1=bias[:, T - N:T], scale=AD ** -0.5, scalar=NEG,
                                                   op0=ALU.add, op1=ALU.max,
                                                   accum_out=mx[:, n:n + 1]).then_inc(masked, 1)
                    dve.wait_ge(masked, START + ITEMS * i + (n + 1))
                    nc.vector.tensor_scalar(nm[:, n:n + 1], mx[:, n:n + 1], -1.0, None, ALU.mult).then_inc(max_ready, 1)
                    if n >= 2:
                        out(n - 2)
                out(ITEMS - 2)
                out(ITEMS - 1)
            for kb in range(TT):
                for h in range(2):
                    n = 2 * kb + h
                    dve.wait_ge(y_tr, START + n + 1)
                    nc.vector.tensor_copy(yaT[:, 3 * h:3 * h + 3, kb * P:(kb + 1) * P],
                                          psT[h][:, 0:384].rearrange("p (a t) -> p a t", t=P)).then_inc(y_out, 1)

        @block.tensor
        def _(pe):
            pe.wait_ge(ld_c, START + 64)
            pe.wait_ge(ld_v, START + 16)
            for kb in range(TT):
                for h in range(2):
                    n = 2 * kb + h
                    if n >= 2:
                        pe.wait_ge(v_out, START + n - 1)
                    for a in range(3):
                        ins = nc.tensor.transpose(psT[h][:, a * P:(a + 1) * P], vT[:, 3 * h + a, kb * P:(kb + 1) * P], ident[:])
                    ins.then_inc(v_tr, 1)
            pe.wait_ge(v_out, START + 2 * TT)

            with pe.Fori(0, AT) as i:
                def scores(n):
                    h, qt = n // TT, n % TT
                    N = (qt + 1) * P
                    pe.wait_ge(masked, START + ITEMS * i + max(n - 1, 0))
                    for a in range(0, N, HALF):
                        b = min(a + HALF, N)
                        ins = nc.tensor.matmul(psS[n % 2][:, a:b], q[h * AD:(h + 1) * AD, qt * P:(qt + 1) * P],
                                               k[h * AD:(h + 1) * AD, a:b], start=True, stop=True)
                    ins.then_inc(s_done, 1)

                def values(n):
                    h, qt = n // TT, n % TT
                    pe.wait_ge(pT_ready, START + G * i + through[n])
                    pe.wait_ge(o_out, START + ITEMS * i + max(n - 1, 0))
                    for kb in range(qt + 1):
                        ins = nc.tensor.matmul(psO[n % 2][:, 0:AD], pT[n % 2][:, kb, :],
                                               V[:, kb, bass.ds(i * P + h * AD, AD)], start=(kb == 0), stop=(kb == qt))
                    ins.then_inc(pv_done, 1)

                pe.wait_ge(rope_done, START + 2 * i + 2)
                scores(0)
                grp = 0
                for n in range(ITEMS):
                    if n + 1 < ITEMS:
                        scores(n + 1)
                    pe.wait_ge(exp_done, START + ITEMS * i + (n + 1))
                    for b in range(groups[n]):
                        pe.wait_ge(pT_ready, START + G * i + max(grp - 1, 0))
                        for kb in range(4 * b, min(4 * b + 4, n % TT + 1)):
                            ins = nc.tensor.transpose(psT[grp % 2][:, kb % 4 * P:(kb % 4 + 1) * P],
                                                      pb[n % 2][:, kb * P:(kb + 1) * P], ident[:])
                        ins.then_inc(tr_done, 1)
                        grp += 1
                    if n >= 1:
                        values(n - 1)
                values(ITEMS - 1)
            pe.wait_ge(o_out, START + ITEMS * AT)
            for kb in range(TT):
                for h in range(2):
                    n = 2 * kb + h
                    if n >= 2:
                        pe.wait_ge(y_out, START + n - 1)
                    for a in range(3):
                        ins = nc.tensor.transpose(psT[h][:, a * P:(a + 1) * P], ya[:, kb, (3 * h + a) * P:(3 * h + a + 1) * P], ident[:])
                    ins.then_inc(y_tr, 1)


def stage_deltanet(nc, g):
    C = P
    NC = T // C
    HH = DH // 2
    W = HH * P
    LEVELS = 7
    with ExitStack() as ctx:
        def sb(name, shape, dt=F32):
            return ctx.enter_context(nc.sbuf_tensor(name, shape, dt))

        def full(name):
            return sb(name, [P, 2, HH, P])

        sem = ctx.enter_context(stage_semaphores(nc, "d",
            "ld_c tr1 ld_qkv y_out ld_gate stored ones sumsq tk rnorm chunk_factors w_mm tkb tq tqd state_mm "
            "kd kg M X_mm LT state decayed out_sumsq out_rnorm beta exp z_abs ez G_ready exps squares tr2 qT "
            "kbT decay decay_exp T_tr T_first X w vn_mm vn o_mm out_squares z g G_mm g_copied rowG vb ss_raw "
            "kT qdT decay_step kk_mm qk T0 TX_mm T TT so_raw on on_tr"))

        ident, upto, later = sb("d_ident", [P, P]), sb("d_upto", [P, P]), sb("d_later", [P, P])
        level = sb("d_level", [P, LEVELS, P])
        ones, half_power = sb("d_ones", [P, P]), sb("d_half_power", [P, 2 * DH])
        ba, z = sb("d_ba", [P, NC, 2 * DH]), sb("d_z", [P, NC, DH])
        neg_a, dtb, gain = sb("d_neg_a", [P, DH]), sb("d_dtb", [P, DH]), sb("d_gain", [P, 1])
        ez, gg = sb("d_ez", [P, NC, DH]), sb("d_gg", [P, NC, DH])
        beta, eG, eK, gl = (sb(f"d_{n}", [P, NC, DH]) for n in ("beta", "eG", "eK", "gl"))
        Gs = sb("d_Gs", [P, NC, DH])
        gB = full("d_gB")
        cbeta, ceG, ceK, cgl, cG = (sb(f"d_c{n}", [P, DH]) for n in ("beta", "eG", "eK", "gl", "G"))
        raw = [sb(f"d_raw{n}", [P, DH, P]) for n in range(3)]
        gate = sb("d_gate", [P, DH, P])
        sq = sb("d_sq", [P, 2, 2, HH, P])
        ss, rn = sb("d_ss", [P, 2 * DH]), sb("d_rn", [P, 2 * DH])
        tq, tqd, tk, tkb, kd, kg, vb = (full(f"d_{n}") for n in ("tq", "tqd", "tk", "tkb", "kd", "kg", "vb"))
        qT, kT, kbT, qdT = (full(f"d_{n}T") for n in ("q", "k", "kb", "qd"))
        dec, MT, qk = full("d_dec"), full("d_MT"), full("d_qk")
        LT = [full(f"d_LT{u}") for u in range(2)]
        Tm, TT_, X = full("d_Tm"), full("d_TT"), full("d_X")
        nwT, vn, S, S2 = full("d_nwT"), full("d_vn"), full("d_S"), full("d_S2")
        sqo, so, ro, on = full("d_sqo"), sb("d_so", [P, DH]), sb("d_ro", [P, DH]), full("d_on")
        ybT = sb("d_ybT", [P, DH, T])
        ps = {n: ctx.enter_context(nc.psum_tensor(f"d_ps{n}", [P, 2, HALF], F32)) for n in "ABCD"}

        def pw(n, h=None):
            v = ps[n][:, :, 0:W].rearrange("p a (b t) -> p a b t", t=P)
            return v if h is None else v[:, h]

        def cast(v, h=None):
            v = v.rearrange("p (a b) -> p a b", a=2)
            if h is None:
                return v.unsqueeze(3).broadcast_to([P, 2, HH, P])
            return v[:, h].unsqueeze(2).broadcast_to([P, HH, P])

        def heads(v, h):
            return v.unsqueeze(1).broadcast_to([P, HH, P])

        def at(v, h):
            return v[:, h // HH, h % HH, :]

        block = ctx.enter_context(nc.Block())

        @block.sync
        def _(sp):
            srcs = [(ident, g.ident), (upto, g.upto), (later, g.notlater), (level, g.level), (ba, g.ba),
                    (neg_a, g.a_log.partition_broadcast(P)), (dtb, g.dt_bias.partition_broadcast(P)),
                    (gain, g.norm_gain)]
            for d, s in srcs:
                sp.dma_start(d[:], s).then_inc(sem("ld_c"), 16)
            with sp.Fori(0, NC) as i:
                sp.wait_ge(sem("tr1"), START + 3 * i)
                for n in range(3):
                    src = g.hT[N_ATT + n * DH:N_ATT + (n + 1) * DH, :, bass.ds(i * C, C)]
                    sp.dma_start(raw[n][:], src.rearrange("n p t -> p n t")).then_inc(sem("ld_qkv"), 16)
                sp.wait_ge(sem("y_out"), START + 2 * i)
                src = g.hT[N_ATT + N_DN:N_ATT + N_DN + N_GB, :, bass.ds(i * C, C)]
                sp.dma_start(gate[:], src.rearrange("n p t -> p n t")).then_inc(sem("ld_gate"), 16)
            sp.wait_ge(sem("y_out"), START + 2 * NC)
            sp.dma_start(g.y[AT:AT + DH].rearrange("n p t -> p n t"), ybT[:]).then_inc(sem("stored"), 16)
            sp.wait_ge(sem("stored"), START + 16)

        @block.gpsimd
        def _(pool):
            nc.gpsimd.memset(ones[:], 1.0).then_inc(sem("ones"), 1)
            nc.gpsimd.memset(half_power[:], -0.5).then_inc(sem("ones"), 1)
            nc.gpsimd.memset(S[:], 0.0).then_inc(sem("ones"), 1)
            pool.wait_ge(sem("ones"), START + 3)
            with pool.Fori(0, NC) as i:
                pool.wait_ge(sem("sumsq"), START + i + 1)
                pool.wait_ge(sem("tk"), START + 2 * i)
                nc.gpsimd.tensor_tensor(rn[:], ss[:], half_power[:], ALU.pow).then_inc(sem("rnorm"), 1)
                pool.wait_ge(sem("tk"), START + 2 * i + 2)
                pool.wait_ge(sem("chunk_factors"), START + i + 1)
                pool.wait_ge(sem("w_mm"), START + 2 * i)
                nc.gpsimd.tensor_tensor(tkb[:], tk[:], cast(cbeta[:]), ALU.mult).then_inc(sem("tkb"), 1)
                pool.wait_ge(sem("tq"), START + i + 1)
                nc.gpsimd.tensor_tensor(tqd[:], tq[:], cast(ceG[:]), ALU.mult).then_inc(sem("tqd"), 1)
                pool.wait_ge(sem("state_mm"), START + i)
                nc.gpsimd.tensor_tensor(kd[:], tk[:], cast(ceK[:]), ALU.mult).then_inc(sem("kd"), 1)
                pool.wait_ge(sem("tkb"), START + i + 1)
                nc.gpsimd.tensor_tensor(kg[:], tkb[:], cast(ceG[:]), ALU.mult).then_inc(sem("kg"), 1)
                for v in range(1, LEVELS):
                    u = v % 2
                    for h in range(2):
                        pool.wait_ge(sem("M"), START + 2 * i + 1 + h)
                        pool.wait_ge(sem("X_mm"), START + 12 * i + max(2 * (v - 3) + h + 1, 0))
                        nc.gpsimd.tensor_tensor(LT[u][:, h], MT[:, h], heads(level[:, v, :], h), ALU.mult).then_inc(sem("LT"), 1)
                pool.wait_ge(sem("state"), START + i)
                nc.gpsimd.tensor_tensor(S2[:], S[:], cast(cgl[:]), ALU.mult).then_inc(sem("decayed"), 1)
                pool.wait_ge(sem("out_sumsq"), START + i + 1)
                nc.gpsimd.tensor_tensor(ro[:], so[:], half_power[:, 0:DH], ALU.pow).then_inc(sem("out_rnorm"), 1)

        @block.scalar
        def _(act):
            act.wait_ge(sem("ld_c"), START + 16 * 8)
            nc.scalar.activation(beta[:], ba[:, :, 0:DH], ACT.Sigmoid).then_inc(sem("beta"), 1)
            nc.scalar.activation(neg_a[:], neg_a[:], ACT.Exp).then_inc(sem("exp"), 1)
            act.wait_ge(sem("z_abs"), START + 1)
            nc.scalar.activation(ez[:], ez[:], ACT.Exp, scale=-1.0).then_inc(sem("ez"), 1)
            act.wait_ge(sem("ez"), START + 1)
            nc.scalar.activation(ez[:], ez[:], ACT.Ln, bias=1.0).then_inc(sem("ez"), 1)
            act.wait_ge(sem("G_ready"), START + 1)
            nc.scalar.activation(eG[:], Gs[:], ACT.Exp).then_inc(sem("exps"), 1)
            nc.scalar.activation(gl[:], gl[:], ACT.Exp).then_inc(sem("exps"), 1)
            nc.scalar.activation(eK[:], eK[:], ACT.Exp).then_inc(sem("exps"), 1)
            with act.Fori(0, NC) as i:
                for n, name in ((0, "A"), (1, "B")):
                    act.wait_ge(sem("tr1"), START + 3 * i + n + 1)
                    act.wait_ge(sem("sumsq"), START + i)
                    nc.scalar.activation(sq[:, n], pw(name), ACT.Square).then_inc(sem("squares"), 1)
                act.wait_ge(sem("tr2"), START + 4 * i + 1)
                nc.scalar.copy(qT[:], pw("A")).then_inc(sem("qT"), 1)
                act.wait_ge(sem("tr2"), START + 4 * i + 3)
                nc.scalar.copy(kbT[:], pw("C")).then_inc(sem("kbT"), 1)
                act.wait_ge(sem("decay"), START + i + 1)
                nc.scalar.activation(dec[:], dec[:], ACT.Exp).then_inc(sem("decay_exp"), 1)
                for h in range(2):
                    act.wait_ge(sem("T_tr"), START + 2 * i + h + 1)
                    nc.scalar.copy(Tm[:, h], pw("A", h)).then_inc(sem("T_first"), 1)
                for v in range(1, LEVELS):
                    for h in range(2):
                        act.wait_ge(sem("X_mm"), START + 12 * i + 2 * (v - 1) + h + 1)
                        nc.scalar.copy(X[:, h], pw("B", h)).then_inc(sem("X"), 1)
                for h in range(2):
                    act.wait_ge(sem("w_mm"), START + 2 * i + h + 1)
                    nc.scalar.mul(nwT[:, h], pw("A", h), -1.0).then_inc(sem("w"), 1)
                for h in range(2):
                    act.wait_ge(sem("vn_mm"), START + 2 * i + h + 1)
                    nc.scalar.copy(vn[:, h], pw("B", h)).then_inc(sem("vn"), 1)
                act.wait_ge(sem("o_mm"), START + i + 1)
                nc.scalar.activation(sqo[:], pw("C"), ACT.Square).then_inc(sem("out_squares"), 1)

        @block.vector
        def _(dve):
            dve.wait_ge(sem("ld_c"), START + 16 * 8)
            nc.vector.tensor_tensor(z[:], ba[:, :, DH:], dtb[:].unsqueeze(1).broadcast_to([P, NC, DH]), ALU.add).then_inc(sem("z"), 1)
            dve.wait_ge(sem("z"), START + 1)
            nc.vector.tensor_scalar(ez[:], z[:], -1.0, None, ALU.mult).then_inc(sem("z"), 1)
            dve.wait_ge(sem("z"), START + 2)
            nc.vector.tensor_tensor(ez[:], ez[:], z[:], ALU.max).then_inc(sem("z_abs"), 1)
            nc.vector.tensor_scalar(z[:], z[:], 0.0, None, ALU.max).then_inc(sem("z"), 1)
            dve.wait_ge(sem("z"), START + 3)
            dve.wait_ge(sem("ez"), START + 2)
            nc.vector.tensor_tensor(z[:], z[:], ez[:], ALU.add).then_inc(sem("z"), 1)
            dve.wait_ge(sem("exp"), START + 1)
            dve.wait_ge(sem("z"), START + 4)
            nc.vector.tensor_scalar(z[:], z[:], -1.0, None, ALU.mult).then_inc(sem("z"), 1)
            dve.wait_ge(sem("z"), START + 5)
            nc.vector.tensor_tensor(gg[:], z[:], neg_a[:].unsqueeze(1).broadcast_to([P, NC, DH]), ALU.mult).then_inc(sem("g"), 1)
            dve.wait_ge(sem("G_mm"), START + 2)
            G2 = NC * DH
            nc.vector.tensor_copy(Gs[:].rearrange("p a b -> p (a b)"), ps["A"][:, 0, 0:G2])
            nc.vector.tensor_copy(gl[:].rearrange("p a b -> p (a b)"), ps["B"][:, 0, 0:G2]).then_inc(sem("g_copied"), 1)
            dve.wait_ge(sem("g_copied"), START + 1)
            nc.vector.tensor_tensor(eK[:], gl[:], Gs[:], ALU.subtract).then_inc(sem("G_ready"), 1)
            dve.wait_ge(sem("exps"), START + 3)
            dve.wait_ge(sem("beta"), START + 1)
            with dve.Fori(0, NC) as i:
                dve.wait_ge(sem("decayed"), START + i)
                dve.wait_ge(sem("kg"), START + i)
                dve.wait_ge(sem("rowG"), START + i)
                dve.wait_ge(sem("g"), START + 1)
                for d, s in ((cbeta, beta), (ceG, eG), (ceK, eK), (cgl, gl), (cG, Gs)):
                    nc.vector.tensor_copy(d[:], s[:, bass.ds(i, 1), :].rearrange("p a b -> p (a b)"))
                nc.vector.tensor_copy(gB[:].rearrange("p a b t -> p (a b) t"),
                                      gg[:, bass.ds(i, 1), :].rearrange("p a b -> p (a b)").unsqueeze(2).broadcast_to([P, DH, P])).then_inc(sem("chunk_factors"), 1)
                dve.wait_ge(sem("tr1"), START + 3 * i + 3)
                dve.wait_ge(sem("chunk_factors"), START + i + 1)
                dve.wait_ge(sem("vn_mm"), START + 2 * i)
                nc.vector.tensor_tensor(vb[:], pw("C"), cast(cbeta[:]), ALU.mult).then_inc(sem("vb"), 1)
                dve.wait_ge(sem("squares"), START + 2 * i + 2)
                dve.wait_ge(sem("rnorm"), START + i)
                nc.vector.tensor_reduce(ss[:], sq[:].rearrange("p n a b t -> p (n a b) t"), AX.X, ALU.add).then_inc(sem("ss_raw"), 1)
                dve.wait_ge(sem("ss_raw"), START + 3 * i + 1)
                nc.vector.tensor_scalar(ss[:, 0:DH], ss[:, 0:DH], 1e-6, float(DD), ALU.add, ALU.mult).then_inc(sem("ss_raw"), 1)
                nc.vector.tensor_scalar(ss[:, DH:], ss[:, DH:], 1e-6, None, ALU.add).then_inc(sem("ss_raw"), 1)
                dve.wait_ge(sem("ss_raw"), START + 3 * i + 3)
                dve.sem_inc(sem("sumsq"), 1)
                dve.wait_ge(sem("rnorm"), START + i + 1)
                dve.wait_ge(sem("tr2"), START + 4 * i)
                dve.wait_ge(sem("kd"), START + i)
                for h in range(2):
                    nc.vector.tensor_tensor(tk[:, h], pw("B", h), cast(rn[:, DH:], h), ALU.mult).then_inc(sem("tk"), 1)
                nc.vector.tensor_tensor(tq[:], pw("A"), cast(rn[:, 0:DH]), ALU.mult).then_inc(sem("tq"), 1)
                dve.wait_ge(sem("tr2"), START + 4 * i + 2)
                nc.vector.tensor_copy(kT[:], pw("B")).then_inc(sem("kT"), 1)
                dve.wait_ge(sem("tr2"), START + 4 * i + 4)
                nc.vector.tensor_copy(qdT[:], pw("D")).then_inc(sem("qdT"), 1)
                dve.wait_ge(sem("rowG"), START + i + 1)
                nc.vector.tensor_tensor(dec[:], pw("C"), cast(cG[:]), ALU.subtract).then_inc(sem("decay_step"), 1)
                dve.wait_ge(sem("decay_step"), START + 2 * i + 1)
                d6 = dec[:].rearrange("p a b t -> p (a b) t")
                nc.vector.tensor_tensor(d6, d6, later[:].unsqueeze(1).broadcast_to([P, DH, P]), ALU.add).then_inc(sem("decay_step"), 1)
                dve.wait_ge(sem("decay_step"), START + 2 * i + 2)
                dve.sem_inc(sem("decay"), 1)
                dve.wait_ge(sem("decay_exp"), START + i + 1)
                dve.wait_ge(sem("kk_mm"), START + 2 * i + 2)
                for h in range(2):
                    nc.vector.tensor_tensor(MT[:, h], pw("A", h), dec[:, h], ALU.mult).then_inc(sem("M"), 1)
                nc.vector.tensor_tensor(qk[:], pw("D"), dec[:], ALU.mult).then_inc(sem("qk"), 1)
                for h in range(2):
                    dve.wait_ge(sem("M"), START + 2 * i + h + 1)
                    nc.vector.tensor_tensor(TT_[:, h], MT[:, h], heads(level[:, 0, :], h), ALU.mult).then_inc(sem("T0"), 1)
                for h in range(2):
                    dve.wait_ge(sem("T0"), START + 4 * i + h + 1)
                    nc.vector.tensor_tensor(TT_[:, h], heads(ident[:], h), TT_[:, h], ALU.subtract).then_inc(sem("T0"), 1)
                for v in range(1, LEVELS):
                    for h in range(2):
                        dve.wait_ge(sem("TX_mm"), START + 12 * i + 2 * (v - 1) + h + 1)
                        if v < LEVELS - 1:
                            nc.vector.tensor_tensor(Tm[:, h], Tm[:, h], pw("C", h), ALU.subtract).then_inc(sem("T"), 1)
                        nc.vector.tensor_tensor(TT_[:, h], TT_[:, h], pw("D", h), ALU.subtract).then_inc(sem("TT"), 1)
                dve.wait_ge(sem("decayed"), START + i + 1)
                dve.wait_ge(sem("state_mm"), START + i + 1)
                nc.vector.tensor_tensor(S[:], S2[:], pw("D"), ALU.add).then_inc(sem("state"), 1)
                dve.wait_ge(sem("out_squares"), START + i + 1)
                dve.wait_ge(sem("out_rnorm"), START + i)
                nc.vector.tensor_reduce(so[:], sqo[:].rearrange("p a b t -> p (a b) t"), AX.X, ALU.add).then_inc(sem("so_raw"), 1)
                dve.wait_ge(sem("so_raw"), START + 2 * i + 1)
                nc.vector.tensor_scalar(so[:], so[:], 1.0 / DD, 1e-6, ALU.mult, ALU.add).then_inc(sem("so_raw"), 1)
                dve.wait_ge(sem("so_raw"), START + 2 * i + 2)
                dve.sem_inc(sem("out_sumsq"), 1)
                dve.wait_ge(sem("out_rnorm"), START + i + 1)
                nc.vector.tensor_tensor(on[:], pw("C"), cast(ro[:]), ALU.mult).then_inc(sem("on"), 1)
                dve.wait_ge(sem("ld_gate"), START + 16 * (i + 1))
                for h in range(2):
                    dve.wait_ge(sem("on_tr"), START + 2 * i + h + 1)
                    nc.vector.scalar_tensor_tensor(ybT[:, h * HH:(h + 1) * HH, bass.ds(i * C, C)], pw("A", h), gain[:, 0:1],
                                                   gate[:, h * HH:(h + 1) * HH, :], ALU.mult, ALU.mult).then_inc(sem("y_out"), 1)

        @block.tensor
        def _(pe):
            pe.wait_ge(sem("g"), START + 1)
            pe.wait_ge(sem("ones"), START + 3)
            gf = gg[:].rearrange("p a b -> p (a b)")
            nc.tensor.matmul(ps["A"][:, 0, 0:NC * DH], upto[:], gf, start=True, stop=True).then_inc(sem("G_mm"), 1)
            nc.tensor.matmul(ps["B"][:, 0, 0:NC * DH], ones[:], gf, start=True, stop=True).then_inc(sem("G_mm"), 1)
            pe.wait_ge(sem("g_copied"), START + 1)
            with pe.Fori(0, NC) as i:
                pe.wait_ge(sem("ld_qkv"), START + 48 * (i + 1))
                pe.wait_ge(sem("y_out"), START + 2 * i)
                for n, name in enumerate("ABC"):
                    for h in range(DH):
                        ins = nc.tensor.transpose(at(pw(name), h), raw[n][:, h, :], ident[:])
                    ins.then_inc(sem("tr1"), 1)

                def turn(name, src, ready, count=1):
                    pe.wait_ge(sem(ready), START + count * i + count)
                    for h in range(DH):
                        ins = nc.tensor.transpose(at(pw(name), h), at(src, h), ident[:])
                    ins.then_inc(sem("tr2"), 1)

                turn("A", tq, "tq")
                turn("B", tk, "tk", 2)
                pe.wait_ge(sem("vb"), START + i + 1)
                turn("C", tkb, "tkb")
                pe.wait_ge(sem("state"), START + i)
                turn("D", tqd, "tqd")
                pe.wait_ge(sem("kT"), START + i + 1)
                pe.wait_ge(sem("kbT"), START + i + 1)
                pe.wait_ge(sem("qT"), START + i + 1)
                for h in range(DH):
                    ins = nc.tensor.matmul(at(pw("A"), h), at(kT, h), at(kbT, h), start=True, stop=True)
                ins.then_inc(sem("kk_mm"), 1)
                for h in range(DH):
                    ins = nc.tensor.matmul(at(pw("C"), h), at(gB, h), upto[:], start=True, stop=True)
                ins.then_inc(sem("rowG"), 1)
                pe.wait_ge(sem("qdT"), START + i + 1)
                for h in range(DH):
                    ins = nc.tensor.matmul(at(pw("D"), h), at(kT, h), at(qT, h), start=True, stop=True)
                ins.then_inc(sem("kk_mm"), 1)
                for h in range(2):
                    pe.wait_ge(sem("T0"), START + 4 * i + 3 + h)
                    for a in range(HH):
                        ins = nc.tensor.transpose(pw("A", h)[:, a], TT_[:, h, a, :], ident[:])
                    ins.then_inc(sem("T_tr"), 1)
                pe.wait_ge(sem("qk"), START + i + 1)
                for v in range(1, LEVELS):
                    for h in range(2):
                        pe.wait_ge(sem("LT"), START + 12 * i + 2 * (v - 1) + h + 1)
                        if v == 1:
                            pe.wait_ge(sem("T_first"), START + 2 * i + h + 1)
                        else:
                            pe.wait_ge(sem("T"), START + 10 * i + 2 * (v - 2) + h + 1)
                            pe.wait_ge(sem("TT"), START + 12 * i + 2 * (v - 2) + h + 1)
                        for a in range(HH):
                            ins = nc.tensor.matmul(pw("B", h)[:, a], LT[v % 2][:, h, a, :], Tm[:, h, a, :], start=True, stop=True)
                        ins.then_inc(sem("X_mm"), 1)
                    for h in range(2):
                        pe.wait_ge(sem("X"), START + 12 * i + 2 * (v - 1) + h + 1)
                        for a in range(HH):
                            if v < LEVELS - 1:
                                nc.tensor.matmul(pw("C", h)[:, a], TT_[:, h, a, :], X[:, h, a, :], start=True, stop=True)
                            ins = nc.tensor.matmul(pw("D", h)[:, a], X[:, h, a, :], TT_[:, h, a, :], start=True, stop=True)
                        ins.then_inc(sem("TX_mm"), 1)
                for h in range(2):
                    pe.wait_ge(sem("TT"), START + 12 * i + 2 * (LEVELS - 2) + h + 1)
                    pe.wait_ge(sem("kg"), START + i + 1)
                    for a in range(HH):
                        ins = nc.tensor.matmul(pw("A", h)[:, a], kg[:, h, a, :], TT_[:, h, a, :], start=True, stop=True)
                    ins.then_inc(sem("w_mm"), 1)
                pe.wait_ge(sem("state"), START + i)
                for h in range(2):
                    pe.wait_ge(sem("w"), START + 2 * i + h + 1)
                    for a in range(HH):
                        nc.tensor.matmul(pw("B", h)[:, a], TT_[:, h, a, :], vb[:, h, a, :], start=True, stop=False)
                        ins = nc.tensor.matmul(pw("B", h)[:, a], nwT[:, h, a, :], S[:, h, a, :], start=False, stop=True)
                    ins.then_inc(sem("vn_mm"), 1)
                for h in range(2):
                    pe.wait_ge(sem("vn"), START + 2 * i + h + 1)
                    for a in range(HH):
                        nc.tensor.matmul(pw("C", h)[:, a], qdT[:, h, a, :], S[:, h, a, :], start=True, stop=False)
                        ins = nc.tensor.matmul(pw("C", h)[:, a], qk[:, h, a, :], vn[:, h, a, :], start=False, stop=True)
                ins.then_inc(sem("o_mm"), 1)
                pe.wait_ge(sem("kd"), START + i + 1)
                for h in range(DH):
                    ins = nc.tensor.matmul(at(pw("D"), h), at(kd, h), at(vn, h), start=True, stop=True)
                ins.then_inc(sem("state_mm"), 1)
                pe.wait_ge(sem("on"), START + i + 1)
                for h in range(2):
                    for a in range(HH):
                        ins = nc.tensor.transpose(pw("A", h)[:, a], on[:, h, a, :], ident[:])
                    ins.then_inc(sem("on_tr"), 1)


def float32r_products(wh, wl, xh, xl):
    return ((wh, xh), (wh, xl), (wl, xh))


def stage_merge(nc, g):
    NK = 2 * AT
    with ExitStack() as ctx:
        def sb(name, shape, dt=F32):
            return ctx.enter_context(nc.sbuf_tensor(name, shape, dt))

        sem = ctx.enter_context(stage_semaphores(nc, "m",
            "y_lo ld_y0 ld_y1 ld_w0 ld_w1 ld_g0 ld_g1 w_lo gated y_hi w_hi mm ps_read"))

        yraw = [sb(f"m_yraw{u}", [P, T]) for u in range(2)]
        yh, yl = sb("m_yh", [P, NK, T], F32R), sb("m_yl", [P, NK, T], F32R)
        wraw = [sb(f"m_wraw{u}", [P, NK, P]) for u in range(2)]
        wh = [sb(f"m_wh{u}", [P, NK, P], F32R) for u in range(2)]
        wl = [sb(f"m_wl{u}", [P, NK, P], F32R) for u in range(2)]
        gates = [sb(f"m_gates{u}", [P, 2, T]) for u in range(2)]
        ps = [[ctx.enter_context(nc.psum_tensor(f"m_ps{u}{b}", [P, T], F32)) for b in range(2)] for u in range(2)]
        block = ctx.enter_context(nc.Block())

        @block.sync
        def _(sp):
            for k in range(NK):
                if k >= 2:
                    sp.wait_ge(sem("y_lo"), START + k - 1)
                sp.dma_start(yraw[k % 2][:], g.y[k]).then_inc(sem(f"ld_y{k % 2}"), 16)
                if k < 2:
                    sp.dma_start(wraw[k][:], g.w_branch[k]).then_inc(sem(f"ld_w{k}"), 16)
                    for b in range(2):
                        sp.dma_start(gates[k][:, b, :], g.hT[N_IN - N_BR + b * KD + k]).then_inc(sem(f"ld_g{k}"), 16)
            with sp.Fori(0, KD // 2 - 1) as i:
                for u in range(2):
                    sp.wait_ge(sem("w_lo"), START + 2 * i + (u + 1))
                    sp.dma_start(wraw[u][:], g.w_branch[bass.ds(2 * i + (2 + u), 1)].rearrange("o p k c -> (o p) k c")).then_inc(sem(f"ld_w{u}"), 16)
                    sp.wait_ge(sem("gated"), START + 4 * i + (2 * u + 2))
                    for b in range(2):
                        sp.dma_start(gates[u][:, b, :], g.hT[bass.ds(2 * i + (N_IN - N_BR + b * KD + 2 + u), 1)].rearrange("o p t -> (o p) t")).then_inc(sem(f"ld_g{u}"), 16)

        @block.scalar
        def _(act):
            for k in range(NK):
                act.wait_ge(sem(f"ld_y{k % 2}"), START + 16 * (k // 2 + 1))
                nc.scalar.copy(yh[:, k, :], yraw[k % 2][:]).then_inc(sem("y_hi"), 1)
            for u in range(2):
                act.wait_ge(sem(f"ld_w{u}"), START + 16)
                nc.scalar.copy(wh[u][:], wraw[u][:]).then_inc(sem("w_hi"), 1)
            with act.Fori(0, KD // 2 - 1) as i:
                for u in range(2):
                    act.wait_ge(sem("mm"), START + 2 * i + (u + 1))
                    act.wait_ge(sem(f"ld_w{u}"), START + 16 * i + 32)
                    nc.scalar.copy(wh[u][:], wraw[u][:]).then_inc(sem("w_hi"), 1)

        @block.vector
        def _(dve):
            for k in range(NK):
                dve.wait_ge(sem("y_hi"), START + k + 1)
                nc.vector.tensor_tensor(yl[:, k, :], yraw[k % 2][:], yh[:, k, :].bitcast(F32), ALU.subtract).then_inc(sem("y_lo"), 1)
            for u in range(2):
                dve.wait_ge(sem("w_hi"), START + u + 1)
                nc.vector.tensor_tensor(wl[u][:], wraw[u][:], wh[u][:].bitcast(F32), ALU.subtract).then_inc(sem("w_lo"), 1)

            def body(i, last=False):
                for u in range(2):
                    dve.wait_ge(sem("mm"), START + 2 * i + (u + 1))
                    if not last:
                        dve.wait_ge(sem("w_hi"), START + 2 * i + (u + 3))
                        nc.vector.tensor_tensor(wl[u][:], wraw[u][:], wh[u][:].bitcast(F32), ALU.subtract).then_inc(sem("w_lo"), 1)
                    dve.wait_ge(sem(f"ld_g{u}"), START + 32 * i + 32)
                    for b in range(2):
                        nc.vector.tensor_tensor(gates[u][:, b, :], gates[u][:, b, :], ps[u][b][:], ALU.mult).then_inc(sem("ps_read"), 1)
                    dve.wait_ge(sem("ps_read"), START + 4 * i + (2 * u + 2))
                    nc.vector.tensor_tensor(g.merged[:, bass.ds(2 * i + u, 1), :].rearrange("p o t -> p (o t)"),
                                            gates[u][:, 0, :], gates[u][:, 1, :], ALU.add).then_inc(sem("gated"), 2)

            with dve.Fori(0, KD // 2 - 1) as i:
                body(i)
            body(KD // 2 - 1, last=True)

        @block.tensor
        def _(pe):
            pe.wait_ge(sem("y_lo"), START + NK)
            with pe.Fori(0, KD // 2) as i:
                for u in range(2):
                    pe.wait_ge(sem("w_lo"), START + 2 * i + (u + 1))
                    pe.wait_ge(sem("ps_read"), START + 4 * i)
                    for b in range(2):
                        for h in range(2):
                            for k in range(AT):
                                for n, (a, x) in enumerate(float32r_products(wh, wl, yh, yl)):
                                    ins = nc.tensor.matmul(ps[u][b][:, h * HALF:(h + 1) * HALF], a[u][:, b * AT + k, :],
                                                           x[:, b * AT + k, h * HALF:(h + 1) * HALF],
                                                           start=(k == 0 and n == 0), stop=(k == AT - 1 and n == 2))
                    ins.then_inc(sem("mm"), 1)


def stage_out_norm(nc, g):
    with ExitStack() as ctx:
        def sb(name, shape, dt=F32):
            return ctx.enter_context(nc.sbuf_tensor(name, shape, dt))

        sem = ctx.enter_context(stage_semaphores(nc, "o",
            "ld_c w_lo ld_w0 ld_w1 z ld_x0 ld_x1 x1 st_x10 st_x11 xT sp_passed st_xT0 st_xT1 power var normed "
            "rstd scaled w_hi mm m_hi turned m_lo stats passed aggr"))

        wraw = [sb(f"o_wraw{u}", [P, D]) for u in range(2)]
        wh, wl = sb("o_wh", [P, KD, D], F32R), sb("o_wl", [P, KD, D], F32R)
        mh = [sb(f"o_mh{u}", [P, KD, P], F32R) for u in range(2)]
        ml = [sb(f"o_ml{u}", [P, KD, P], F32R) for u in range(2)]
        x = [sb(f"o_x{u}", [P, D]) for u in range(2)]
        z = [sb(f"o_z{u}", [P, D]) for u in range(2)]
        xT = [sb(f"o_xT{u}", [P, KD, P]) for u in range(2)]
        gain, bias, ident = sb("o_gain", [P, D]), sb("o_bias", [P, D]), sb("o_ident", [P, P])
        stats, mv, rstd, power = sb("o_stats", [P, 2, 6]), sb("o_mv", [P, 2]), sb("o_rstd", [P, 1]), sb("o_power", [P, 1])
        ps = [ctx.enter_context(nc.psum_tensor(f"o_ps{u}", [P, D], F32)) for u in range(2)]
        psT = ctx.enter_context(nc.psum_tensor("o_psT", [P, D], F32))
        block = ctx.enter_context(nc.Block())

        @block.sync
        def _(sp):
            for d, s in ((gain, g.ln1_gain.partition_broadcast(P)), (bias, g.ln1_bias.partition_broadcast(P)), (ident, g.ident)):
                sp.dma_start(d[:], s).then_inc(sem("ld_c"), 16)
            for k in range(KD):
                if k >= 2:
                    sp.wait_ge(sem("w_lo"), START + k - 1)
                sp.dma_start(wraw[k % 2][:], g.w_out[k * P:(k + 1) * P, :]).then_inc(sem(f"ld_w{k % 2}"), 16)
            with sp.Fori(0, TT // 2) as i:
                for u in range(2):
                    sp.wait_ge(sem("z"), START + 2 * i)
                    sp.dma_start(x[u][:], g.x[bass.ds(2 * i * P + u * P, P), :]).then_inc(sem(f"ld_x{u}"), 16)
                for u in range(2):
                    sp.wait_ge(sem("x1"), START + 2 * i + (u + 1))
                    sp.dma_start(g.x1[bass.ds(2 * i * P + u * P, P), :], z[u][:]).then_inc(sem(f"st_x1{u}"), 16)
                    wait_alone(sp, sem("xT"), START + 2 * i + (u + 1), sem("sp_passed"))
                    sp.dma_start(g.x1T[:, :, bass.ds(2 * i * P + u * P, P)].rearrange("k p t -> p k t"), xT[u][:]).then_inc(sem(f"st_xT{u}"), 16)
            for u in range(2):
                sp.wait_ge(sem(f"st_x1{u}"), START + 16 * (TT // 2))
                sp.wait_ge(sem(f"st_xT{u}"), START + 16 * (TT // 2))

        @block.gpsimd
        def _(pool):
            nc.gpsimd.memset(power[:], -0.5).then_inc(sem("power"), 1)
            pool.wait_ge(sem("ld_c"), START + 48)
            pool.wait_ge(sem("power"), START + 1)
            with pool.Fori(0, TT // 2) as i:
                for u in range(2):
                    pool.wait_ge(sem("var"), START + 2 * i + (u + 1))
                    pool.wait_ge(sem("normed"), START + 2 * i + u)
                    nc.gpsimd.tensor_tensor(rstd[:], mv[:, 1:2], power[:], ALU.pow).then_inc(sem("rstd"), 1)
                    pool.wait_ge(sem("normed"), START + 2 * i + (u + 1))
                    nc.gpsimd.tensor_tensor(z[u][:], z[u][:], gain[:], ALU.mult).then_inc(sem("scaled"), 1)
                    pool.wait_ge(sem("scaled"), START + 2 * i + (u + 1))
                    nc.gpsimd.tensor_tensor(z[u][:], z[u][:], bias[:], ALU.add).then_inc(sem("x1"), 1)

        @block.scalar
        def _(act):
            for k in range(KD):
                act.wait_ge(sem(f"ld_w{k % 2}"), START + 16 * (k // 2 + 1))
                nc.scalar.copy(wh[:, k, :], wraw[k % 2][:]).then_inc(sem("w_hi"), 1)
            with act.Fori(0, TT // 2) as i:
                for u in range(2):
                    act.wait_ge(sem("mm"), START + 2 * i)
                    nc.scalar.copy(mh[u][:], g.merged[:, :, bass.ds(2 * i * P + u * P, P)]).then_inc(sem("m_hi"), 1)
                for u in range(2):
                    act.wait_ge(sem(f"st_xT{u}"), START + 16 * i)
                    act.wait_ge(sem("turned"), START + 2 * i + (u + 1))
                    nc.scalar.copy(xT[u][:], psT[:].rearrange("p (k t) -> p k t", t=P)).then_inc(sem("xT"), 1)

        @block.vector
        def _(dve):
            for k in range(KD):
                dve.wait_ge(sem("w_hi"), START + k + 1)
                nc.vector.tensor_tensor(wl[:, k, :], wraw[k % 2][:], wh[:, k, :].bitcast(F32), ALU.subtract).then_inc(sem("w_lo"), 1)
            with dve.Fori(0, TT // 2) as i:
                for u in range(2):
                    dve.wait_ge(sem("m_hi"), START + 2 * i + (u + 1))
                    nc.vector.tensor_tensor(ml[u][:], g.merged[:, :, bass.ds(2 * i * P + u * P, P)], mh[u][:].bitcast(F32), ALU.subtract).then_inc(sem("m_lo"), 1)
                for u in range(2):
                    dve.wait_ge(sem(f"ld_x{u}"), START + 16 * i + 16)
                    dve.wait_ge(sem(f"st_x1{u}"), START + 16 * i)
                    dve.wait_ge(sem("turned"), START + 2 * i)
                    dve.wait_ge(sem("mm"), START + 2 * i + (u + 1))
                    nc.vector.scalar_tensor_tensor(z[u][:], x[u][:], ALPHA, ps[u][:], ALU.mult, ALU.add).then_inc(sem("z"), 1)
                    dve.wait_ge(sem("z"), START + 2 * i + (u + 1))
                    dve.wait_ge(sem("normed"), START + 2 * i + u)
                    for h in range(2):
                        ins = nc.vector.bn_stats(stats[:, h, :], z[u][:, h * HALF:(h + 1) * HALF])
                    ins.then_inc(sem("stats"), 1)
                    wait_alone(dve, sem("stats"), START + 2 * i + (u + 1), sem("passed"))
                    nc.vector.bn_aggr(mv[:], stats[:]).then_inc(sem("aggr"), 1)
                    dve.wait_ge(sem("aggr"), START + 2 * i + (u + 1))
                    nc.vector.tensor_scalar(mv[:, 1:2], mv[:, 1:2], 1e-5, None, ALU.add).then_inc(sem("var"), 1)
                    dve.wait_ge(sem("rstd"), START + 2 * i + (u + 1))
                    nc.vector.tensor_scalar(z[u][:], z[u][:], mv[:, 0:1], rstd[:, 0:1], ALU.subtract, ALU.mult).then_inc(sem("normed"), 1)

        @block.tensor
        def _(pe):
            pe.wait_ge(sem("w_lo"), START + KD)
            pe.wait_ge(sem("ld_c"), START + 48)
            with pe.Fori(0, TT // 2) as i:
                for u in range(2):
                    pe.wait_ge(sem("m_lo"), START + 2 * i + (u + 1))
                    pe.wait_ge(sem("z"), START + 2 * i)
                    for h in range(2):
                        for k in range(KD):
                            for n, (a, b) in enumerate(float32r_products(mh, ml, wh, wl)):
                                ins = nc.tensor.matmul(ps[u][:, h * HALF:(h + 1) * HALF], a[u][:, k, :], b[:, k, h * HALF:(h + 1) * HALF],
                                                       start=(k == 0 and n == 0), stop=(k == KD - 1 and n == 2))
                    ins.then_inc(sem("mm"), 1)
                for u in range(2):
                    pe.wait_ge(sem("x1"), START + 2 * i + (u + 1))
                    pe.wait_ge(sem("xT"), START + 2 * i + u)
                    for k in range(KD):
                        ins = nc.tensor.transpose(psT[:, k * P:(k + 1) * P], z[u][:, k * P:(k + 1) * P], ident[:])
                    ins.then_inc(sem("turned"), 1)


def stage_scores(nc, g):
    N = 2 * PH
    with ExitStack() as ctx:
        def sb(name, shape, dt=F32):
            return ctx.enter_context(nc.sbuf_tensor(name, shape, dt))

        sem = ctx.enter_context(stage_semaphores(nc, "s",
            "x_lo ld_x0 ld_x1 ld_w0 ld_w1 ld_k s_out st_s0 st_s1 w_lo x_hi w_hi mm s_mm q"))

        xraw = [sb(f"s_xraw{u}", [P, T]) for u in range(2)]
        xh, xl = g.x1h, g.x1l
        wraw = [sb(f"s_wraw{u}", [P, KD, P]) for u in range(2)]
        wh = [sb(f"s_wh{u}", [P, KD, P], F32R) for u in range(2)]
        wl = [sb(f"s_wl{u}", [P, KD, P], F32R) for u in range(2)]
        keys = sb("s_keys", [P, N, PK])
        q = [sb(f"s_q{u}", [P, T]) for u in range(2)]
        sout = [sb(f"s_out{u}", [P, TT, PK]) for u in range(2)]
        psq = [ctx.enter_context(nc.psum_tensor(f"s_psq{u}", [P, T], F32)) for u in range(2)]
        pss = [ctx.enter_context(nc.psum_tensor(f"s_pss{u}", [P, T], F32)) for u in range(2)]
        block = ctx.enter_context(nc.Block())

        @block.sync
        def _(sp):
            for k in range(KD):
                if k >= 2:
                    sp.wait_ge(sem("x_lo"), START + k - 1)
                sp.dma_start(xraw[k % 2][:], g.x1T[k]).then_inc(sem(f"ld_x{k % 2}"), 16)
                if k < 2:
                    sp.dma_start(wraw[k][:], g.w_query[k]).then_inc(sem(f"ld_w{k}"), 16)
            sp.dma_start(keys[:], g.keys.rearrange("n c k -> c n k")).then_inc(sem("ld_k"), 16)

            def store(i, u):
                sp.wait_ge(sem("s_out"), START + 2 * i + (u + 1))
                sp.dma_start(g.s[:, :, bass.ds(2 * i + u, 1), :].rearrange("t p o k -> p t (o k)"), sout[u][:]).then_inc(sem(f"st_s{u}"), 16)

            with sp.Fori(0, N // 2 - 1) as i:
                for u in range(2):
                    sp.wait_ge(sem("w_lo"), START + 2 * i + (u + 1))
                    sp.dma_start(wraw[u][:], g.w_query[bass.ds(2 * i + (2 + u), 1)].rearrange("o p k c -> (o p) k c")).then_inc(sem(f"ld_w{u}"), 16)
                for u in range(2):
                    store(i, u)
            for u in range(2):
                store(N // 2 - 1, u)
            for u in range(2):
                sp.wait_ge(sem(f"st_s{u}"), START + 16 * (N // 2))

        @block.scalar
        def _(act):
            for k in range(KD):
                act.wait_ge(sem(f"ld_x{k % 2}"), START + 16 * (k // 2 + 1))
                nc.scalar.copy(xh[:, k, :], xraw[k % 2][:]).then_inc(sem("x_hi"), 1)

            def split(u, n):
                act.wait_ge(sem(f"ld_w{u}"), START + n)
                nc.scalar.copy(wh[u][:], wraw[u][:]).then_inc(sem("w_hi"), 1)

            split(0, 16)
            split(1, 16)

            def body(i, last=False):
                for u in range(2):
                    act.wait_ge(sem("mm"), START + 2 * i + (u + 1))
                    act.wait_ge(sem("s_mm"), START + 2 * i)
                    nc.scalar.copy(q[u][:], psq[u][:]).then_inc(sem("q"), 1)
                    if not last:
                        split(u, 16 * i + 32)

            with act.Fori(0, N // 2 - 1) as i:
                body(i)
            body(N // 2 - 1, last=True)

        @block.vector
        def _(dve):
            for k in range(KD):
                dve.wait_ge(sem("x_hi"), START + k + 1)
                nc.vector.tensor_tensor(xl[:, k, :], xraw[k % 2][:], xh[:, k, :].bitcast(F32), ALU.subtract).then_inc(sem("x_lo"), 1)

            def split(u, n):
                dve.wait_ge(sem("w_hi"), START + n)
                nc.vector.tensor_tensor(wl[u][:], wraw[u][:], wh[u][:].bitcast(F32), ALU.subtract).then_inc(sem("w_lo"), 1)

            split(0, 1)
            split(1, 2)

            def body(i, last=False):
                for u in range(2):
                    if not last:
                        split(u, 2 * i + (u + 3))
                for u in range(2):
                    dve.wait_ge(sem(f"st_s{u}"), START + 16 * i)
                    dve.wait_ge(sem("s_mm"), START + 2 * i + (u + 1))
                    nc.vector.tensor_copy(sout[u][:], pss[u][:].rearrange("p (t k) -> p t k", t=TT)).then_inc(sem("s_out"), 1)

            with dve.Fori(0, N // 2 - 1) as i:
                body(i)
            body(N // 2 - 1, last=True)

        @block.tensor
        def _(pe):
            pe.wait_ge(sem("x_lo"), START + KD)
            pe.wait_ge(sem("ld_k"), START + 16)

            def queries(i, u):
                pe.wait_ge(sem("w_lo"), START + 2 * i + (u + 1))
                pe.wait_ge(sem("q"), START + 2 * i)
                for h in range(2):
                    for k in range(KD):
                        for n, (a, b) in enumerate(float32r_products(wh, wl, xh, xl)):
                            ins = nc.tensor.matmul(psq[u][:, h * HALF:(h + 1) * HALF], a[u][:, k, :], b[:, k, h * HALF:(h + 1) * HALF],
                                                   start=(k == 0 and n == 0), stop=(k == KD - 1 and n == 2))
                ins.then_inc(sem("mm"), 1)

            def scores(i, u):
                pe.wait_ge(sem("q"), START + 2 * i + (u + 1))
                pe.wait_ge(sem("s_out"), START + 2 * i)
                for t in range(TT):
                    ins = nc.tensor.matmul(pss[u][:, t * PK:(t + 1) * PK], q[u][:, t * P:(t + 1) * P],
                                           keys[:, bass.ds(2 * i + u, 1), :].rearrange("p o k -> p (o k)"), start=True, stop=True)
                ins.then_inc(sem("s_mm"), 1)

            with pe.Fori(0, N // 2) as i:
                queries(i, 0)
                queries(i, 1)
                scores(i, 0)
                scores(i, 1)


GONE = -3e38

def stage_down_and_route(nc, g):
    SLOTS = PK // TT
    GT = 8
    NG = P // GT
    PIECES = 14
    WQ = 4

    def plan(groups, own, next):
        assert sum(groups) == NG and len(groups) == SLOTS
        def spans(counts):
            counts = counts + [0] * (SLOTS - len(counts))
            return [range(sum(counts[:n]), sum(counts[:n + 1])) for n in range(SLOTS)]
        return dict(groups=spans(groups), own=spans(own), next=spans(next), turn=groups.index(next_positive(groups)) - 1)

    def next_positive(counts):
        return [n for n in counts if n][0]

    FIRST = plan([0] * 6 + [2, 2, 1, 2, 1, 2, 1, 2, 2, 1], [4, 3, 3, 2, 1, 1], [0] * 5 + [2, 1, 1, 2, 1, 1, 2, 1, 1, 1, 1])
    INNER = plan([0] * 4 + [2, 1, 1] * 4, [], [1] * PIECES)
    LAST = plan([0] * 4 + [2] * 8 + [0] * 4, [], [])
    HB = 2 * NG
    with ExitStack() as ctx:
        def sb(name, shape, dt=F32):
            return ctx.enter_context(nc.sbuf_tensor(name, shape, dt))

        sem = ctx.enter_context(stage_semaphores(nc, "r",
            "ld_d0 ld_d1 ld_st ld_c st_W d_lo gelu st_a0 st_a1 st_used W d_hi shifted exp onehot turned rt "
            "d_mm w_mm gated eq picked pieces passed ranks zsum summed routed"))
        xh, xl = g.x1h, g.x1l
        draw = [sb(f"r_draw{u}", [P, KD, P]) for u in range(2)]
        dh = [sb(f"r_dh{u}", [P, KD, P], F32R) for u in range(2)]
        dl = [sb(f"r_dl{u}", [P, KD, P], F32R) for u in range(2)]
        act_out = [sb(f"r_act{u}", [P, T]) for u in range(2)]
        ident, iota = sb("r_ident", [P, P]), sb("r_iota", [P, P])
        st = sb("r_st", [P, 2 * PH, PK])
        val, idx = sb("r_val", [P, PH, 2, TOP]), sb("r_idx", [P, PH, 2, TOP], U32)
        keyf = sb("r_keyf", [P, PH, 2, TOP])
        cand = sb("r_cand", [P, PH, TOP, TOP])
        best, flat = sb("r_best", [P, PH, TOP]), sb("r_flat", [P, PH, TOP], U32)
        rank = sb("r_rank", [P, 2, PH, TOP], U32)
        rankf = sb("r_rankf", [P, 2, PH, TOP])
        zsum = sb("r_zsum", [P, PH])
        route = sb("r_route", [P, 3, PH, TOP])
        rt = sb("r_rt", [P, 3, P])
        oi = [sb(f"r_oi{u}", [P, GT, PK]) for u in range(2)]
        oj = [sb(f"r_oj{u}", [P, GT, PK]) for u in range(2)]
        W = sb("r_W", [P, PK, P])
        psd = [ctx.enter_context(nc.psum_tensor(f"r_psd{u}", [P, T], F32)) for u in range(2)]
        psw = [ctx.enter_context(nc.psum_tensor(f"r_psw{u}", [P, HALF], F32)) for u in range(2)]
        psT = ctx.enter_context(nc.psum_tensor("r_psT", [P, HALF], F32))
        block = ctx.enter_context(nc.Block())

        @block.sync
        def _(sp):
            def load_d(c, n):
                sp.dma_start(draw[n][:], g.down[bass.ds(c, 1)].rearrange("o p k e -> (o p) k e")).then_inc(sem(f"ld_d{n}"), 16)

            def load_st(t):
                sp.dma_start(st[:], g.s[bass.ds(t, 1)].rearrange("o p n k -> (o p) n k")).then_inc(sem("ld_st"), 16)

            for d, s in ((ident, g.ident), (iota, g.iota)):
                sp.dma_start(d[:], s).then_inc(sem("ld_c"), 16)
            load_st(0)
            load_d(0, 0)
            load_d(1, 1)

            def store_W(t, q):
                w = PK // WQ
                sp.dma_start(g.W[q * w:(q + 1) * w, :, bass.ds(t * P, P)].rearrange("j p t -> p j t"),
                             W[:, q * w:(q + 1) * w, :]).then_inc(sem("st_W"), 16)

            def slot(t, s, load=True):
                c, n = SLOTS * t + s, s % 2
                if load:
                    sp.wait_ge(sem("d_lo"), START + c + 1)
                    load_d(c + 2, n)
                sp.wait_ge(sem("gelu"), START + c + 1)
                sp.dma_start(g.act[bass.ds(c, 1)].rearrange("o p t -> (o p) t"), act_out[n][:]).then_inc(sem(f"st_a{n}"), 16)

            def tile(t, scores=True):
                for s in range(WQ, SLOTS + WQ):
                    slot(t, s)
                    if s == 12 and scores:
                        sp.wait_ge(sem("st_used"), START + t + 2)
                        load_st(t + 2)
                    if s >= SLOTS:
                        if s == SLOTS:
                            sp.wait_ge(sem("W"), START + HB * t + HB)
                        store_W(t, s - SLOTS)

            for s in range(WQ):
                slot(0, s)
            sp.wait_ge(sem("st_used"), START + 1)
            load_st(1)
            with sp.Fori(0, TT - 2) as t:
                tile(t)
            tile(TT - 2, scores=False)
            for s in range(WQ, SLOTS):
                slot(TT - 1, s, load=(s < SLOTS - 2))
                if s >= SLOTS - WQ:
                    sp.wait_ge(sem("W"), START + HB * TT)
                    store_W(TT - 1, s - (SLOTS - WQ))
            sp.wait_ge(sem("st_W"), START + 16 * WQ * TT)
            for n in range(2):
                sp.wait_ge(sem(f"st_a{n}"), START + 16 * PK // 2)

        @block.scalar
        def _(act):
            def split_d(c, n, count):
                act.wait_ge(sem(f"ld_d{n}"), START + count)
                nc.scalar.copy(dh[n][:], draw[n][:]).then_inc(sem("d_hi"), 1)

            def topk_exp(t):
                act.wait_ge(sem("shifted"), START + t + 1)
                nc.scalar.activation(route[:, 2], route[:, 2], ACT.Exp).then_inc(sem("exp"), 1)

            def topk_turn(t):
                act.wait_ge(sem("onehot"), START + NG * t)
                act.wait_ge(sem("turned"), START + t + 1)
                nc.scalar.copy(rt[:], psT[:, 0:3 * P].rearrange("p (c t) -> p c t", t=P)).then_inc(sem("rt"), 1)

            split_d(0, 0, 16)
            split_d(1, 1, 16)

            def tile(t, kind):
                for s in range(SLOTS):
                    c, n = SLOTS * t + s, s % 2
                    act.wait_ge(sem("d_mm"), START + c + 1)
                    if kind is not FIRST or s >= 2:
                        act.wait_ge(sem(f"st_a{n}"), START + 16 * (SLOTS // 2) * t + 16 * (s // 2))
                    nc.scalar.activation(act_out[n][:], psd[n][:], ACT.Gelu).then_inc(sem("gelu"), 1)
                    for m in kind["groups"][s]:
                        if m == 0 and kind is not FIRST:
                            act.wait_ge(sem("st_W"), START + 16 * WQ * t)
                        for b in range(2):
                            act.wait_ge(sem("w_mm"), START + HB * t + (2 * m + b + 1))
                            nc.scalar.copy(W[:, :, m * GT + 4 * b:m * GT + 4 * b + 4].rearrange("p j t -> p t j"),
                                           psw[b][:].rearrange("p (t j) -> p t j", j=PK)).then_inc(sem("W"), 1)
                    if not (kind is LAST and s >= SLOTS - 2):
                        split_d(c + 2, n, 16 * (SLOTS // 2) * t + 16 * (s // 2) + 32)
                    if EXP in kind["own"][s]:
                        topk_exp(t)
                    if EXP in kind["next"][s]:
                        topk_exp(t + 1)
                    if s == kind["turn"]:
                        topk_turn(t)

            EXP = 10
            tile(0, FIRST)
            with act.Fori(1, TT - 1) as t:
                tile(t, INNER)
            tile(TT - 1, LAST)

        @block.gpsimd
        def _(pool):
            def gate(t, m):
                u = m % 2
                pool.wait_ge(sem("onehot"), START + NG * t + (m + 1))
                nc.gpsimd.tensor_tensor(oi[u][:], oi[u][:], rt[:, 2, m * GT:(m + 1) * GT].unsqueeze(2).broadcast_to([P, GT, PK]),
                                        ALU.mult).then_inc(sem("gated"), 1)

            def pick(t, side):
                pool.wait_ge(sem("eq"), START + 2 * t + (side + 1))
                nc.gpsimd.tensor_tensor(cand[:], cand[:], keyf[:, :, side, :].unsqueeze(2).broadcast_to([P, PH, TOP, TOP]),
                                        ALU.mult).then_inc(sem("picked"), 1)

            def tile(t, kind):
                for s in range(SLOTS):
                    for m in kind["groups"][s]:
                        gate(t, m)
                    for side, piece in ((0, 11), (1, 12)):
                        if piece in kind["own"][s]:
                            pick(t, side)
                        if piece in kind["next"][s]:
                            pick(t + 1, side)

            tile(0, FIRST)
            with pool.Fori(1, TT - 1) as t:
                tile(t, INNER)
            tile(TT - 1, LAST)

        @block.vector
        def _(dve):
            def split_d(c, n):
                dve.wait_ge(sem("d_hi"), START + c + 1)
                nc.vector.tensor_tensor(dl[n][:], draw[n][:], dh[n][:].bitcast(F32), ALU.subtract).then_inc(sem("d_lo"), 1)

            def topk(t, piece):
                def before():
                    wait_alone(dve, sem("pieces"), START + PIECES * t + piece, sem("passed"))

                done = None
                pairs = [(h, p, 2 * h + p) for h in range(PH) for p in range(2)]
                if piece == 0:
                    wait_alone(dve, sem("ld_st"), START + 16 * t + 16, sem("passed"))
                    before()
                    for h, p, n in pairs:
                        done = nc.vector.max(val[:, h, p, 0:8], st[:, n, :])
                elif piece == 1:
                    before()
                    for h, p, n in pairs:
                        done = nc.vector.max_index(idx[:, h, p, 0:8], val[:, h, p, 0:8], st[:, n, :])
                elif piece == 2:
                    before()
                    for h, p, n in pairs:
                        done = nc.vector.match_replace(out=st[:, n, :], in_to_replace=val[:, h, p, 0:8], in_values=st[:, n, :], imm_value=GONE)
                elif piece == 3:
                    before()
                    for h, p, n in pairs:
                        done = nc.vector.max(val[:, h, p, 8:16], st[:, n, :])
                elif piece == 4:
                    before()
                    for h, p, n in pairs:
                        done = nc.vector.max_index(idx[:, h, p, 8:16], val[:, h, p, 8:16], st[:, n, :])
                elif piece == 5:
                    before()
                    dve.sem_inc(sem("st_used"), 1)
                    nc.vector.tensor_copy(keyf[:], idx[:])
                    done = nc.vector.tensor_tensor(cand[:], val[:, :, 0, :].unsqueeze(3).broadcast_to([P, PH, TOP, TOP]),
                                                   val[:, :, 1, :].unsqueeze(2).broadcast_to([P, PH, TOP, TOP]), ALU.add)
                elif piece == 6:
                    before()
                    for h in range(PH):
                        done = nc.vector.max(best[:, h, 0:8], sums[:, h])
                elif piece == 7:
                    before()
                    for h in range(PH):
                        done = nc.vector.max_index(flat[:, h, 0:8], best[:, h, 0:8], sums[:, h])
                elif piece == 8:
                    before()
                    for h in range(PH):
                        done = nc.vector.match_replace(out=sums[:, h], in_to_replace=best[:, h, 0:8], in_values=sums[:, h], imm_value=GONE)
                elif piece == 9:
                    before()
                    for h in range(PH):
                        done = nc.vector.max(best[:, h, 8:16], sums[:, h])
                elif piece == 10:
                    before()
                    for h in range(PH):
                        nc.vector.max_index(flat[:, h, 8:16], best[:, h, 8:16], sums[:, h])
                    dve.wait_ge(sem("turned"), START + t)
                    nc.vector.tensor_tensor(route[:, 2], best[:], best[:, :, 0:1].broadcast_to([P, PH, TOP]), ALU.subtract).then_inc(sem("shifted"), 1)
                    dve.wait_ge(sem("shifted"), START + t + 1)
                    dve.sem_inc(sem("pieces"), 1)
                elif piece == 11:
                    before()
                    nc.vector.tensor_scalar(rank[:, 0], flat[:], 4, None, ALU.logical_shift_right)
                    nc.vector.tensor_scalar(rank[:, 1], flat[:], 15, None, ALU.bitwise_and).then_inc(sem("ranks"), 1)
                    wait_alone(dve, sem("ranks"), START + 2 * t + 1, sem("passed"))
                    nc.vector.tensor_copy(rankf[:], rank[:]).then_inc(sem("ranks"), 1)
                    dve.wait_ge(sem("ranks"), START + 2 * t + 2)
                    nc.vector.tensor_tensor(cand[:], rankf[:, 0].unsqueeze(3).broadcast_to([P, PH, TOP, TOP]),
                                            ranks16, ALU.is_equal).then_inc(sem("eq"), 1)
                    dve.wait_ge(sem("exp"), START + t + 1)
                    nc.vector.tensor_reduce(zsum[:], route[:, 2], AX.X, ALU.add).then_inc(sem("zsum"), 1)
                    dve.wait_ge(sem("zsum"), START + 2 * t + 1)
                    nc.vector.reciprocal(zsum[:], zsum[:]).then_inc(sem("zsum"), 1)
                    dve.wait_ge(sem("zsum"), START + 2 * t + 2)
                    done = nc.vector.tensor_tensor(route[:, 2], route[:, 2], zsum[:].unsqueeze(2).broadcast_to([P, PH, TOP]), ALU.mult)
                elif piece == 12:
                    dve.wait_ge(sem("picked"), START + 2 * t + 1)
                    nc.vector.tensor_reduce(route[:, 0], cand[:], AX.X, ALU.add).then_inc(sem("summed"), 1)
                    dve.wait_ge(sem("summed"), START + 2 * t + 1)
                    nc.vector.tensor_tensor(cand[:], rankf[:, 1].unsqueeze(3).broadcast_to([P, PH, TOP, TOP]),
                                            ranks16, ALU.is_equal).then_inc(sem("eq"), 1)
                    dve.sem_inc(sem("pieces"), 1)
                elif piece == 13:
                    dve.wait_ge(sem("picked"), START + 2 * t + 2)
                    nc.vector.tensor_reduce(route[:, 1], cand[:], AX.X, ALU.add).then_inc(sem("summed"), 1)
                    dve.wait_ge(sem("summed"), START + 2 * t + 2)
                    before()
                    dve.sem_inc(sem("pieces"), 1)
                    dve.sem_inc(sem("routed"), 1)
                if done is not None:
                    done.then_inc(sem("pieces"), 1)

            sums = cand[:].rearrange("p h a b -> p h (a b)")
            ranks16 = iota[:, 0:TOP].unsqueeze(1).unsqueeze(1).broadcast_to([P, PH, TOP, TOP])

            split_d(0, 0)
            split_d(1, 1)
            dve.wait_ge(sem("ld_c"), START + 32)

            def tile(t, kind):
                for s in range(SLOTS):
                    c, n = SLOTS * t + s, s % 2
                    for m in kind["groups"][s]:
                        u = m % 2
                        if m == 0:
                            dve.wait_ge(sem("rt"), START + t + 1)
                        if m >= 2:
                            dve.wait_ge(sem("w_mm"), START + HB * t + 2 * (m - 1))
                        elif kind is not FIRST:
                            dve.wait_ge(sem("w_mm"), START + HB * t)
                        keys = iota[:].unsqueeze(1).broadcast_to([P, GT, PK])
                        nc.vector.tensor_tensor(oj[u][:], keys, rt[:, 1, m * GT:(m + 1) * GT].unsqueeze(2).broadcast_to([P, GT, PK]), ALU.is_equal)
                        nc.vector.tensor_tensor(oi[u][:], keys, rt[:, 0, m * GT:(m + 1) * GT].unsqueeze(2).broadcast_to([P, GT, PK]),
                                                ALU.is_equal).then_inc(sem("onehot"), 1)
                    if not (kind is LAST and s >= SLOTS - 2):
                        split_d(c + 2, n)
                    for piece in kind["own"][s]:
                        topk(t, piece)
                    for piece in kind["next"][s]:
                        topk(t + 1, piece)

            tile(0, FIRST)
            with dve.Fori(1, TT - 1) as t:
                tile(t, INNER)
            tile(TT - 1, LAST)

        @block.tensor
        def _(pe):
            def turn(t):
                pe.wait_ge(sem("routed"), START + t + 1)
                pe.wait_ge(sem("rt"), START + t)
                for c in range(3):
                    ins = nc.tensor.transpose(psT[:, c * P:(c + 1) * P], route[:, c].rearrange("p h a -> p (h a)"), ident[:])
                ins.then_inc(sem("turned"), 1)

            def tile(t, kind):
                for s in range(SLOTS):
                    c, n = SLOTS * t + s, s % 2
                    pe.wait_ge(sem("d_lo"), START + c + 1)
                    if kind is not FIRST or s >= 2:
                        pe.wait_ge(sem("gelu"), START + c - 1)
                    for h in range(2):
                        for k in range(KD):
                            for m, (a, b) in enumerate(float32r_products(dh, dl, xh, xl)):
                                ins = nc.tensor.matmul(psd[n][:, h * HALF:(h + 1) * HALF], a[n][:, k, :], b[:, k, h * HALF:(h + 1) * HALF],
                                                       start=(k == 0 and m == 0), stop=(k == KD - 1 and m == 2))
                    ins.then_inc(sem("d_mm"), 1)
                    for m in kind["groups"][s]:
                        pe.wait_ge(sem("gated"), START + NG * t + (m + 1))
                        for b in range(2):
                            if m > 0 or kind is not FIRST:
                                pe.wait_ge(sem("W"), START + (HB * t + (2 * m + b - 1) if m > 0 else HB * t))
                            for k in range(4):
                                ins = nc.tensor.matmul(psw[b][:, k * PK:(k + 1) * PK], oi[m % 2][:, 4 * b + k, :], oj[m % 2][:, 4 * b + k, :],
                                                       start=True, stop=True)
                            ins.then_inc(sem("w_mm"), 1)
                    if s == kind["turn"]:
                        turn(t)

            tile(0, FIRST)
            with pe.Fori(1, TT - 1) as t:
                tile(t, INNER)
            tile(TT - 1, LAST)


def stage_up(nc, g):
    NCH = PK
    G = 4
    NR = NCH // G
    NB = 8
    with ExitStack() as ctx:
        def sb(name, shape, dt=F32):
            return ctx.enter_context(nc.sbuf_tensor(name, shape, dt))

        sem = ctx.enter_context(stage_semaphores(nc, "e",
            "y_add rstd normed stats aggr var scaled final ld_A0 ld_A1 ld_u0 ld_u1 ld_y C_lo ld_ln st_out "
            "y_mm u_hi weighted C_hi power y_init"))
        y = sb("e_y", [P, TT, D])
        uraw = [sb(f"e_uraw{u}", [P, D]) for u in range(2)]
        araw = [sb(f"e_araw{u}", [P, T]) for u in range(2)]
        Wt = [sb(f"e_W{u}", [P, T]) for u in range(2)]
        uh = [sb(f"e_uh{u}", [P, D], F32R) for u in range(2 * G)]
        ul = [sb(f"e_ul{u}", [P, D], F32R) for u in range(2 * G)]
        Ch = [sb(f"e_Ch{u}", [P, T], F32R) for u in range(2 * G)]
        Cl = [sb(f"e_Cl{u}", [P, T], F32R) for u in range(2 * G)]
        stats, mv = [sb(f"e_stats{u}", [P, 2, 6]) for u in range(2)], [sb(f"e_mv{u}", [P, 2]) for u in range(2)]
        rstd, power = [sb(f"e_rstd{u}", [P, 1]) for u in range(2)], sb("e_power", [P, 1])
        psy = [ctx.enter_context(nc.psum_tensor(f"e_psy{u}", [P, HALF], F32)) for u in range(NB)]
        block = ctx.enter_context(nc.Block())

        def stats_of(dve, t):
            u = t % 2
            dve.wait_ge(sem("y_add"), START + 16 * (NR - 1) + 2 * t + 2)
            if t >= 2:
                dve.wait_ge(sem("rstd"), START + t - 1)
                dve.wait_ge(sem("normed"), START + t - 1)
            for h in range(2):
                ins = nc.vector.bn_stats(stats[u][:, h, :], y[:, t, h * HALF:(h + 1) * HALF])
            ins.then_inc(sem("stats"), 1)
            dve.wait_ge(sem("stats"), START + t + 1)
            nc.vector.bn_aggr(mv[u][:], stats[u][:]).then_inc(sem("aggr"), 1)
            dve.wait_ge(sem("aggr"), START + t + 1)
            nc.vector.tensor_scalar(mv[u][:, 1:2], mv[u][:, 1:2], 1e-5, None, ALU.add).then_inc(sem("var"), 1)

        def norm(dve, t):
            u = t % 2
            dve.wait_ge(sem("rstd"), START + t + 1)
            nc.vector.tensor_scalar(y[:, t, :], y[:, t, :], mv[u][:, 0:1], rstd[u][:, 0:1], ALU.subtract, ALU.mult).then_inc(sem("normed"), 1)

        def affine(pool, t):
            pool.wait_ge(sem("normed"), START + t + 1)
            nc.gpsimd.tensor_tensor(y[:, t, :], y[:, t, :], araw[0][:], ALU.mult).then_inc(sem("scaled"), 1)
            pool.wait_ge(sem("scaled"), START + t + 1)
            nc.gpsimd.tensor_tensor(y[:, t, :], y[:, t, :], araw[1][:], ALU.add).then_inc(sem("final"), 1)

        @block.sync
        def _(sp):
            def load(c, n):
                for d, s, name in ((araw, g.act, "A"), (Wt, g.W, "A"), (uraw, g.up, "u")):
                    sp.dma_start(d[n][:], s[bass.ds(c, 1)].rearrange("o p k -> (o p) k")).then_inc(sem(f"ld_{name}{n}"), 16)

            load(0, 0)
            load(1, 1)
            for t in range(TT):
                sp.dma_start(y[:, t, :], g.x1[t * P:(t + 1) * P, :]).then_inc(sem("ld_y"), 16)
            with sp.Fori(0, NCH // 2 - 1) as i:
                for n in range(2):
                    sp.wait_ge(sem("C_lo"), START + 2 * i + (n + 1))
                    load(2 * i + (n + 2), n)
            sp.wait_ge(sem("C_lo"), START + NCH)
            for d, s in ((araw[0], g.ln2_gain), (araw[1], g.ln2_bias)):
                sp.dma_start(d[:], s.partition_broadcast(P)).then_inc(sem("ld_ln"), 16)
            for t in range(TT):
                sp.wait_ge(sem("final"), START + t + 1)
                sp.dma_start(g.out[t * P:(t + 1) * P, :], y[:, t, :]).then_inc(sem("st_out"), 16)
            sp.wait_ge(sem("st_out"), START + 16 * TT)

        @block.scalar
        def _(act):
            def prepare(r, par, pair):
                for q in range(G):
                    c, n, s = G * r + q, q % 2, par * G + q
                    act.wait_ge(sem(f"ld_u{n}"), START + 16 * (G // 2) * r + 16 * (q // 2 + 1))
                    if q == 0 and pair is not None:
                        act.wait_ge(sem("y_mm"), START + pair)
                    nc.scalar.copy(uh[s][:], uraw[n][:]).then_inc(sem("u_hi"), 1)
                    act.wait_ge(sem("weighted"), START + c + 1)
                    nc.scalar.copy(Ch[s][:], araw[n][:]).then_inc(sem("C_hi"), 1)

            prepare(0, 0, None)
            prepare(1, 1, None)
            with act.Fori(0, NR // 2 - 1) as i:
                for par in range(2):
                    prepare(2 * i + (2 + par), par, 32 * i + 16 * (par + 1))

        @block.gpsimd
        def _(pool):
            nc.gpsimd.memset(power[:], -0.5).then_inc(sem("power"), 1)
            with pool.Fori(0, NCH // 2) as i:
                for n in range(2):
                    pool.wait_ge(sem(f"ld_A{n}"), START + 32 * i + 32)
                    nc.gpsimd.tensor_tensor(araw[n][:], araw[n][:], Wt[n][:], ALU.mult).then_inc(sem("weighted"), 1)
            pool.wait_ge(sem("power"), START + 1)
            pool.wait_ge(sem("ld_ln"), START + 32)
            for t in range(TT):
                pool.wait_ge(sem("var"), START + t + 1)
                nc.gpsimd.tensor_tensor(rstd[t % 2][:], mv[t % 2][:, 1:2], power[:], ALU.pow).then_inc(sem("rstd"), 1)
                if t >= 1:
                    affine(pool, t - 1)
            affine(pool, TT - 1)

        @block.vector
        def _(dve):
            def low(r, par, q):
                c, n, s = G * r + q, q % 2, par * G + q
                dve.wait_ge(sem("u_hi"), START + c + 1)
                nc.vector.tensor_tensor(ul[s][:], uraw[n][:], uh[s][:].bitcast(F32), ALU.subtract)
                dve.wait_ge(sem("C_hi"), START + c + 1)
                nc.vector.tensor_tensor(Cl[s][:], araw[n][:], Ch[s][:].bitcast(F32), ALU.subtract).then_inc(sem("C_lo"), 1)

            def add(r, b):
                dve.wait_ge(sem("y_mm"), START + 16 * r + (b + 1))
                o = y[:, b // 2, b % 2 * HALF:(b % 2 + 1) * HALF]
                nc.vector.tensor_tensor(o, o, psy[b % NB][:], ALU.add).then_inc(sem("y_add"), 1)

            for q in range(G):
                low(0, 0, q)
            for t in range(TT):
                dve.wait_ge(sem("ld_y"), START + 16 * TT)
                nc.vector.tensor_scalar(y[:, t, :], y[:, t, :], ALPHA, None, ALU.mult).then_inc(sem("y_init"), 1)
            for q in range(G):
                low(1, 1, q)
            dve.wait_ge(sem("y_init"), START + TT)
            with dve.Fori(0, NR // 2 - 1) as i:
                for par in range(2):
                    for b in range(2 * TT):
                        add(2 * i + par, b)
                    for q in range(G):
                        low(2 * i + (2 + par), par, q)
            for r in (NR - 2, NR - 1):
                for b in range(2 * TT):
                    add(r, b)
                    if r == NR - 1 and b % 2:
                        stats_of(dve, b // 2)
                    if r == NR - 1 and b % 2 == 0 and b > 0:
                        norm(dve, b // 2 - 1)
            norm(dve, TT - 1)

        @block.tensor
        def _(pe):
            def up(r, par, first=False):
                pe.wait_ge(sem("C_lo"), START + G * r + G)
                for b in range(2 * TT):
                    t, h = b // 2, b % 2
                    if not first or b >= NB:
                        pe.wait_ge(sem("y_add"), START + 16 * r + (b - NB + 1))
                    for q in range(G):
                        s = G * par + q
                        for m, (a, v) in enumerate(float32r_products(Ch, Cl, uh, ul)):
                            ins = nc.tensor.matmul(psy[b % NB][:], a[s][:, t * P:(t + 1) * P], v[s][:, h * HALF:(h + 1) * HALF],
                                                   start=(q == 0 and m == 0), stop=(q == G - 1 and m == 2))
                    ins.then_inc(sem("y_mm"), 1)

            up(0, 0, first=True)
            up(1, 1)
            with pe.Fori(1, NR // 2) as i:
                for par in range(2):
                    up(2 * i + par, par)


def build_program(nc, g):
    def dram(name, shape):
        return nc.dram_tensor(name, shape, F32, kind="Internal").ap()

    g.hT = dram("hT", (N_IN, P, T))
    g.ba = dram("ba", (P, TT, 2 * DH))
    g.y = dram("y", (2 * AT, P, T))
    g.x1 = dram("x1", (T, D))
    g.x1T = dram("x1T", (KD, P, T))
    g.s = dram("s", (TT, P, 2 * PH, PK))
    g.act = dram("act", (PK, P, T))
    g.W = dram("W", (PK, P, T))
    stage_project(nc, g)
    stage_attention(nc, g)
    stage_deltanet(nc, g)
    with nc.sbuf_tensor("merged", [P, KD, T], F32) as merged:
        g.merged = merged
        stage_merge(nc, g)
        stage_out_norm(nc, g)
    with nc.sbuf_tensor("x1h", [P, KD, T], F32R) as g.x1h, nc.sbuf_tensor("x1l", [P, KD, T], F32R) as g.x1l:
        stage_scores(nc, g)
        stage_down_and_route(nc, g)
    stage_up(nc, g)


def host_constants():
    inv = (np.float32(10000.0) ** (-np.arange(0, AD, 2, dtype=np.float32) / np.float32(AD))).astype(np.float32)
    ang = (np.arange(T, dtype=np.float32)[:, None] * inv[None, :]).astype(np.float32)
    c, s = np.cos(ang).T, np.sin(ang).T
    d = np.arange(P)[:, None] - np.arange(T)[None, :] + (T - P)
    n = np.zeros(d.shape, np.float64)
    for window, r in ((128, 1), (512, 4), (2048, 16)):
        n += (d >= 0) & (d % r == 0) & (d <= window)
    bias = np.where(n > 0, np.log(np.maximum(n, 1.0)) * AD ** 0.5, NEG)
    i = np.arange(P)
    later = (i[None, :] >= i[:, None])
    level = np.zeros((P, 7, P), np.float32)
    for n in range(7):
        b = 1 << n
        same = (i[None, :] // (2 * b)) == (i[:, None] // (2 * b))
        level[:, n, :] = same & (i[:, None] // b % 2 == 0) & (i[None, :] // b % 2 == 1)
    return {
        "ident": np.eye(P, dtype=np.float32),
        "cos": np.ascontiguousarray(np.concatenate([c] * 4).astype(np.float32)),
        "sin": np.ascontiguousarray(np.concatenate([-s, s] * 2).astype(np.float32)),
        "bias": bias.astype(np.float32),
        "upto": later.astype(np.float32),
        "notlater": np.where(later, 0.0, NEG).astype(np.float32),
        "level": level,
        "iota": np.tile(np.arange(P, dtype=np.float32), (P, 1)),
    }


class Arrays:
    pass


def kernel(**inputs):
    import concourse.bacc as bacc
    from concourse.bass_utils import run_bass_kernel_spmd

    a = {k: np.asarray(v) for k, v in inputs.items()}
    w_in = a["w_in"][0]
    ba0 = 3 * AW + 3 * DW
    cols = np.r_[0:ba0, ba0 + 2 * DH:w_in.shape[1]]
    arrays = {
        "x": a["x"][0],
        "xT": a["x"][0].T,
        "w_in": w_in[:, cols].reshape(KD, P, N_IN, P).transpose(2, 1, 0, 3),
        "w_ba": w_in[:, ba0:ba0 + 2 * DH],
        "conv": a["dn_conv"][0].reshape(CONV, N_DN, P).transpose(2, 1, 0),
        "a_log": a["dn_A_log"][0],
        "dt_bias": a["dn_dt_bias"][0],
        "norm_gain": a["dn_norm_gain"][0][:, None],
        "w_branch": np.concatenate([a["w_branch_attn"][0], a["w_branch_delta"][0]]).reshape(2 * AT, P, KD, P).transpose(2, 1, 0, 3),
        "w_out": a["w_out"][0],
        "ln1_gain": a["ln1_gain"][0],
        "ln1_bias": a["ln1_bias"][0],
        "w_query": a["peer_w_query"][0].reshape(KD, P, 2 * PH, P).transpose(2, 1, 0, 3),
        "keys": a["peer_sub_keys"][0].reshape(2 * PH, PK, P).transpose(0, 2, 1),
        "down": a["peer_expert_down"][0].reshape(PK, PK, KD, P).transpose(1, 3, 2, 0),
        "up": a["peer_expert_up"][0].reshape(PK, PK, D).transpose(1, 0, 2),
        "ln2_gain": a["ln2_gain"][0],
        "ln2_bias": a["ln2_bias"][0],
        **host_constants(),
    }
    nc = bacc.Bacc("TRN2", target_bir_lowering=False, num_devices=1)
    g = Arrays()
    given = {}
    for name, v in arrays.items():
        v = np.ascontiguousarray(v)
        given[f"in_{name}"] = v
        g.__dict__[name] = nc.dram_tensor(f"in_{name}", v.shape, mybir.dt.from_np(v.dtype), kind="ExternalInput").ap()
    g.out = nc.dram_tensor("out", (T, D), F32, kind="ExternalOutput").ap()
    build_program(nc, g)
    r = run_bass_kernel_spmd(nc, [given], core_ids=[0])
    return r.results[0]["out"].reshape(1, T, D)
```

```python
import numpy as np

import concourse.bass as bass
from concourse import mybir
from contextlib import ExitStack, contextmanager

F32 = mybir.dt.float32
F32R = mybir.dt.float32r
U32 = mybir.dt.uint32
ALU = mybir.AluOpType
ACT = mybir.ActivationFunctionType
AX = mybir.AxisListType

P = 128
D = 1024
T = 1024
KD = D // P
TT = T // P
HALF = 512
AH, AD = 12, 64
AW = AH * AD
AT = AW // P
DH, DD = 6, 128
DW = DH * DD
CONV = 4
N_ATT = 3 * AT
N_DN = 3 * DH
N_GB = DH
N_BR = 2 * KD
N_IN = N_ATT + N_DN + N_GB + N_BR
PH, PK, TOP = 8, 128, 16
ALPHA = 2.0 ** 0.25
NEG = -1e30
START = 16


class Step:

    def __init__(self, sem, base=0):
        self.sem, self.base, self.n = sem, base, 0

    def inc(self, ins, by=1):
        self.n += by
        ins.then_inc(self.sem, by)
        return self.at()

    def at(self, back=0):
        return START + self.base + (self.n - back)

    def wait(self, eng, back=0):
        eng.wait_ge(self.sem, self.at(back))


@contextmanager
def stage_semaphores(nc, prefix, names):
    held = {name: nc.alloc_semaphore(f"{prefix}_{name}") for name in names.split()}
    for s in held.values():
        nc.gpsimd.sem_inc(s, START)
    nc.all_engine_barrier()
    yield held.__getitem__
    nc.clear_and_free_semaphores(list(held.values()))
    nc.all_engine_barrier()


def wait_alone(eng, sem, value, passed):
    eng.wait_ge(sem, value)
    eng.sem_inc(passed, 1)


def stage_project(nc, g):
    with ExitStack() as ctx:
        def sb(name, shape, dt=F32):
            return ctx.enter_context(nc.sbuf_tensor(name, shape, dt))

        sem = ctx.enter_context(stage_semaphores(nc, "p",
            "ld_x0 ld_x1 ld_x2 ld_x3 ld_x4 ld_x5 ld_x6 ld_x7 ld_w0 ld_w1 ld_c x_hi x_lo w_hi w_lo mm_done "
            "ba_done ba_out ba_st out_ready cin_ready cout_ready conv_step zeroed stored0 stored1"))

        xh, xl = sb("p_xh", [P, KD, T], F32R), sb("p_xl", [P, KD, T], F32R)
        wraw = [sb(f"p_wraw{u}", [P, KD, P]) for u in range(2)]
        wh = [sb(f"p_wh{u}", [P, KD, P], F32R) for u in range(2)]
        wl = [sb(f"p_wl{u}", [P, KD, P], F32R) for u in range(2)]
        cin = [sb(f"p_cin{u}", [P, CONV - 1 + T]) for u in range(2)]
        cout = [sb(f"p_cout{u}", [P, T]) for u in range(2)]
        out = [sb(f"p_out{u}", [P, T]) for u in range(2)]
        cw = sb("p_cw", [P, N_DN, CONV])
        wba = sb("p_wba", [P, KD, 2 * DH])
        ba = sb("p_ba", [P, TT, 2 * DH])
        x = sb("p_x", [P, KD, T])
        ps = [ctx.enter_context(nc.psum_tensor(f"p_ps{u}", [P, T], F32)) for u in range(2)]
        psb = ctx.enter_context(nc.psum_tensor("p_psb", [P, HALF], F32))

        ld_x = [sem(f"ld_x{u}") for u in range(KD)]
        ld_w = [sem(f"ld_w{u}") for u in range(2)]
        ld_c = sem("ld_c")
        x_hi, x_lo = sem("x_hi"), sem("x_lo")
        w_hi, w_lo = sem("w_hi"), sem("w_lo")
        mm_done = sem("mm_done")
        ba_done, ba_out, ba_st = sem("ba_done"), sem("ba_out"), sem("ba_st")
        out_ready = sem("out_ready")
        cin_ready, cout_ready, conv_step = sem("cin_ready"), sem("cout_ready"), sem("conv_step")
        zeroed = sem("zeroed")
        stored = [sem(f"stored{u}") for u in range(2)]
        block = ctx.enter_context(nc.Block())
        pairs = N_IN // 2
        att, dn, gb = N_ATT // 2, N_DN // 2, N_GB // 2

        @block.sync
        def _(sp):
            for k in range(KD):
                sp.dma_start(x[:, k, :], g.xT[k * P:(k + 1) * P, :]).then_inc(ld_x[k], 16)
                if k < 2:
                    sp.dma_start(wraw[k][:], g.w_in[k]).then_inc(ld_w[k], 16)
            sp.dma_start(wba[:], g.w_ba.rearrange("(k p) c -> p k c", p=P)).then_inc(ld_c, 16)
            sp.dma_start(cw[:], g.conv).then_inc(ld_c, 16)

            def store(i, u):
                sp.wait_ge(out_ready, START + 2 * i + (u + 1))
                sp.dma_start(g.hT[bass.ds(2 * i + u, 1)].rearrange("o p t -> (o p) t"), out[u][:]).then_inc(stored[u], 16)

            with sp.Fori(0, pairs - 1) as i:
                for u in range(2):
                    sp.wait_ge(w_lo, START + 2 * i + (u + 1))
                    sp.dma_start(wraw[u][:], g.w_in[bass.ds(2 * i + (2 + u), 1)].rearrange("o p k c -> (o p) k c")).then_inc(ld_w[u], 16)
                    store(i, u)
            for u in range(2):
                store(pairs - 1, u)
            sp.wait_ge(ba_out, START + 1)
            sp.dma_start(g.ba, ba[:]).then_inc(ba_st, 16)
            sp.wait_ge(ba_st, START + 16)
            for u in range(2):
                sp.wait_ge(stored[u], START + 16 * pairs)

        @block.scalar
        def _(act):
            def split(u, n):
                act.wait_ge(ld_w[u], START + n)
                nc.scalar.copy(wh[u][:], wraw[u][:]).then_inc(w_hi, 1)

            for k in range(KD):
                act.wait_ge(ld_x[k], START + 16)
                nc.scalar.copy(xh[:, k, :], x[:, k, :]).then_inc(x_hi, 1)
                if k < 2:
                    split(k, 16)

            def body(i, kind, last=False):
                for u in range(2):
                    act.wait_ge(mm_done, START + 2 * i + (u + 1))
                    if kind == "conv":
                        j = i - att
                        act.wait_ge(cout_ready, START + 2 * j + u)
                        nc.scalar.copy(cin[u][:, CONV - 1:], ps[u][:]).then_inc(cin_ready, 1)
                    else:
                        act.wait_ge(stored[u], START + 16 * i)
                        f = {"att": ACT.Copy, "gb": ACT.Silu, "br": ACT.Sigmoid}[kind]
                        nc.scalar.activation(out[u][:], ps[u][:], f).then_inc(out_ready, 1)
                    if not last:
                        split(u, 16 * i + 32)
                    if kind == "conv":
                        act.wait_ge(cout_ready, START + 2 * j + (u + 1))
                        act.wait_ge(stored[u], START + 16 * i)
                        nc.scalar.activation(out[u][:], cout[u][:], ACT.Silu).then_inc(out_ready, 1)

            act.wait_ge(zeroed, START + 2)
            with act.Fori(0, att) as i:
                body(i, "att")
            with act.Fori(att, att + dn) as i:
                body(i, "conv")
            with act.Fori(att + dn, att + dn + gb) as i:
                body(i, "gb")
            with act.Fori(att + dn + gb, pairs - 1) as i:
                body(i, "br")
            body(pairs - 1, "br", last=True)

        @block.vector
        def _(dve):
            nc.vector.memset(cin[0][:, 0:CONV - 1], 0.0).then_inc(zeroed, 1)
            nc.vector.memset(cin[1][:, 0:CONV - 1], 0.0).then_inc(zeroed, 1)
            def split(u, n):
                dve.wait_ge(w_hi, START + n)
                nc.vector.tensor_tensor(wl[u][:], wraw[u][:], wh[u][:].bitcast(F32), ALU.subtract).then_inc(w_lo, 1)

            for k in range(KD):
                dve.wait_ge(x_hi, START + k + 1)
                nc.vector.tensor_tensor(xl[:, k, :], x[:, k, :], xh[:, k, :].bitcast(F32), ALU.subtract).then_inc(x_lo, 1)
                if k < 2:
                    split(k, k + 1)
            dve.wait_ge(ld_c, START + 32)

            def body(i, conv):
                for u in range(2):
                    if conv:
                        j = i - att
                        step = Step(conv_step, 6 * j + 3 * u)
                        dve.wait_ge(cin_ready, START + 2 * j + (u + 1))
                        dve.wait_ge(out_ready, START + 2 * i + u)
                        w = [cw[:, bass.ds(2 * j + u, 1), t:t + 1].rearrange("p a b -> p (a b)") for t in range(CONV)]
                        step.inc(nc.vector.tensor_scalar(cout[u][:], cin[u][:, 0:T], w[0], None, ALU.mult))
                        for t in range(1, CONV):
                            step.wait(dve)
                            ins = nc.vector.scalar_tensor_tensor(cout[u][:], cin[u][:, t:t + T], w[t], cout[u][:],
                                                                 ALU.mult, ALU.add)
                            if t < CONV - 1:
                                step.inc(ins)
                        ins.then_inc(cout_ready, 1)
                    split(u, 2 * i + (u + 3))

            with dve.Fori(0, att) as i:
                body(i, False)
            with dve.Fori(att, att + dn) as i:
                body(i, True)
            with dve.Fori(att + dn, pairs - 1) as i:
                body(i, False)
            dve.wait_ge(ba_done, START + 1)
            nc.vector.tensor_copy(ba[:], psb[:, 0:TT * 2 * DH].rearrange("p (t c) -> p t c", t=TT)).then_inc(ba_out, 1)

        @block.tensor
        def _(pe):
            with pe.Fori(0, pairs) as i:
                for u in range(2):
                    pe.wait_ge(w_lo, START + 2 * i + (u + 1))
                    for k in range(KD):
                        if u == 0:
                            pe.wait_ge(x_lo, START + k + 1)
                        for h in range(2):
                            for n, (a, b) in enumerate(((wh, xh), (wh, xl), (wl, xh))):
                                ins = nc.tensor.matmul(ps[u][:, h * HALF:(h + 1) * HALF], a[u][:, k, :], b[:, k, h * HALF:(h + 1) * HALF],
                                                       start=(k == 0 and n == 0), stop=(k == KD - 1 and n == 2))
                    ins.then_inc(mm_done, 1)
            pe.wait_ge(ld_c, START + 32)
            for t in range(TT):
                for k in range(KD):
                    ins = nc.tensor.matmul(psb[:, t * 2 * DH:(t + 1) * 2 * DH], x[:, k, t * P:(t + 1) * P],
                                           wba[:, k, :], start=(k == 0), stop=(k == KD - 1))
            ins.then_inc(ba_done, 1)


def stage_attention(nc, g):
    HPT = P // AD
    ITEMS = HPT * TT
    groups = [1 + qt // 4 for qt in range(TT)] * HPT
    through = [sum(groups[:n + 1]) for n in range(ITEMS)]
    G = sum(groups)
    LAG = 3
    with ExitStack() as ctx:
        def sb(name, shape, dt=F32):
            return ctx.enter_context(nc.sbuf_tensor(name, shape, dt))

        sem = ctx.enter_context(stage_semaphores(nc, "a",
            "ld_table ld_c ld_v ld_q v_tr v_out turned rope_done split ld_V0 ld_V1 stacked0 stacked1 s_done "
            "masked max_ready exp_done tr_done pT_ready pv_done recip_done o_out y_tr y_out passed stored"))

        cos, sin = sb("a_cos", [P, T]), sb("a_sin", [P, T])
        bias, ident = sb("a_bias", [P, T]), sb("a_ident", [P, P])
        vT, V = sb("a_vT", [P, AT, T]), sb("a_V", [P, TT, AW])
        raw = [sb(f"a_raw{n}", [P, T]) for n in range(4)]
        qk = [sb(f"a_{n}", [P, T]) for n in "qk"]
        qk_hi = [sb(f"a_{n}_hi", [P, T], F32R) for n in "qk"]
        qk_lo = [sb(f"a_{n}_lo", [P, T], F32R) for n in "qk"]
        stack = [[[sb(f"a_stack{u}{h}{n}", [P, T], F32R) for n in range(3)] for h in range(HPT)] for u in range(2)]
        Vs = [sb(f"a_Vs{u}", [P, TT, P]) for u in range(2)]
        sc = [sb(f"a_sc{u}", [P, T]) for u in range(2)]
        pb = [sb(f"a_pb{u}", [P, T]) for u in range(2)]
        pT = [sb(f"a_pT{u}", [P, TT, P]) for u in range(2)]
        ya, yaT = sb("a_ya", [P, TT, AW]), vT
        mx, nm = sb("a_mx", [P, ITEMS]), sb("a_nm", [P, ITEMS])
        rs, ri = sb("a_rs", [P, ITEMS]), sb("a_ri", [P, ITEMS])
        psS = [ctx.enter_context(nc.psum_tensor(f"a_psS{u}", [P, T], F32)) for u in range(2)]
        psT = [ctx.enter_context(nc.psum_tensor(f"a_psT{u}", [P, HALF], F32)) for u in range(2)]
        psO = [ctx.enter_context(nc.psum_tensor(f"a_psO{u}", [P, HALF], F32)) for u in range(2)]

        ld_table, ld_c, ld_v, ld_q = sem("ld_table"), sem("ld_c"), sem("ld_v"), sem("ld_q")
        v_tr, v_out = sem("v_tr"), sem("v_out")
        turned, rope_done, split, ld_V = sem("turned"), sem("rope_done"), sem("split"), [sem(f"ld_V{u}") for u in range(2)]
        stacked = [sem(f"stacked{u}") for u in range(2)]
        s_done, masked, max_ready = sem("s_done"), sem("masked"), sem("max_ready")
        exp_done, tr_done, pT_ready = sem("exp_done"), sem("tr_done"), sem("pT_ready")
        pv_done, recip_done, o_out = sem("pv_done"), sem("recip_done"), sem("o_out")
        y_tr, y_out, passed, stored = sem("y_tr"), sem("y_out"), sem("passed"), sem("stored")
        block = ctx.enter_context(nc.Block())

        def multiply(engine, eng, i, n):
            eng.wait_ge(ld_q, START + 160 * i + 160)
            engine.tensor_tensor(raw[n][:], raw[n][:], (cos, sin)[n % 2][:], ALU.mult).then_inc(turned, 1)

        def add_and_split(engine, eng, n, products, sums):
            eng.wait_ge(turned, START + products)
            engine.tensor_tensor(qk[n][:], raw[2 * n][:], raw[2 * n + 1][:], ALU.add).then_inc(rope_done, 1)
            engine.tensor_tensor(qk_hi[n][:], raw[2 * n][:], raw[2 * n + 1][:], ALU.add).then_inc(rope_done, 1)
            eng.wait_ge(rope_done, START + sums)
            engine.tensor_tensor(qk_lo[n][:], qk[n][:], qk_hi[n][:].bitcast(F32), ALU.subtract).then_inc(split, 1)

        def evac(act, i, n, grp):
            qt = n % TT
            for b in range(groups[n]):
                act.wait_ge(tr_done, START + G * i + (grp + 1))
                act.wait_ge(pv_done, START + ITEMS * i + max(n - 1, 0))
                w = min(4, qt + 1 - 4 * b)
                nc.scalar.copy(pT[n % 2][:, 4 * b:4 * b + w, :],
                               psT[grp % 2][:, 0:w * P].rearrange("p (a t) -> p a t", t=P)).then_inc(pT_ready, 1)
                grp += 1
            return grp

        @block.sync
        def _(sp):
            for d, s in ((cos, g.cos), (sin, g.sin)):
                sp.dma_start(d[:], s).then_inc(ld_table, 16)

            def load(i):
                for n, first in ((0, 0), (2, AT)):
                    src = g.hT[bass.ds(i + first, 1)].rearrange("o p t -> (o p) t")
                    sp.dma_start(raw[n][:], src).then_inc(ld_q, 16)
                    for r in range(4):
                        s = r ^ 1
                        sp.dma_start(raw[n + 1][32 * r:32 * r + 32, :], src[32 * s:32 * s + 32, :]).then_inc(ld_q, 16)

            def restack(par):
                for h in range(HPT):
                    rows = slice(h * AD, (h + 1) * AD)
                    for n, parts in enumerate(((qk_hi[0], qk_lo[0]), (qk_hi[1], qk_hi[1]), (qk_lo[1], qk_lo[1]))):
                        for m, part in enumerate(parts):
                            sp.dma_start(stack[par][h][n][m * AD:(m + 1) * AD, :].bitcast(F32), part[rows, :].bitcast(F32)).then_inc(stacked[par], 16)

            def columns(i, par):
                sp.dma_start(Vs[par][:], V[:, :, bass.ds(i * P, P)]).then_inc(ld_V[par], 16)

            load(0)
            sp.dma_start(ident[:], g.ident).then_inc(ld_c, 16)
            for n in range(AT):
                sp.dma_start(vT[:, n, :], g.hT[2 * AT + n]).then_inc(ld_v, 16)
            sp.dma_start(bias[:], g.bias).then_inc(ld_c, 16)
            sp.wait_ge(split, START + 2)
            restack(0)
            load(1)
            sp.wait_ge(v_out, START + 2 * TT)
            columns(0, 0)
            columns(1, 1)

            def ahead(j, par, more=True):
                if more:
                    sp.wait_ge(rope_done, START + 8 * j + (4 * par + 8))
                    load(2 * j + (par + 2))
                sp.wait_ge(split, START + 4 * j + (2 * par + 4))
                if par:
                    sp.wait_ge(s_done, START + 2 * ITEMS * j + ITEMS)
                else:
                    sp.wait_ge(s_done, START + 2 * ITEMS * j)
                restack(1 - par)
                if more:
                    sp.wait_ge(pv_done, START + 2 * ITEMS * j + ITEMS * (par + 1))
                    columns(2 * j + (par + 2), par)

            with sp.Fori(0, AT // 2 - 1) as j:
                ahead(j, 0)
                ahead(j, 1)
            ahead(AT // 2 - 1, 0, more=False)
            for kb in range(0, TT, 2):
                sp.wait_ge(y_out, START + 2 * kb + 4)
                cols = slice(kb * P, (kb + 2) * P)
                sp.dma_start(g.y[0:AT, :, cols].rearrange("n p t -> p n t"), yaT[:, :, cols]).then_inc(stored, 16)
            sp.wait_ge(stored, START + 16 * TT // 2)

        @block.scalar
        def _(act):
            def tile(i):
                grp = 0
                for n in range(ITEMS):
                    N = (n % TT + 1) * P
                    act.wait_ge(max_ready, START + ITEMS * i + (n + 1))
                    act.wait_ge(tr_done, START + (G * i + (through[n - 2] if n >= 2 else 0)))
                    nc.scalar.activation(pb[n % 2][:, 0:N], sc[n % 2][:, 0:N], ACT.Exp, bias=nm[:, n:n + 1],
                                         accum_out=rs[:, n:n + 1]).then_inc(exp_done, 1)
                    if n >= 1:
                        grp = evac(act, i, n - 1, grp)
                grp = evac(act, i, ITEMS - 1, grp)

            with act.Fori(0, AT // 2) as j:
                tile(2 * j)
                tile(2 * j + 1)

        @block.gpsimd
        def _(pool):
            pool.wait_ge(ld_table, START + 32)

            def rope(i, u, use):
                for n in range(4):
                    multiply(nc.gpsimd, pool, i, n)
                pool.wait_ge(stacked[u], START + use)
                for n in range(2):
                    add_and_split(nc.gpsimd, pool, n, 4 * i + (2 * n + 2), 4 * i + (2 * n + 2))

            FILL = 16 * 6 * HPT
            for n in (0, 1):
                multiply(nc.gpsimd, pool, 0, n)
            add_and_split(nc.gpsimd, pool, 0, 4, 4)
            rope(1, 0, FILL)
            with pool.Fori(1, AT // 2) as j:
                for par in range(2):
                    if par == 0:
                        rope(2 * j, 1, FILL * j)
                    else:
                        rope(2 * j + 1, 0, FILL * j + FILL)

        @block.vector
        def _(dve):
            dve.wait_ge(ld_table, START + 32)
            for n in (2, 3):
                multiply(nc.vector, dve, 0, n)
            add_and_split(nc.vector, dve, 1, 4, 4)
            for kb in range(TT):
                for h in range(2):
                    n = 2 * kb + h
                    dve.wait_ge(v_tr, START + n + 1)
                    nc.vector.tensor_copy(V[:, kb, h * 384:(h + 1) * 384], psT[h][:, 0:384]).then_inc(v_out, 1)
            dve.wait_ge(ld_c, START + 32)

            def tile(i):
                def out(n):
                    h, qt = n // TT, n % TT
                    dve.wait_ge(exp_done, START + ITEMS * i + (n + 1))
                    nc.vector.reciprocal(ri[:, n:n + 1], rs[:, n:n + 1]).then_inc(recip_done, 1)
                    dve.wait_ge(recip_done, START + ITEMS * i + (n + 1))
                    dve.wait_ge(pv_done, START + ITEMS * i + (n + 1))
                    nc.vector.tensor_scalar(ya[:, qt, bass.ds(i * P + h * AD, AD)], psO[n % 2][:, 0:AD],
                                            ri[:, n:n + 1], None, ALU.mult).then_inc(o_out, 1)

                for n in range(ITEMS):
                    qt = n % TT
                    N = (qt + 1) * P
                    dve.wait_ge(exp_done, START + ITEMS * i + max(n - 1, 0))
                    wait_alone(dve, s_done, START + ITEMS * i + (n + 1), passed)
                    nc.vector.tensor_tensor_reduce(out=sc[n % 2][:, 0:N], in0=psS[n % 2][:, 0:N],
                                                   in1=bias[:, T - N:T], scale=AD ** -0.5, scalar=NEG,
                                                   op0=ALU.add, op1=ALU.max,
                                                   accum_out=mx[:, n:n + 1]).then_inc(masked, 1)
                    dve.wait_ge(masked, START + ITEMS * i + (n + 1))
                    nc.vector.tensor_scalar(nm[:, n:n + 1], mx[:, n:n + 1], -1.0, None, ALU.mult).then_inc(max_ready, 1)
                    if n >= LAG:
                        out(n - LAG)
                for n in range(ITEMS - LAG, ITEMS):
                    out(n)

            with dve.Fori(0, AT // 2) as j:
                tile(2 * j)
                tile(2 * j + 1)
            for kb in range(TT):
                for h in range(2):
                    n = 2 * kb + h
                    dve.wait_ge(y_tr, START + n + 1)
                    nc.vector.tensor_copy(yaT[:, 3 * h:3 * h + 3, kb * P:(kb + 1) * P],
                                          psT[h][:, 0:384].rearrange("p (a t) -> p a t", t=P)).then_inc(y_out, 1)

        @block.tensor
        def _(pe):
            pe.wait_ge(ld_c, START + 32)
            pe.wait_ge(ld_v, START + 16 * AT)
            for kb in range(TT):
                for h in range(2):
                    n = 2 * kb + h
                    if n >= 2:
                        pe.wait_ge(v_out, START + n - 1)
                    for a in range(3):
                        ins = nc.tensor.transpose(psT[h][:, a * P:(a + 1) * P], vT[:, 3 * h + a, kb * P:(kb + 1) * P], ident[:])
                    ins.then_inc(v_tr, 1)
            pe.wait_ge(v_out, START + 2 * TT)

            def tile(i, par):
                v = Vs[par]

                def scores(n):
                    h, qt = n // TT, n % TT
                    N = (qt + 1) * P
                    pe.wait_ge(masked, START + ITEMS * i + max(n - 1, 0))
                    q, k_hi, k_lo = stack[par][h]
                    N += N % 256
                    for a in range(0, N, HALF):
                        b = min(a + HALF, N)
                        for m, k in enumerate((k_hi, k_lo)):
                            ins = nc.tensor.matmul(psS[n % 2][:, a:b], q[:, qt * P:(qt + 1) * P], k[:, a:b],
                                                   start=(m == 0), stop=(m == 1))
                    ins.then_inc(s_done, 1)

                def values(n):
                    h, qt = n // TT, n % TT
                    pe.wait_ge(pT_ready, START + G * i + through[n])
                    pe.wait_ge(o_out, START + ITEMS * i + max(n - 1, 0))
                    for kb in range(qt + 1):
                        ins = nc.tensor.matmul(psO[n % 2][:, 0:AD], pT[n % 2][:, kb, :],
                                               v[:, kb, h * AD:(h + 1) * AD], start=(kb == 0), stop=(kb == qt))
                    ins.then_inc(pv_done, 1)

                pe.wait_ge(stacked[par], START + 48 * HPT * (i - par) + 96 * HPT)
                pe.wait_ge(ld_V[par], START + 8 * (i - par) + 16)
                scores(0)
                scores(1)
                grp = 0
                for n in range(ITEMS):
                    if n + 2 < ITEMS:
                        scores(n + 2)
                    pe.wait_ge(exp_done, START + ITEMS * i + (n + 1))
                    for b in range(groups[n]):
                        pe.wait_ge(pT_ready, START + G * i + max(grp - 1, 0))
                        for kb in range(4 * b, min(4 * b + 4, n % TT + 1)):
                            ins = nc.tensor.transpose(psT[grp % 2][:, kb % 4 * P:(kb % 4 + 1) * P],
                                                      pb[n % 2][:, kb * P:(kb + 1) * P], ident[:])
                        ins.then_inc(tr_done, 1)
                        grp += 1
                    if n >= 1:
                        values(n - 1)
                values(ITEMS - 1)

            with pe.Fori(0, AT // 2) as j:
                tile(2 * j, 0)
                tile(2 * j + 1, 1)
            pe.wait_ge(o_out, START + ITEMS * AT)
            for kb in range(TT):
                for h in range(2):
                    n = 2 * kb + h
                    if n >= 2:
                        pe.wait_ge(y_out, START + n - 1)
                    for a in range(3):
                        ins = nc.tensor.transpose(psT[h][:, a * P:(a + 1) * P], ya[:, kb, (3 * h + a) * P:(3 * h + a + 1) * P], ident[:])
                    ins.then_inc(y_tr, 1)


def stage_deltanet(nc, g):
    C = P
    NC = T // C
    HH = DH // 2
    W = HH * P
    LEVELS = 7
    with ExitStack() as ctx:
        def sb(name, shape, dt=F32):
            return ctx.enter_context(nc.sbuf_tensor(name, shape, dt))

        def full(name):
            return sb(name, [P, 2, HH, P])

        sem = ctx.enter_context(stage_semaphores(nc, "d",
            "ld_c ld_raw0 ld_raw1 ld_raw2 ld_gate stored front0 front1 front2 y_out ones sumsq tk rnorm "
            "chunk_factors tr2 kg tkb tq tqd M X_mm LT state decayed w_mm state_mm kd out_sumsq out_rnorm "
            "beta exp z_abs ez squares turned qdT kbT qT decay decay_exp T_tr T_first X w vn_mm vn o_mm "
            "out_squares G_ready exps z g rowG decay_step ss_raw vb on_tr qk kT kk_mm T0 TX_mm T TT so_raw on "
            "G_mm g_copied"))

        ident, upto, later = sb("d_ident", [P, P]), sb("d_upto", [P, P]), sb("d_later", [P, P])
        level = sb("d_level", [P, LEVELS, P])
        ones, half_power = sb("d_ones", [P, P]), sb("d_half_power", [P, 2 * DH])
        ba, z = sb("d_ba", [P, NC, 2 * DH]), sb("d_z", [P, NC, DH])
        neg_a, dtb, gain = sb("d_neg_a", [P, DH]), sb("d_dtb", [P, DH]), sb("d_gain", [P, 1])
        ez, gg = sb("d_ez", [P, NC, DH]), sb("d_gg", [P, NC, DH])
        beta, eG, eK, gl = (sb(f"d_{n}", [P, NC, DH]) for n in ("beta", "eG", "eK", "gl"))
        Gs = sb("d_Gs", [P, NC, DH])
        gB = full("d_gB")
        cbeta, ceG, ceK, cgl, cG = (sb(f"d_c{n}", [P, DH]) for n in ("beta", "eG", "eK", "gl", "G"))
        raw = [sb(f"d_raw{n}", [P, DH, P]) for n in range(3)]
        gate = sb("d_gate", [P, DH, P])
        sq = sb("d_sq", [P, 2, 2, HH, P])
        ss, rn = sb("d_ss", [P, 2 * DH]), sb("d_rn", [P, 2 * DH])
        tq, tqd, tk, tkb, kd, kg, vb = (full(f"d_{n}") for n in ("tq", "tqd", "tk", "tkb", "kd", "kg", "vb"))
        qT, kT, kbT, qdT = (full(f"d_{n}T") for n in ("q", "k", "kb", "qd"))
        dec, MT, qk = full("d_dec"), full("d_MT"), full("d_qk")
        LT = [full(f"d_LT{u}") for u in range(2)]
        Tm, TT_, X = full("d_Tm"), full("d_TT"), full("d_X")
        nwT, vn, S, S2 = full("d_nwT"), full("d_vn"), full("d_S"), full("d_S2")
        sqo, so, ro, on = full("d_sqo"), sb("d_so", [P, DH]), sb("d_ro", [P, DH]), full("d_on")
        ybT = sb("d_ybT", [P, DH, T])
        ps = {n: ctx.enter_context(nc.psum_tensor(f"d_ps{n}", [P, 2, HALF], F32)) for n in "ABCD"}

        def pw(n, h=None):
            v = ps[n][:, :, 0:W].rearrange("p a (b t) -> p a b t", t=P)
            return v if h is None else v[:, h]

        def cast(v, h=None):
            v = v.rearrange("p (a b) -> p a b", a=2)
            if h is None:
                return v.unsqueeze(3).broadcast_to([P, 2, HH, P])
            return v[:, h].unsqueeze(2).broadcast_to([P, HH, P])

        def heads(v, h):
            return v.unsqueeze(1).broadcast_to([P, HH, P])

        def at(v, h):
            return v[:, h // HH, h % HH, :]

        block = ctx.enter_context(nc.Block())

        @block.sync
        def _(sp):
            srcs = [(ident, g.ident), (upto, g.upto), (later, g.notlater), (level, g.level), (ba, g.ba),
                    (neg_a, g.a_log.partition_broadcast(P)), (dtb, g.dt_bias.partition_broadcast(P)),
                    (gain, g.norm_gain)]
            for d, s in srcs:
                sp.dma_start(d[:], s).then_inc(sem("ld_c"), 16)

            def load(i, n):
                src = g.hT[N_ATT + n * DH:N_ATT + (n + 1) * DH, :, bass.ds(i * C, C)]
                sp.dma_start(raw[n][:], src.rearrange("n p t -> p n t")).then_inc(sem(f"ld_raw{n}"), 16)

            def load_gate(i):
                src = g.hT[N_ATT + N_DN:N_ATT + N_DN + N_GB, :, bass.ds(i * C, C)]
                sp.dma_start(gate[:], src.rearrange("n p t -> p n t")).then_inc(sem("ld_gate"), 16)

            def store(i):
                sp.dma_start(g.y[AT:AT + DH, :, bass.ds(i * C, C)].rearrange("n p t -> p n t"),
                             ybT[:, :, bass.ds(i * C, C)]).then_inc(sem("stored"), 16)

            for n in range(3):
                load(0, n)
            load_gate(0)
            with sp.Fori(1, NC) as i:
                for n in range(3):
                    sp.wait_ge(sem(f"front{n}"), START + i)
                    load(i, n)
                sp.wait_ge(sem("y_out"), START + 2 * i)
                load_gate(i)
                store(i - 1)
            sp.wait_ge(sem("y_out"), START + 2 * NC)
            store(NC - 1)
            sp.wait_ge(sem("stored"), START + 16 * NC)

        @block.gpsimd
        def _(pool):
            nc.gpsimd.memset(ones[:], 1.0).then_inc(sem("ones"), 1)
            nc.gpsimd.memset(half_power[:], -0.5).then_inc(sem("ones"), 1)
            nc.gpsimd.memset(S[:], 0.0).then_inc(sem("ones"), 1)
            pool.wait_ge(sem("ones"), START + 3)

            def norm(f):
                pool.wait_ge(sem("sumsq"), START + f + 1)
                pool.wait_ge(sem("tk"), START + f)
                nc.gpsimd.tensor_tensor(rn[:], ss[:], half_power[:], ALU.pow).then_inc(sem("rnorm"), 1)

            def front(f):
                pool.wait_ge(sem("chunk_factors"), START + f + 1)
                pool.wait_ge(sem("tr2"), START + 4 * f)
                pool.wait_ge(sem("kg"), START + f)
                pool.wait_ge(sem("tk"), START + f + 1)
                nc.gpsimd.tensor_tensor(tkb[:], tk[:], cast(cbeta[:]), ALU.mult).then_inc(sem("tkb"), 1)
                pool.wait_ge(sem("tq"), START + f + 1)
                nc.gpsimd.tensor_tensor(tqd[:], tq[:], cast(ceG[:]), ALU.mult).then_inc(sem("tqd"), 1)

            def chunk(i, last=False):
                def select(v):
                    for h in range(2):
                        pool.wait_ge(sem("M"), START + 2 * i + 1 + h)
                        if v >= 3:
                            pool.wait_ge(sem("X_mm"), START + 12 * i + 2 * (v - 3) + h + 1)
                        nc.gpsimd.tensor_tensor(LT[v % 2][:, h], MT[:, h], heads(level[:, v, :], h), ALU.mult).then_inc(sem("LT"), 1)

                pool.wait_ge(sem("state"), START + i)
                nc.gpsimd.tensor_tensor(S2[:], S[:], cast(cgl[:]), ALU.mult).then_inc(sem("decayed"), 1)
                pool.wait_ge(sem("w_mm"), START + 2 * i)
                pool.wait_ge(sem("tkb"), START + i + 1)
                nc.gpsimd.tensor_tensor(kg[:], tkb[:], cast(ceG[:]), ALU.mult).then_inc(sem("kg"), 1)
                pool.wait_ge(sem("state_mm"), START + i)
                nc.gpsimd.tensor_tensor(kd[:], tk[:], cast(ceK[:]), ALU.mult).then_inc(sem("kd"), 1)
                for v in range(1, LEVELS - 1):
                    select(v)
                if not last:
                    norm(i + 1)
                select(LEVELS - 1)
                if not last:
                    front(i + 1)
                pool.wait_ge(sem("out_sumsq"), START + i + 1)
                nc.gpsimd.tensor_tensor(ro[:], so[:], half_power[:, 0:DH], ALU.pow).then_inc(sem("out_rnorm"), 1)

            norm(0)
            front(0)
            with pool.Fori(0, NC - 1) as i:
                chunk(i)
            chunk(NC - 1, last=True)

        @block.scalar
        def _(act):
            act.wait_ge(sem("ld_c"), START + 16 * 8)
            nc.scalar.activation(beta[:], ba[:, :, 0:DH], ACT.Sigmoid).then_inc(sem("beta"), 1)
            nc.scalar.activation(neg_a[:], neg_a[:], ACT.Exp).then_inc(sem("exp"), 1)
            act.wait_ge(sem("z_abs"), START + 1)
            nc.scalar.activation(ez[:], ez[:], ACT.Exp, scale=-1.0).then_inc(sem("ez"), 1)
            act.wait_ge(sem("ez"), START + 1)
            nc.scalar.activation(ez[:], ez[:], ACT.Ln, bias=1.0).then_inc(sem("ez"), 1)

            def front(f, n):
                act.wait_ge(sem(f"front{n}"), START + f + 1)
                act.wait_ge(sem("sumsq"), START + f)
                nc.scalar.activation(sq[:, n], pw("A"), ACT.Square).then_inc(sem("squares"), 1)
                act.wait_ge(sem("tr2"), START + 4 * f)
                act.wait_ge(sem("kd"), START + f)
                act.wait_ge(sem("tqd"), START + f)
                nc.scalar.copy((tq, tk)[n][:], pw("A")).then_inc(sem("turned"), 1)

            def chunk(i, last=False):
                act.wait_ge(sem("tr2"), START + 4 * i + 2)
                nc.scalar.copy(qdT[:], pw("C")).then_inc(sem("qdT"), 1)
                act.wait_ge(sem("tr2"), START + 4 * i + 3)
                nc.scalar.copy(kbT[:], pw("B")).then_inc(sem("kbT"), 1)
                act.wait_ge(sem("tr2"), START + 4 * i + 4)
                nc.scalar.copy(qT[:], pw("A")).then_inc(sem("qT"), 1)
                act.wait_ge(sem("decay"), START + i + 1)
                nc.scalar.activation(dec[:], dec[:], ACT.Exp).then_inc(sem("decay_exp"), 1)
                for h in range(2):
                    act.wait_ge(sem("T_tr"), START + 2 * i + h + 1)
                    nc.scalar.copy(Tm[:, h], pw("A", h)).then_inc(sem("T_first"), 1)
                for v in range(1, LEVELS):
                    for h in range(2):
                        act.wait_ge(sem("X_mm"), START + 12 * i + 2 * (v - 1) + h + 1)
                        nc.scalar.copy(X[:, h], pw("B", h)).then_inc(sem("X"), 1)
                    if v in (2, 3) and not last:
                        front(i + 1, v - 2)
                for h in range(2):
                    act.wait_ge(sem("w_mm"), START + 2 * i + h + 1)
                    nc.scalar.mul(nwT[:, h], pw("A", h), -1.0).then_inc(sem("w"), 1)
                for h in range(2):
                    act.wait_ge(sem("vn_mm"), START + 2 * i + h + 1)
                    nc.scalar.copy(vn[:, h], pw("B", h)).then_inc(sem("vn"), 1)
                act.wait_ge(sem("o_mm"), START + i + 1)
                nc.scalar.activation(sqo[:], pw("A"), ACT.Square).then_inc(sem("out_squares"), 1)

            front(0, 0)
            front(0, 1)
            act.wait_ge(sem("G_ready"), START + 1)
            nc.scalar.activation(eG[:], Gs[:], ACT.Exp).then_inc(sem("exps"), 1)
            nc.scalar.activation(gl[:], gl[:], ACT.Exp).then_inc(sem("exps"), 1)
            nc.scalar.activation(eK[:], eK[:], ACT.Exp).then_inc(sem("exps"), 1)
            with act.Fori(0, NC - 1) as i:
                chunk(i)
            chunk(NC - 1, last=True)

        @block.vector
        def _(dve):
            dve.wait_ge(sem("ld_c"), START + 16 * 8)
            nc.vector.tensor_tensor(z[:], ba[:, :, DH:], dtb[:].unsqueeze(1).broadcast_to([P, NC, DH]), ALU.add).then_inc(sem("z"), 1)
            dve.wait_ge(sem("z"), START + 1)
            nc.vector.tensor_scalar(ez[:], z[:], -1.0, None, ALU.mult).then_inc(sem("z"), 1)
            dve.wait_ge(sem("z"), START + 2)
            nc.vector.tensor_tensor(ez[:], ez[:], z[:], ALU.max).then_inc(sem("z_abs"), 1)
            nc.vector.tensor_scalar(z[:], z[:], 0.0, None, ALU.max).then_inc(sem("z"), 1)
            dve.wait_ge(sem("z"), START + 3)
            dve.wait_ge(sem("ez"), START + 2)
            nc.vector.tensor_tensor(z[:], z[:], ez[:], ALU.add).then_inc(sem("z"), 1)
            dve.wait_ge(sem("exp"), START + 1)
            dve.wait_ge(sem("z"), START + 4)
            nc.vector.tensor_scalar(z[:], z[:], -1.0, None, ALU.mult).then_inc(sem("z"), 1)
            dve.wait_ge(sem("z"), START + 5)
            nc.vector.tensor_tensor(gg[:], z[:], neg_a[:].unsqueeze(1).broadcast_to([P, NC, DH]), ALU.mult).then_inc(sem("g"), 1)

            def factors(f):
                dve.wait_ge(sem("decayed"), START + f)
                dve.wait_ge(sem("kg"), START + f)
                dve.wait_ge(sem("kd"), START + f)
                dve.wait_ge(sem("rowG"), START + f)
                dve.wait_ge(sem("decay_step"), START + 2 * f)
                for d, s in ((cbeta, beta), (ceG, eG), (ceK, eK), (cgl, gl), (cG, Gs)):
                    nc.vector.tensor_copy(d[:], s[:, bass.ds(f, 1), :].rearrange("p a b -> p (a b)"))
                nc.vector.tensor_copy(gB[:].rearrange("p a b t -> p (a b) t"),
                                      gg[:, bass.ds(f, 1), :].rearrange("p a b -> p (a b)").unsqueeze(2).broadcast_to([P, DH, P])).then_inc(sem("chunk_factors"), 1)

            def sums(f):
                dve.wait_ge(sem("squares"), START + 2 * f + 2)
                dve.wait_ge(sem("rnorm"), START + f)
                nc.vector.tensor_reduce(ss[:], sq[:].rearrange("p n a b t -> p (n a b) t"), AX.X, ALU.add).then_inc(sem("ss_raw"), 1)
                dve.wait_ge(sem("ss_raw"), START + 3 * f + 1)
                nc.vector.tensor_scalar(ss[:, 0:DH], ss[:, 0:DH], 1e-6, float(DD), ALU.add, ALU.mult).then_inc(sem("ss_raw"), 1)
                nc.vector.tensor_scalar(ss[:, DH:], ss[:, DH:], 1e-6, None, ALU.add).then_inc(sem("ss_raw"), 1)
                dve.wait_ge(sem("ss_raw"), START + 3 * f + 3)
                dve.sem_inc(sem("sumsq"), 1)

            def scale(f):
                dve.wait_ge(sem("rnorm"), START + f + 1)
                dve.wait_ge(sem("turned"), START + 2 * f + 2)
                nc.vector.tensor_tensor(tk[:], tk[:], cast(rn[:, DH:]), ALU.mult).then_inc(sem("tk"), 1)
                nc.vector.tensor_tensor(tq[:], tq[:], cast(rn[:, 0:DH]), ALU.mult).then_inc(sem("tq"), 1)

            def values(f):
                dve.wait_ge(sem("front2"), START + f + 1)
                dve.wait_ge(sem("chunk_factors"), START + f + 1)
                dve.wait_ge(sem("vn_mm"), START + 2 * f)
                nc.vector.tensor_tensor(vb[:], pw("C"), cast(cbeta[:]), ALU.mult).then_inc(sem("vb"), 1)

            def leave(i):
                dve.wait_ge(sem("ld_gate"), START + 16 * i + 16)
                for h in range(2):
                    dve.wait_ge(sem("on_tr"), START + 2 * i + h + 1)
                    nc.vector.scalar_tensor_tensor(ybT[:, h * HH:(h + 1) * HH, bass.ds(i * C, C)], pw("D", h), gain[:, 0:1],
                                                   gate[:, h * HH:(h + 1) * HH, :], ALU.mult, ALU.mult).then_inc(sem("y_out"), 1)

            def begin(i):
                dve.wait_ge(sem("rowG"), START + i + 1)
                dve.wait_ge(sem("qk"), START + i)
                nc.vector.tensor_tensor(dec[:], pw("C"), cast(cG[:]), ALU.subtract).then_inc(sem("decay_step"), 1)
                dve.wait_ge(sem("tr2"), START + 4 * i + 1)
                nc.vector.tensor_copy(kT[:], pw("B")).then_inc(sem("kT"), 1)

            def chunk(i, first=False, last=False):
                dve.wait_ge(sem("decay_step"), START + 2 * i + 1)
                d6 = dec[:].rearrange("p a b t -> p (a b) t")
                nc.vector.tensor_tensor(d6, d6, later[:].unsqueeze(1).broadcast_to([P, DH, P]), ALU.add).then_inc(sem("decay_step"), 1)
                dve.wait_ge(sem("decay_step"), START + 2 * i + 2)
                dve.sem_inc(sem("decay"), 1)
                if not first:
                    leave(i - 1)
                dve.wait_ge(sem("decay_exp"), START + i + 1)
                dve.wait_ge(sem("kk_mm"), START + 2 * i + 1)
                for h in range(2):
                    nc.vector.tensor_tensor(MT[:, h], pw("A", h), dec[:, h], ALU.mult).then_inc(sem("M"), 1)
                for h in range(2):
                    dve.wait_ge(sem("M"), START + 2 * i + h + 1)
                    nc.vector.tensor_tensor(TT_[:, h], MT[:, h], heads(level[:, 0, :], h), ALU.mult).then_inc(sem("T0"), 1)
                for h in range(2):
                    dve.wait_ge(sem("T0"), START + 4 * i + h + 1)
                    nc.vector.tensor_tensor(TT_[:, h], heads(ident[:], h), TT_[:, h], ALU.subtract).then_inc(sem("T0"), 1)
                dve.wait_ge(sem("kk_mm"), START + 2 * i + 2)
                nc.vector.tensor_tensor(qk[:], pw("D"), dec[:], ALU.mult).then_inc(sem("qk"), 1)
                for v in range(1, LEVELS):
                    for h in range(2):
                        dve.wait_ge(sem("TX_mm"), START + 12 * i + 2 * (v - 1) + h + 1)
                        if v < LEVELS - 1:
                            nc.vector.tensor_tensor(Tm[:, h], Tm[:, h], pw("C", h), ALU.subtract).then_inc(sem("T"), 1)
                        nc.vector.tensor_tensor(TT_[:, h], TT_[:, h], pw("D", h), ALU.subtract).then_inc(sem("TT"), 1)
                    if not last:
                        if v == 1:
                            factors(i + 1)
                        elif v == 3:
                            sums(i + 1)
                        elif v == 5:
                            scale(i + 1)
                if not last:
                    values(i + 1)
                dve.wait_ge(sem("decayed"), START + i + 1)
                dve.wait_ge(sem("state_mm"), START + i + 1)
                nc.vector.tensor_tensor(S[:], S2[:], pw("D"), ALU.add).then_inc(sem("state"), 1)
                dve.wait_ge(sem("out_squares"), START + i + 1)
                dve.wait_ge(sem("out_rnorm"), START + i)
                nc.vector.tensor_reduce(so[:], sqo[:].rearrange("p a b t -> p (a b) t"), AX.X, ALU.add).then_inc(sem("so_raw"), 1)
                dve.wait_ge(sem("so_raw"), START + 2 * i + 1)
                nc.vector.tensor_scalar(so[:], so[:], 1.0 / DD, 1e-6, ALU.mult, ALU.add).then_inc(sem("so_raw"), 1)
                dve.wait_ge(sem("so_raw"), START + 2 * i + 2)
                dve.sem_inc(sem("out_sumsq"), 1)
                if not last:
                    begin(i + 1)
                dve.wait_ge(sem("out_rnorm"), START + i + 1)
                nc.vector.tensor_tensor(on[:], pw("A"), cast(ro[:]), ALU.mult).then_inc(sem("on"), 1)

            sums(0)
            dve.wait_ge(sem("G_mm"), START + 2)
            G2 = NC * DH
            nc.vector.tensor_copy(Gs[:].rearrange("p a b -> p (a b)"), ps["B"][:, 0, 0:G2])
            nc.vector.tensor_copy(gl[:].rearrange("p a b -> p (a b)"), ps["D"][:, 0, 0:G2]).then_inc(sem("g_copied"), 1)
            dve.wait_ge(sem("g_copied"), START + 1)
            nc.vector.tensor_tensor(eK[:], gl[:], Gs[:], ALU.subtract).then_inc(sem("G_ready"), 1)
            dve.wait_ge(sem("exps"), START + 3)
            dve.wait_ge(sem("beta"), START + 1)
            factors(0)
            scale(0)
            values(0)
            begin(0)
            chunk(0, first=True)
            with dve.Fori(1, NC - 1) as i:
                chunk(i)
            chunk(NC - 1, last=True)
            leave(NC - 1)

        @block.tensor
        def _(pe):

            def front(f, n, name):
                pe.wait_ge(sem(f"ld_raw{n}"), START + 16 * f + 16)
                if n == 0:
                    pe.wait_ge(sem("T_first"), START + 2 * f)
                elif n == 1:
                    pe.wait_ge(sem("turned"), START + 2 * f + 1)
                for h in range(DH):
                    ins = nc.tensor.transpose(at(pw(name), h), raw[n][:, h, :], ident[:])
                ins.then_inc(sem(f"front{n}"), 1)

            def leave(i):
                pe.wait_ge(sem("on"), START + i + 1)
                pe.wait_ge(sem("state"), START + i + 1)
                for h in range(2):
                    for a in range(HH):
                        ins = nc.tensor.transpose(pw("D", h)[:, a], on[:, h, a, :], ident[:])
                    ins.then_inc(sem("on_tr"), 1)

            def chunk(i, first=False, last=False):
                def turn(name, src, ready):
                    pe.wait_ge(sem(ready), START + i + 1)
                    for h in range(DH):
                        ins = nc.tensor.transpose(at(pw(name), h), at(src, h), ident[:])
                    ins.then_inc(sem("tr2"), 1)

                pe.wait_ge(sem("vb"), START + i + 1)
                for h in range(DH):
                    ins = nc.tensor.matmul(at(pw("C"), h), at(gB, h), upto[:], start=True, stop=True)
                ins.then_inc(sem("rowG"), 1)
                turn("B", tk, "tk")
                pe.wait_ge(sem("decay_step"), START + 2 * i + 1)
                turn("C", tqd, "tqd")
                pe.wait_ge(sem("kT"), START + i + 1)
                turn("B", tkb, "tkb")
                if not first:
                    pe.wait_ge(sem("on"), START + i)
                turn("A", tq, "tq")
                if not first:
                    leave(i - 1)
                pe.wait_ge(sem("kbT"), START + i + 1)
                pe.wait_ge(sem("qT"), START + i + 1)
                for name, src in (("A", kbT), ("D", qT)):
                    if name == "D" and not first:
                        pe.wait_ge(sem("y_out"), START + 2 * i)
                    for h in range(DH):
                        ins = nc.tensor.matmul(at(pw(name), h), at(kT, h), at(src, h), start=True, stop=True)
                    ins.then_inc(sem("kk_mm"), 1)
                for h in range(2):
                    pe.wait_ge(sem("T0"), START + 4 * i + 3 + h)
                    for a in range(HH):
                        ins = nc.tensor.transpose(pw("A", h)[:, a], TT_[:, h, a, :], ident[:])
                    ins.then_inc(sem("T_tr"), 1)
                pe.wait_ge(sem("qk"), START + i + 1)
                pe.wait_ge(sem("qdT"), START + i + 1)
                for v in range(1, LEVELS):
                    for h in range(2):
                        pe.wait_ge(sem("LT"), START + 12 * i + 2 * (v - 1) + h + 1)
                        if v == 1:
                            pe.wait_ge(sem("T_first"), START + 2 * i + h + 1)
                        else:
                            pe.wait_ge(sem("T"), START + 10 * i + 2 * (v - 2) + h + 1)
                            pe.wait_ge(sem("TT"), START + 12 * i + 2 * (v - 2) + h + 1)
                        for a in range(HH):
                            ins = nc.tensor.matmul(pw("B", h)[:, a], LT[v % 2][:, h, a, :], Tm[:, h, a, :], start=True, stop=True)
                        ins.then_inc(sem("X_mm"), 1)
                    for h in range(2):
                        pe.wait_ge(sem("X"), START + 12 * i + 2 * (v - 1) + h + 1)
                        for a in range(HH):
                            if v < LEVELS - 1:
                                nc.tensor.matmul(pw("C", h)[:, a], TT_[:, h, a, :], X[:, h, a, :], start=True, stop=True)
                            ins = nc.tensor.matmul(pw("D", h)[:, a], X[:, h, a, :], TT_[:, h, a, :], start=True, stop=True)
                        ins.then_inc(sem("TX_mm"), 1)
                    if v in (1, 2) and not last:
                        front(i + 1, v - 1, "A")
                if not last:
                    pe.wait_ge(sem("turned"), START + 2 * i + 4)
                for h in range(2):
                    pe.wait_ge(sem("TT"), START + 12 * i + 2 * (LEVELS - 2) + h + 1)
                    pe.wait_ge(sem("kg"), START + i + 1)
                    for a in range(HH):
                        ins = nc.tensor.matmul(pw("A", h)[:, a], kg[:, h, a, :], TT_[:, h, a, :], start=True, stop=True)
                    ins.then_inc(sem("w_mm"), 1)
                pe.wait_ge(sem("state"), START + i)
                for h in range(2):
                    pe.wait_ge(sem("w"), START + 2 * i + h + 1)
                    for a in range(HH):
                        nc.tensor.matmul(pw("B", h)[:, a], TT_[:, h, a, :], vb[:, h, a, :], start=True, stop=False)
                        ins = nc.tensor.matmul(pw("B", h)[:, a], nwT[:, h, a, :], S[:, h, a, :], start=False, stop=True)
                    ins.then_inc(sem("vn_mm"), 1)
                if not last:
                    front(i + 1, 2, "C")
                for h in range(2):
                    pe.wait_ge(sem("vn"), START + 2 * i + h + 1)
                    for a in range(HH):
                        nc.tensor.matmul(pw("A", h)[:, a], qdT[:, h, a, :], S[:, h, a, :], start=True, stop=False)
                        ins = nc.tensor.matmul(pw("A", h)[:, a], qk[:, h, a, :], vn[:, h, a, :], start=False, stop=True)
                ins.then_inc(sem("o_mm"), 1)
                pe.wait_ge(sem("kd"), START + i + 1)
                for h in range(DH):
                    ins = nc.tensor.matmul(at(pw("D"), h), at(kd, h), at(vn, h), start=True, stop=True)
                ins.then_inc(sem("state_mm"), 1)

            pe.wait_ge(sem("ld_c"), START + 16 * 8)
            for n, name in enumerate("AAC"):
                front(0, n, name)
            pe.wait_ge(sem("g"), START + 1)
            pe.wait_ge(sem("ones"), START + 3)
            gf = gg[:].rearrange("p a b -> p (a b)")
            nc.tensor.matmul(ps["B"][:, 0, 0:NC * DH], upto[:], gf, start=True, stop=True).then_inc(sem("G_mm"), 1)
            nc.tensor.matmul(ps["D"][:, 0, 0:NC * DH], ones[:], gf, start=True, stop=True).then_inc(sem("G_mm"), 1)
            pe.wait_ge(sem("g_copied"), START + 1)
            chunk(0, first=True)
            with pe.Fori(1, NC - 1) as i:
                chunk(i)
            chunk(NC - 1, last=True)
            leave(NC - 1)


def float32r_products(wh, wl, xh, xl):
    return ((wh, xh), (wh, xl), (wl, xh))


def stage_merge(nc, g):
    NK = 2 * AT
    with ExitStack() as ctx:
        def sb(name, shape, dt=F32):
            return ctx.enter_context(nc.sbuf_tensor(name, shape, dt))

        sem = ctx.enter_context(stage_semaphores(nc, "m",
            "y_lo ld_y0 ld_y1 ld_y2 ld_y3 ld_w0 ld_w1 ld_g0 ld_g1 w_lo gated y_hi w_hi mm ps_read"))

        NRAW = 4
        yraw = [sb(f"m_yraw{u}", [P, T]) for u in range(NRAW)]
        yh_rest, yl_rest = sb("m_yh", [P, NK - KD, T], F32R), sb("m_yl", [P, NK - KD, T], F32R)
        yh = [g.x1h[:, k, :] if k < KD else yh_rest[:, k - KD, :] for k in range(NK)]
        yl = [g.x1l[:, k, :] if k < KD else yl_rest[:, k - KD, :] for k in range(NK)]
        wraw = [sb(f"m_wraw{u}", [P, NK, P]) for u in range(2)]
        wh = [sb(f"m_wh{u}", [P, NK, P], F32R) for u in range(2)]
        wl = [sb(f"m_wl{u}", [P, NK, P], F32R) for u in range(2)]
        gates = [sb(f"m_gates{u}", [P, 2, T]) for u in range(2)]
        ps = [[ctx.enter_context(nc.psum_tensor(f"m_ps{u}{b}", [P, T], F32)) for b in range(2)] for u in range(2)]
        block = ctx.enter_context(nc.Block())

        @block.sync
        def _(sp):
            for k in range(NK):
                if k >= NRAW:
                    sp.wait_ge(sem("y_lo"), START + k - NRAW + 1)
                sp.dma_start(yraw[k % NRAW][:], g.y[k]).then_inc(sem(f"ld_y{k % NRAW}"), 16)
                if k < 2:
                    sp.dma_start(wraw[k][:], g.w_branch[k]).then_inc(sem(f"ld_w{k}"), 16)
                    for b in range(2):
                        sp.dma_start(gates[k][:, b, :], g.hT[N_IN - N_BR + b * KD + k]).then_inc(sem(f"ld_g{k}"), 16)
            with sp.Fori(0, KD // 2 - 1) as i:
                for u in range(2):
                    sp.wait_ge(sem("w_lo"), START + 2 * i + (u + 1))
                    sp.dma_start(wraw[u][:], g.w_branch[bass.ds(2 * i + (2 + u), 1)].rearrange("o p k c -> (o p) k c")).then_inc(sem(f"ld_w{u}"), 16)
                    sp.wait_ge(sem("gated"), START + 4 * i + (2 * u + 2))
                    for b in range(2):
                        sp.dma_start(gates[u][:, b, :], g.hT[bass.ds(2 * i + (N_IN - N_BR + b * KD + 2 + u), 1)].rearrange("o p t -> (o p) t")).then_inc(sem(f"ld_g{u}"), 16)

        @block.scalar
        def _(act):
            for k in range(NK):
                act.wait_ge(sem(f"ld_y{k % NRAW}"), START + 16 * (k // NRAW + 1))
                nc.scalar.copy(yh[k], yraw[k % NRAW][:]).then_inc(sem("y_hi"), 1)
                if k < 2:
                    act.wait_ge(sem(f"ld_w{k}"), START + 16)
                    nc.scalar.copy(wh[k][:], wraw[k][:]).then_inc(sem("w_hi"), 1)
            with act.Fori(0, KD // 2 - 1) as i:
                for u in range(2):
                    act.wait_ge(sem("mm"), START + 2 * i + (u + 1))
                    act.wait_ge(sem(f"ld_w{u}"), START + 16 * i + 32)
                    nc.scalar.copy(wh[u][:], wraw[u][:]).then_inc(sem("w_hi"), 1)

        @block.vector
        def _(dve):
            for k in range(NK):
                dve.wait_ge(sem("y_hi"), START + k + 1)
                nc.vector.tensor_tensor(yl[k], yraw[k % NRAW][:], yh[k].bitcast(F32), ALU.subtract).then_inc(sem("y_lo"), 1)
                if k < 2:
                    dve.wait_ge(sem("w_hi"), START + k + 1)
                    nc.vector.tensor_tensor(wl[k][:], wraw[k][:], wh[k][:].bitcast(F32), ALU.subtract).then_inc(sem("w_lo"), 1)

            def body(i, last=False):
                for u in range(2):
                    dve.wait_ge(sem("mm"), START + 2 * i + (u + 1))
                    if not last:
                        dve.wait_ge(sem("w_hi"), START + 2 * i + (u + 3))
                        nc.vector.tensor_tensor(wl[u][:], wraw[u][:], wh[u][:].bitcast(F32), ALU.subtract).then_inc(sem("w_lo"), 1)
                    dve.wait_ge(sem(f"ld_g{u}"), START + 32 * i + 32)
                    for b in range(2):
                        nc.vector.tensor_tensor(gates[u][:, b, :], gates[u][:, b, :], ps[u][b][:], ALU.mult).then_inc(sem("ps_read"), 1)
                    dve.wait_ge(sem("ps_read"), START + 4 * i + (2 * u + 2))
                    nc.vector.tensor_tensor(g.merged[:, bass.ds(2 * i + u, 1), :].rearrange("p o t -> p (o t)"),
                                            gates[u][:, 0, :], gates[u][:, 1, :], ALU.add).then_inc(sem("gated"), 2)

            with dve.Fori(0, KD // 2 - 1) as i:
                body(i)
            body(KD // 2 - 1, last=True)

        @block.tensor
        def _(pe):
            with pe.Fori(0, KD // 2) as i:
                for u in range(2):
                    pe.wait_ge(sem("w_lo"), START + 2 * i + (u + 1))
                    pe.wait_ge(sem("ps_read"), START + 4 * i + (2 * u - 2))
                    for b in range(2):
                        for k in range(AT):
                            if u == 0:
                                pe.wait_ge(sem("y_lo"), START + b * AT + k + 1)
                            for h in range(2):
                                for n, (a, x) in enumerate(float32r_products(wh, wl, yh, yl)):
                                    ins = nc.tensor.matmul(ps[u][b][:, h * HALF:(h + 1) * HALF], a[u][:, b * AT + k, :],
                                                           x[b * AT + k][:, h * HALF:(h + 1) * HALF],
                                                           start=(k == 0 and n == 0), stop=(k == AT - 1 and n == 2))
                    ins.then_inc(sem("mm"), 1)


def stage_out_norm(nc, g):
    with ExitStack() as ctx:
        def sb(name, shape, dt=F32):
            return ctx.enter_context(nc.sbuf_tensor(name, shape, dt))

        sem = ctx.enter_context(stage_semaphores(nc, "o",
            "ld_w0 ld_w1 ld_x w_lo ld_c x1 st_x10 st_x11 z power var normed rstd scaled mm m_hi turned x_hi "
            "w_hi m_lo stats passed aggr x_lo"))

        wraw = [sb(f"o_wraw{u}", [P, D]) for u in range(2)]
        wh, wl = sb("o_wh", [P, KD, D], F32R), sb("o_wl", [P, KD, D], F32R)
        mh = [sb(f"o_mh{u}", [P, KD, P], F32R) for u in range(2)]
        ml = [sb(f"o_ml{u}", [P, KD, P], F32R) for u in range(2)]
        x, z = sb("o_x", [P, D]), [sb(f"o_z{u}", [P, D]) for u in range(2)]
        gain, bias, ident = sb("o_gain", [P, D]), sb("o_bias", [P, D]), sb("o_ident", [P, P])
        stats, mv, rstd, power = sb("o_stats", [P, 2, 6]), sb("o_mv", [P, 2]), sb("o_rstd", [P, 1]), sb("o_power", [P, 1])
        ps = [ctx.enter_context(nc.psum_tensor(f"o_ps{u}", [P, D], F32)) for u in range(2)]
        psT = ctx.enter_context(nc.psum_tensor("o_psT", [P, D], F32))
        block = ctx.enter_context(nc.Block())

        @block.sync
        def _(sp):
            sp.dma_start(wraw[0][:], g.w_out[0:P, :]).then_inc(sem("ld_w0"), 16)
            sp.dma_start(wraw[1][:], g.w_out[P:2 * P, :]).then_inc(sem("ld_w1"), 16)
            sp.dma_start(x[:], g.x[0:P, :]).then_inc(sem("ld_x"), 16)
            for k in range(2, KD):
                sp.wait_ge(sem("w_lo"), START + k - 1)
                sp.dma_start(wraw[k % 2][:], g.w_out[k * P:(k + 1) * P, :]).then_inc(sem(f"ld_w{k % 2}"), 16)
            for d, s in ((gain, g.ln1_gain.partition_broadcast(P)), (bias, g.ln1_bias.partition_broadcast(P)), (ident, g.ident)):
                sp.dma_start(d[:], s).then_inc(sem("ld_c"), 16)

            def store(c, u):
                sp.wait_ge(sem("x1"), START + c + 1)
                sp.dma_start(g.x1[bass.ds(c * P, P), :], z[u][:]).then_inc(sem(f"st_x1{u}"), 16)

            with sp.Fori(0, TT // 2 - 1) as i:
                for u in range(2):
                    sp.wait_ge(sem("z"), START + 2 * i + (u + 1))
                    sp.dma_start(x[:], g.x[bass.ds(2 * i * P + (u + 1) * P, P), :]).then_inc(sem("ld_x"), 16)
                    store(2 * i + u, u)
            sp.wait_ge(sem("z"), START + TT - 1)
            sp.dma_start(x[:], g.x[(TT - 1) * P:TT * P, :]).then_inc(sem("ld_x"), 16)
            for u in range(2):
                store(TT - 2 + u, u)
            for u in range(2):
                sp.wait_ge(sem(f"st_x1{u}"), START + 16 * (TT // 2))

        @block.gpsimd
        def _(pool):
            nc.gpsimd.memset(power[:], -0.5).then_inc(sem("power"), 1)
            pool.wait_ge(sem("ld_c"), START + 48)
            pool.wait_ge(sem("power"), START + 1)
            with pool.Fori(0, TT // 2) as i:
                for u in range(2):
                    pool.wait_ge(sem("var"), START + 2 * i + (u + 1))
                    pool.wait_ge(sem("normed"), START + 2 * i + u)
                    nc.gpsimd.tensor_tensor(rstd[:], mv[:, 1:2], power[:], ALU.pow).then_inc(sem("rstd"), 1)
                    pool.wait_ge(sem("normed"), START + 2 * i + (u + 1))
                    nc.gpsimd.tensor_tensor(z[u][:], z[u][:], gain[:], ALU.mult).then_inc(sem("scaled"), 1)
                    pool.wait_ge(sem("scaled"), START + 2 * i + (u + 1))
                    nc.gpsimd.tensor_tensor(z[u][:], z[u][:], bias[:], ALU.add).then_inc(sem("x1"), 1)

        @block.scalar
        def _(act):
            def high(c, u):
                act.wait_ge(sem("mm"), START + c - 1)
                nc.scalar.copy(mh[u][:], g.merged[:, :, bass.ds(c * P, P)]).then_inc(sem("m_hi"), 1)

            def keep(c):
                act.wait_ge(sem("turned"), START + c + 1)
                nc.scalar.copy(g.x1h[:, :, bass.ds(c * P, P)], psT[:].rearrange("p (k t) -> p k t", t=P)).then_inc(sem("x_hi"), 1)

            for u in range(2):
                nc.scalar.copy(mh[u][:], g.merged[:, :, u * P:(u + 1) * P]).then_inc(sem("m_hi"), 1)
            for k in range(KD):
                act.wait_ge(sem(f"ld_w{k % 2}"), START + 16 * (k // 2 + 1))
                nc.scalar.copy(wh[:, k, :], wraw[k % 2][:]).then_inc(sem("w_hi"), 1)

            with act.Fori(1, TT // 2) as i:
                for u in range(2):
                    high(2 * i + u, u)
                    keep(2 * i + (u - 2))
            keep(TT - 2)
            keep(TT - 1)

        @block.vector
        def _(dve):
            def low(c, u):
                dve.wait_ge(sem("m_hi"), START + c + 1)
                nc.vector.tensor_tensor(ml[u][:], g.merged[:, :, bass.ds(c * P, P)], mh[u][:].bitcast(F32), ALU.subtract).then_inc(sem("m_lo"), 1)

            def norm(c, u):
                dve.wait_ge(sem("ld_x"), START + 16 * c + 16)
                dve.wait_ge(sem("mm"), START + c + 1)
                nc.vector.scalar_tensor_tensor(z[u][:], x[:], ALPHA, ps[u][:], ALU.mult, ALU.add).then_inc(sem("z"), 1)
                dve.wait_ge(sem("z"), START + c + 1)
                dve.wait_ge(sem("normed"), START + c)
                for h in range(2):
                    ins = nc.vector.bn_stats(stats[:, h, :], z[u][:, h * HALF:(h + 1) * HALF])
                ins.then_inc(sem("stats"), 1)
                wait_alone(dve, sem("stats"), START + c + 1, sem("passed"))
                nc.vector.bn_aggr(mv[:], stats[:]).then_inc(sem("aggr"), 1)
                dve.wait_ge(sem("aggr"), START + c + 1)
                nc.vector.tensor_scalar(mv[:, 1:2], mv[:, 1:2], 1e-5, None, ALU.add).then_inc(sem("var"), 1)
                dve.wait_ge(sem("rstd"), START + c + 1)
                nc.vector.tensor_scalar(z[u][:], z[u][:], mv[:, 0:1], rstd[:, 0:1], ALU.subtract, ALU.mult).then_inc(sem("normed"), 1)

            def keep(c):
                dve.wait_ge(sem("x_hi"), START + c + 1)
                nc.vector.tensor_tensor(g.x1l[:, :, bass.ds(c * P, P)], psT[:].rearrange("p (k t) -> p k t", t=P),
                                        g.x1h[:, :, bass.ds(c * P, P)].bitcast(F32), ALU.subtract).then_inc(sem("x_lo"), 1)

            def free(c, u):
                dve.wait_ge(sem(f"st_x1{u}"), START + 8 * (c - u))
                dve.wait_ge(sem("turned"), START + c - 1)

            for u in range(2):
                low(u, u)
            for k in range(KD):
                dve.wait_ge(sem("w_hi"), START + k + 1)
                nc.vector.tensor_tensor(wl[:, k, :], wraw[k % 2][:], wh[:, k, :].bitcast(F32), ALU.subtract).then_inc(sem("w_lo"), 1)
            norm(0, 0)

            low(2, 0)
            norm(1, 1)
            low(3, 1)
            keep(0)
            free(2, 0)
            norm(2, 0)
            with dve.Fori(2, TT // 2) as i:
                for u in range(2):
                    c = 2 * i + u
                    low(c, u)
                    keep(c - 3)
                    free(c - 1, 1 - u)
                    norm(c - 1, 1 - u)
            keep(TT - 3)
            free(TT - 1, 1)
            norm(TT - 1, 1)
            keep(TT - 2)
            keep(TT - 1)

        @block.tensor
        def _(pe):
            def products(c, u, first=False):
                pe.wait_ge(sem("m_lo"), START + c + 1)
                if not first:
                    pe.wait_ge(sem("z"), START + c - 1)
                for k in range(KD):
                    if first:
                        pe.wait_ge(sem("w_lo"), START + k + 1)
                    for h in range(2):
                        for n, (a, b) in enumerate(float32r_products(mh, ml, wh, wl)):
                            ins = nc.tensor.matmul(ps[u][:, h * HALF:(h + 1) * HALF], a[u][:, k, :], b[:, k, h * HALF:(h + 1) * HALF],
                                                   start=(k == 0 and n == 0), stop=(k == KD - 1 and n == 2))
                ins.then_inc(sem("mm"), 1)

            def turn(c, u, first=False):
                pe.wait_ge(sem("x1"), START + c + 1)
                if not first:
                    pe.wait_ge(sem("x_lo"), START + c)
                for k in range(KD):
                    ins = nc.tensor.transpose(psT[:, k * P:(k + 1) * P], z[u][:, k * P:(k + 1) * P], ident[:])
                ins.then_inc(sem("turned"), 1)

            products(0, 0, first=True)
            products(1, 1, first=True)
            pe.wait_ge(sem("ld_c"), START + 48)
            turn(0, 0, first=True)
            products(2, 0)
            turn(1, 1)
            products(3, 1)
            turn(2, 0)
            with pe.Fori(2, TT // 2) as i:
                products(2 * i, 0)
                turn(2 * i - 1, 1)
                products(2 * i + 1, 1)
                turn(2 * i, 0)
            turn(TT - 1, 1)


def stage_scores(nc, g):
    N = 2 * PH
    with ExitStack() as ctx:
        def sb(name, shape, dt=F32):
            return ctx.enter_context(nc.sbuf_tensor(name, shape, dt))

        sem = ctx.enter_context(stage_semaphores(nc, "s",
            "ld_w0 ld_w1 ld_k s_out st_s0 st_s1 w_lo w_hi mm s_mm q"))

        xh, xl = g.x1h, g.x1l
        wraw = [sb(f"s_wraw{u}", [P, KD, P]) for u in range(2)]
        wh = [sb(f"s_wh{u}", [P, KD, P], F32R) for u in range(2)]
        wl = [sb(f"s_wl{u}", [P, KD, P], F32R) for u in range(2)]
        keys = sb("s_keys", [P, N, PK])
        q = [sb(f"s_q{u}", [P, T]) for u in range(2)]
        sout = [sb(f"s_out{u}", [P, TT, PK]) for u in range(2)]
        psq = [ctx.enter_context(nc.psum_tensor(f"s_psq{u}", [P, T], F32)) for u in range(2)]
        pss = [ctx.enter_context(nc.psum_tensor(f"s_pss{u}", [P, T], F32)) for u in range(2)]
        block = ctx.enter_context(nc.Block())

        @block.sync
        def _(sp):
            for k in range(2):
                sp.dma_start(wraw[k][:], g.w_query[k]).then_inc(sem(f"ld_w{k}"), 16)
            sp.dma_start(keys[:], g.keys.rearrange("n c k -> c n k")).then_inc(sem("ld_k"), 16)

            def store(i, u):
                sp.wait_ge(sem("s_out"), START + 2 * i + (u + 1))
                sp.dma_start(g.s[:, :, bass.ds(2 * i + u, 1), :].rearrange("t p o k -> p t (o k)"), sout[u][:]).then_inc(sem(f"st_s{u}"), 16)

            with sp.Fori(0, N // 2 - 1) as i:
                for u in range(2):
                    sp.wait_ge(sem("w_lo"), START + 2 * i + (u + 1))
                    sp.dma_start(wraw[u][:], g.w_query[bass.ds(2 * i + (2 + u), 1)].rearrange("o p k c -> (o p) k c")).then_inc(sem(f"ld_w{u}"), 16)
                for u in range(2):
                    store(i, u)
            for u in range(2):
                store(N // 2 - 1, u)
            for u in range(2):
                sp.wait_ge(sem(f"st_s{u}"), START + 16 * (N // 2))

        @block.scalar
        def _(act):
            def split(u, n):
                act.wait_ge(sem(f"ld_w{u}"), START + n)
                nc.scalar.copy(wh[u][:], wraw[u][:]).then_inc(sem("w_hi"), 1)

            split(0, 16)
            split(1, 16)

            def body(i, last=False):
                for u in range(2):
                    act.wait_ge(sem("mm"), START + 2 * i + (u + 1))
                    act.wait_ge(sem("s_mm"), START + 2 * i)
                    nc.scalar.copy(q[u][:], psq[u][:]).then_inc(sem("q"), 1)
                    if not last:
                        split(u, 16 * i + 32)

            with act.Fori(0, N // 2 - 1) as i:
                body(i)
            body(N // 2 - 1, last=True)

        @block.vector
        def _(dve):
            def split(u, n):
                dve.wait_ge(sem("w_hi"), START + n)
                nc.vector.tensor_tensor(wl[u][:], wraw[u][:], wh[u][:].bitcast(F32), ALU.subtract).then_inc(sem("w_lo"), 1)

            split(0, 1)
            split(1, 2)

            def body(i, last=False):
                for u in range(2):
                    if not last:
                        split(u, 2 * i + (u + 3))
                for u in range(2):
                    dve.wait_ge(sem(f"st_s{u}"), START + 16 * i)
                    dve.wait_ge(sem("s_mm"), START + 2 * i + (u + 1))
                    nc.vector.tensor_copy(sout[u][:], pss[u][:].rearrange("p (t k) -> p t k", t=TT)).then_inc(sem("s_out"), 1)

            with dve.Fori(0, N // 2 - 1) as i:
                body(i)
            body(N // 2 - 1, last=True)

        @block.tensor
        def _(pe):

            def queries(i, u):
                pe.wait_ge(sem("w_lo"), START + 2 * i + (u + 1))
                pe.wait_ge(sem("q"), START + 2 * i + (u - 1))
                for h in range(2):
                    for k in range(KD):
                        for n, (a, b) in enumerate(float32r_products(wh, wl, xh, xl)):
                            ins = nc.tensor.matmul(psq[u][:, h * HALF:(h + 1) * HALF], a[u][:, k, :], b[:, k, h * HALF:(h + 1) * HALF],
                                                   start=(k == 0 and n == 0), stop=(k == KD - 1 and n == 2))
                ins.then_inc(sem("mm"), 1)

            def scores(i, u):
                pe.wait_ge(sem("ld_k"), START + 16)
                pe.wait_ge(sem("q"), START + 2 * i + (u + 1))
                pe.wait_ge(sem("s_out"), START + 2 * i + (u - 1))
                for t in range(TT):
                    ins = nc.tensor.matmul(pss[u][:, t * PK:(t + 1) * PK], q[u][:, t * P:(t + 1) * P],
                                           keys[:, bass.ds(2 * i + u, 1), :].rearrange("p o k -> p (o k)"), start=True, stop=True)
                ins.then_inc(sem("s_mm"), 1)

            with pe.Fori(0, N // 2) as i:
                queries(i, 0)
                queries(i, 1)
                scores(i, 0)
                scores(i, 1)


GONE = -3e38

def stage_down_and_route(nc, g):
    SLOTS = PK // TT
    GT = 8
    NG = P // GT
    PIECES = 14
    WQ = 4

    def plan(groups, own, next):
        assert sum(groups) == NG and len(groups) == SLOTS
        def spans(counts):
            counts = counts + [0] * (SLOTS - len(counts))
            return [range(sum(counts[:n]), sum(counts[:n + 1])) for n in range(SLOTS)]
        first_routed = min(n for n in range(SLOTS) if groups[n])
        return dict(groups=spans(groups), own=spans(own), next=spans(next), turn=first_routed - 1)

    FIRST = plan([0] * 6 + [2, 2, 1, 2, 1, 2, 1, 2, 2, 1], [4, 3, 3, 2, 1, 1], [0] * 5 + [2, 1, 1, 2, 1, 1, 2, 1, 1, 1, 1])
    INNER = plan([0] * 4 + [2, 1, 1] * 4, [], [1] * PIECES)
    LAST = plan([0] * 4 + [2] * 8 + [0] * 4, [], [])
    HB = 2 * NG
    with ExitStack() as ctx:
        def sb(name, shape, dt=F32):
            return ctx.enter_context(nc.sbuf_tensor(name, shape, dt))

        sem = ctx.enter_context(stage_semaphores(nc, "r",
            "ld_d0 ld_d1 ld_st ld_c st_W d_lo gelu st_a0 st_a1 st_used W d_hi shifted exp onehot turned rt "
            "d_mm w_mm gated eq picked summed pieces passed ranks zsum routed"))
        xh, xl = g.x1h, g.x1l
        draw = [sb(f"r_draw{u}", [P, KD, P]) for u in range(2)]
        dh = [sb(f"r_dh{u}", [P, KD, P], F32R) for u in range(2)]
        dl = [sb(f"r_dl{u}", [P, KD, P], F32R) for u in range(2)]
        act_out = [sb(f"r_act{u}", [P, T]) for u in range(2)]
        ident, iota = sb("r_ident", [P, P]), sb("r_iota", [P, P])
        st = sb("r_st", [P, 2 * PH, PK])
        val, idx = sb("r_val", [P, PH, 2, TOP]), sb("r_idx", [P, PH, 2, TOP], U32)
        keyf = sb("r_keyf", [P, PH, 2, TOP])
        cand = sb("r_cand", [P, PH, TOP, TOP])
        best, flat = sb("r_best", [P, PH, TOP]), sb("r_flat", [P, PH, TOP], U32)
        rank = sb("r_rank", [P, 2, PH, TOP], U32)
        rankf = sb("r_rankf", [P, 2, PH, TOP])
        zsum = sb("r_zsum", [P, PH])
        route = sb("r_route", [P, 3, PH, TOP])
        rt = sb("r_rt", [P, 3, P])
        oi = [sb(f"r_oi{u}", [P, GT, PK]) for u in range(2)]
        oj = [sb(f"r_oj{u}", [P, GT, PK]) for u in range(2)]
        W = sb("r_W", [P, PK, P])
        psd = [ctx.enter_context(nc.psum_tensor(f"r_psd{u}", [P, T], F32)) for u in range(2)]
        psw = [ctx.enter_context(nc.psum_tensor(f"r_psw{u}", [P, HALF], F32)) for u in range(2)]
        psT = ctx.enter_context(nc.psum_tensor("r_psT", [P, HALF], F32))
        block = ctx.enter_context(nc.Block())

        @block.sync
        def _(sp):
            def load_d(c, n):
                sp.dma_start(draw[n][:], g.down[bass.ds(c, 1)].rearrange("o p k e -> (o p) k e")).then_inc(sem(f"ld_d{n}"), 16)

            def load_st(t):
                sp.dma_start(st[:], g.s[bass.ds(t, 1)].rearrange("o p n k -> (o p) n k")).then_inc(sem("ld_st"), 16)

            for d, s in ((ident, g.ident), (iota, g.iota)):
                sp.dma_start(d[:], s).then_inc(sem("ld_c"), 16)
            load_st(0)
            load_d(0, 0)
            load_d(1, 1)

            def store_W(t, q):
                w = PK // WQ
                sp.dma_start(g.W[q * w:(q + 1) * w, :, bass.ds(t * P, P)].rearrange("j p t -> p j t"),
                             W[:, q * w:(q + 1) * w, :]).then_inc(sem("st_W"), 16)

            def slot(t, s, load=True):
                c, n = SLOTS * t + s, s % 2
                if load:
                    sp.wait_ge(sem("d_lo"), START + c + 1)
                    load_d(c + 2, n)
                sp.wait_ge(sem("gelu"), START + c + 1)
                sp.dma_start(g.act[bass.ds(c, 1)].rearrange("o p t -> (o p) t"), act_out[n][:]).then_inc(sem(f"st_a{n}"), 16)

            def tile(t, scores=True):
                for s in range(WQ, SLOTS + WQ):
                    slot(t, s)
                    if s == 12 and scores:
                        sp.wait_ge(sem("st_used"), START + t + 2)
                        load_st(t + 2)
                    if s >= SLOTS:
                        if s == SLOTS:
                            sp.wait_ge(sem("W"), START + HB * t + HB)
                        store_W(t, s - SLOTS)

            for s in range(WQ):
                slot(0, s)
            sp.wait_ge(sem("st_used"), START + 1)
            load_st(1)
            with sp.Fori(0, TT - 2) as t:
                tile(t)
            tile(TT - 2, scores=False)
            for s in range(WQ, SLOTS):
                slot(TT - 1, s, load=(s < SLOTS - 2))
                if s >= SLOTS - WQ:
                    sp.wait_ge(sem("W"), START + HB * TT)
                    store_W(TT - 1, s - (SLOTS - WQ))
            sp.wait_ge(sem("st_W"), START + 16 * WQ * TT)
            for n in range(2):
                sp.wait_ge(sem(f"st_a{n}"), START + 16 * PK // 2)

        @block.scalar
        def _(act):
            def split_d(c, n, count):
                act.wait_ge(sem(f"ld_d{n}"), START + count)
                nc.scalar.copy(dh[n][:], draw[n][:]).then_inc(sem("d_hi"), 1)

            def topk_exp(t):
                act.wait_ge(sem("shifted"), START + t + 1)
                nc.scalar.activation(route[:, 2], route[:, 2], ACT.Exp).then_inc(sem("exp"), 1)

            def topk_turn(t):
                act.wait_ge(sem("onehot"), START + NG * t)
                act.wait_ge(sem("turned"), START + t + 1)
                nc.scalar.copy(rt[:], psT[:, 0:3 * P].rearrange("p (c t) -> p c t", t=P)).then_inc(sem("rt"), 1)

            split_d(0, 0, 16)
            split_d(1, 1, 16)

            def tile(t, kind):
                for s in range(SLOTS):
                    c, n = SLOTS * t + s, s % 2
                    act.wait_ge(sem("d_mm"), START + c + 1)
                    if kind is not FIRST or s >= 2:
                        act.wait_ge(sem(f"st_a{n}"), START + 16 * (SLOTS // 2) * t + 16 * (s // 2))
                    nc.scalar.activation(act_out[n][:], psd[n][:], ACT.Gelu).then_inc(sem("gelu"), 1)
                    for m in kind["groups"][s]:
                        if m == 0 and kind is not FIRST:
                            act.wait_ge(sem("st_W"), START + 16 * WQ * t)
                        for b in range(2):
                            act.wait_ge(sem("w_mm"), START + HB * t + (2 * m + b + 1))
                            nc.scalar.copy(W[:, :, m * GT + 4 * b:m * GT + 4 * b + 4].rearrange("p j t -> p t j"),
                                           psw[b][:].rearrange("p (t j) -> p t j", j=PK)).then_inc(sem("W"), 1)
                    if not (kind is LAST and s >= SLOTS - 2):
                        split_d(c + 2, n, 16 * (SLOTS // 2) * t + 16 * (s // 2) + 32)
                    if EXP in kind["own"][s]:
                        topk_exp(t)
                    if EXP in kind["next"][s]:
                        topk_exp(t + 1)
                    if s == kind["turn"]:
                        topk_turn(t)

            EXP = 10
            tile(0, FIRST)
            with act.Fori(1, TT - 1) as t:
                tile(t, INNER)
            tile(TT - 1, LAST)

        @block.gpsimd
        def _(pool):
            def gate(t, m):
                u = m % 2
                pool.wait_ge(sem("onehot"), START + NG * t + (m + 1))
                nc.gpsimd.tensor_tensor(oi[u][:], oi[u][:], rt[:, 2, m * GT:(m + 1) * GT].unsqueeze(2).broadcast_to([P, GT, PK]),
                                        ALU.mult).then_inc(sem("gated"), 1)

            def tile(t, kind):
                for s in range(SLOTS):
                    for m in kind["groups"][s]:
                        gate(t, m)

            tile(0, FIRST)
            with pool.Fori(1, TT - 1) as t:
                tile(t, INNER)
            tile(TT - 1, LAST)

        @block.vector
        def _(dve):
            def split_d(c, n):
                dve.wait_ge(sem("d_hi"), START + c + 1)
                nc.vector.tensor_tensor(dl[n][:], draw[n][:], dh[n][:].bitcast(F32), ALU.subtract).then_inc(sem("d_lo"), 1)

            def topk(t, piece):
                def pick(side):
                    dve.wait_ge(sem("eq"), START + 2 * t + (side + 1))
                    nc.vector.tensor_tensor(cand[:], cand[:], keyf[:, :, side, :].unsqueeze(2).broadcast_to([P, PH, TOP, TOP]),
                                            ALU.mult).then_inc(sem("picked"), 1)
                    dve.wait_ge(sem("picked"), START + 2 * t + (side + 1))
                    nc.vector.tensor_reduce(route[:, side], cand[:], AX.X, ALU.add).then_inc(sem("summed"), 1)

                def before():
                    wait_alone(dve, sem("pieces"), START + PIECES * t + piece, sem("passed"))

                done = None
                pairs = [(h, p, 2 * h + p) for h in range(PH) for p in range(2)]
                if piece == 0:
                    wait_alone(dve, sem("ld_st"), START + 16 * t + 16, sem("passed"))
                    before()
                    for h, p, n in pairs:
                        done = nc.vector.max(val[:, h, p, 0:8], st[:, n, :])
                elif piece == 1:
                    before()
                    for h, p, n in pairs:
                        done = nc.vector.max_index(idx[:, h, p, 0:8], val[:, h, p, 0:8], st[:, n, :])
                elif piece == 2:
                    before()
                    for h, p, n in pairs:
                        done = nc.vector.match_replace(out=st[:, n, :], in_to_replace=val[:, h, p, 0:8], in_values=st[:, n, :], imm_value=GONE)
                elif piece == 3:
                    before()
                    for h, p, n in pairs:
                        done = nc.vector.max(val[:, h, p, 8:16], st[:, n, :])
                elif piece == 4:
                    before()
                    for h, p, n in pairs:
                        done = nc.vector.max_index(idx[:, h, p, 8:16], val[:, h, p, 8:16], st[:, n, :])
                elif piece == 5:
                    before()
                    dve.sem_inc(sem("st_used"), 1)
                    nc.vector.tensor_copy(keyf[:], idx[:])
                    done = nc.vector.tensor_tensor(cand[:], val[:, :, 0, :].unsqueeze(3).broadcast_to([P, PH, TOP, TOP]),
                                                   val[:, :, 1, :].unsqueeze(2).broadcast_to([P, PH, TOP, TOP]), ALU.add)
                elif piece == 6:
                    before()
                    for h in range(PH):
                        done = nc.vector.max(best[:, h, 0:8], sums[:, h])
                elif piece == 7:
                    before()
                    for h in range(PH):
                        done = nc.vector.max_index(flat[:, h, 0:8], best[:, h, 0:8], sums[:, h])
                elif piece == 8:
                    before()
                    for h in range(PH):
                        done = nc.vector.match_replace(out=sums[:, h], in_to_replace=best[:, h, 0:8], in_values=sums[:, h], imm_value=GONE)
                elif piece == 9:
                    before()
                    for h in range(PH):
                        done = nc.vector.max(best[:, h, 8:16], sums[:, h])
                elif piece == 10:
                    before()
                    for h in range(PH):
                        nc.vector.max_index(flat[:, h, 8:16], best[:, h, 8:16], sums[:, h])
                    dve.wait_ge(sem("turned"), START + t)
                    nc.vector.tensor_tensor(route[:, 2], best[:], best[:, :, 0:1].broadcast_to([P, PH, TOP]), ALU.subtract).then_inc(sem("shifted"), 1)
                    dve.wait_ge(sem("shifted"), START + t + 1)
                    dve.sem_inc(sem("pieces"), 1)
                elif piece == 11:
                    before()
                    nc.vector.tensor_scalar(rank[:, 0], flat[:], 4, None, ALU.logical_shift_right)
                    nc.vector.tensor_scalar(rank[:, 1], flat[:], 15, None, ALU.bitwise_and).then_inc(sem("ranks"), 1)
                    wait_alone(dve, sem("ranks"), START + 2 * t + 1, sem("passed"))
                    nc.vector.tensor_copy(rankf[:], rank[:]).then_inc(sem("ranks"), 1)
                    dve.wait_ge(sem("ranks"), START + 2 * t + 2)
                    nc.vector.tensor_tensor(cand[:], rankf[:, 0].unsqueeze(3).broadcast_to([P, PH, TOP, TOP]),
                                            ranks16, ALU.is_equal).then_inc(sem("eq"), 1)
                    dve.wait_ge(sem("exp"), START + t + 1)
                    nc.vector.tensor_reduce(zsum[:], route[:, 2], AX.X, ALU.add).then_inc(sem("zsum"), 1)
                    dve.wait_ge(sem("zsum"), START + 2 * t + 1)
                    nc.vector.reciprocal(zsum[:], zsum[:]).then_inc(sem("zsum"), 1)
                    dve.wait_ge(sem("zsum"), START + 2 * t + 2)
                    done = nc.vector.tensor_tensor(route[:, 2], route[:, 2], zsum[:].unsqueeze(2).broadcast_to([P, PH, TOP]), ALU.mult)
                elif piece == 12:
                    pick(0)
                    dve.wait_ge(sem("summed"), START + 2 * t + 1)
                    nc.vector.tensor_tensor(cand[:], rankf[:, 1].unsqueeze(3).broadcast_to([P, PH, TOP, TOP]),
                                            ranks16, ALU.is_equal).then_inc(sem("eq"), 1)
                    dve.sem_inc(sem("pieces"), 1)
                elif piece == 13:
                    pick(1)
                    dve.wait_ge(sem("summed"), START + 2 * t + 2)
                    before()
                    dve.sem_inc(sem("pieces"), 1)
                    dve.sem_inc(sem("routed"), 1)
                if done is not None:
                    done.then_inc(sem("pieces"), 1)

            sums = cand[:].rearrange("p h a b -> p h (a b)")
            ranks16 = iota[:, 0:TOP].unsqueeze(1).unsqueeze(1).broadcast_to([P, PH, TOP, TOP])

            split_d(0, 0)
            split_d(1, 1)
            dve.wait_ge(sem("ld_c"), START + 32)

            def tile(t, kind):
                for s in range(SLOTS):
                    c, n = SLOTS * t + s, s % 2
                    for m in kind["groups"][s]:
                        u = m % 2
                        if m == 0:
                            dve.wait_ge(sem("rt"), START + t + 1)
                        if m >= 2:
                            dve.wait_ge(sem("w_mm"), START + HB * t + 2 * (m - 1))
                        elif kind is not FIRST:
                            dve.wait_ge(sem("w_mm"), START + HB * t)
                        keys = iota[:].unsqueeze(1).broadcast_to([P, GT, PK])
                        nc.vector.tensor_tensor(oj[u][:], keys, rt[:, 1, m * GT:(m + 1) * GT].unsqueeze(2).broadcast_to([P, GT, PK]), ALU.is_equal)
                        nc.vector.tensor_tensor(oi[u][:], keys, rt[:, 0, m * GT:(m + 1) * GT].unsqueeze(2).broadcast_to([P, GT, PK]),
                                                ALU.is_equal).then_inc(sem("onehot"), 1)
                    for piece in kind["own"][s]:
                        topk(t, piece)
                    for piece in kind["next"][s]:
                        topk(t + 1, piece)
                    if not (kind is LAST and s >= SLOTS - 2):
                        split_d(c + 2, n)

            tile(0, FIRST)
            with dve.Fori(1, TT - 1) as t:
                tile(t, INNER)
            tile(TT - 1, LAST)

        @block.tensor
        def _(pe):
            def turn(t):
                pe.wait_ge(sem("routed"), START + t + 1)
                pe.wait_ge(sem("rt"), START + t)
                for c in range(3):
                    ins = nc.tensor.transpose(psT[:, c * P:(c + 1) * P], route[:, c].rearrange("p h a -> p (h a)"), ident[:])
                ins.then_inc(sem("turned"), 1)

            def tile(t, kind):
                for s in range(SLOTS):
                    c, n = SLOTS * t + s, s % 2
                    pe.wait_ge(sem("d_lo"), START + c + 1)
                    if kind is not FIRST or s >= 2:
                        pe.wait_ge(sem("gelu"), START + c - 1)
                    for h in range(2):
                        for k in range(KD):
                            for m, (a, b) in enumerate(float32r_products(dh, dl, xh, xl)):
                                ins = nc.tensor.matmul(psd[n][:, h * HALF:(h + 1) * HALF], a[n][:, k, :], b[:, k, h * HALF:(h + 1) * HALF],
                                                       start=(k == 0 and m == 0), stop=(k == KD - 1 and m == 2))
                    ins.then_inc(sem("d_mm"), 1)
                    for m in kind["groups"][s]:
                        pe.wait_ge(sem("gated"), START + NG * t + (m + 1))
                        for b in range(2):
                            if m > 0 or kind is not FIRST:
                                pe.wait_ge(sem("W"), START + (HB * t + (2 * m + b - 1) if m > 0 else HB * t))
                            for k in range(4):
                                ins = nc.tensor.matmul(psw[b][:, k * PK:(k + 1) * PK], oi[m % 2][:, 4 * b + k, :], oj[m % 2][:, 4 * b + k, :],
                                                       start=True, stop=True)
                            ins.then_inc(sem("w_mm"), 1)
                    if s == kind["turn"]:
                        turn(t)

            tile(0, FIRST)
            with pe.Fori(1, TT - 1) as t:
                tile(t, INNER)
            tile(TT - 1, LAST)


def stage_up(nc, g):
    NCH = PK
    G = 4
    NR = NCH // G
    NB = 8
    with ExitStack() as ctx:
        def sb(name, shape, dt=F32):
            return ctx.enter_context(nc.sbuf_tensor(name, shape, dt))

        sem = ctx.enter_context(stage_semaphores(nc, "e",
            "y_add rstd normed stats aggr var scaled final ld_A0 ld_A1 ld_u0 ld_u1 C_lo ld_y ld_ln st_out "
            "y_mm u_hi weighted C_hi power y_init scaled_last final_last"))
        y = sb("e_y", [P, TT, D])
        uraw = [sb(f"e_uraw{u}", [P, D]) for u in range(2)]
        araw = [sb(f"e_araw{u}", [P, T]) for u in range(2)]
        Wt = [sb(f"e_W{u}", [P, T]) for u in range(2)]
        uh = [sb(f"e_uh{u}", [P, D], F32R) for u in range(2 * G)]
        ul = [sb(f"e_ul{u}", [P, D], F32R) for u in range(2 * G)]
        Ch = [sb(f"e_Ch{u}", [P, T], F32R) for u in range(2 * G)]
        Cl = [sb(f"e_Cl{u}", [P, T], F32R) for u in range(2 * G)]
        stats, mv = [sb(f"e_stats{u}", [P, 2, 6]) for u in range(2)], [sb(f"e_mv{u}", [P, 2]) for u in range(2)]
        rstd, power = [sb(f"e_rstd{u}", [P, 1]) for u in range(2)], sb("e_power", [P, 1])
        psy = [ctx.enter_context(nc.psum_tensor(f"e_psy{u}", [P, HALF], F32)) for u in range(NB)]
        block = ctx.enter_context(nc.Block())

        def stats_of(dve, t):
            u = t % 2
            dve.wait_ge(sem("y_add"), START + 16 * (NR - 1) + 2 * t + 2)
            if t >= 2:
                dve.wait_ge(sem("rstd"), START + t - 1)
                dve.wait_ge(sem("normed"), START + t - 1)
            for h in range(2):
                ins = nc.vector.bn_stats(stats[u][:, h, :], y[:, t, h * HALF:(h + 1) * HALF])
            ins.then_inc(sem("stats"), 1)
            dve.wait_ge(sem("stats"), START + t + 1)
            nc.vector.bn_aggr(mv[u][:], stats[u][:]).then_inc(sem("aggr"), 1)
            dve.wait_ge(sem("aggr"), START + t + 1)
            nc.vector.tensor_scalar(mv[u][:, 1:2], mv[u][:, 1:2], 1e-5, None, ALU.add).then_inc(sem("var"), 1)

        def norm(dve, t):
            u = t % 2
            dve.wait_ge(sem("rstd"), START + t + 1)
            nc.vector.tensor_scalar(y[:, t, :], y[:, t, :], mv[u][:, 0:1], rstd[u][:, 0:1], ALU.subtract, ALU.mult).then_inc(sem("normed"), 1)

        def affine(engine, eng, t, done):
            scaled, n = (sem("scaled_last"), 1) if t == TT - 1 else (sem("scaled"), t + 1)
            eng.wait_ge(sem("normed"), START + t + 1)
            engine.tensor_tensor(y[:, t, :], y[:, t, :], araw[0][:], ALU.mult).then_inc(scaled, 1)
            eng.wait_ge(scaled, START + n)
            engine.tensor_tensor(y[:, t, :], y[:, t, :], araw[1][:], ALU.add).then_inc(sem(done), 1)

        @block.sync
        def _(sp):
            def load(c, n):
                for d, s, name in ((araw, g.act, "A"), (Wt, g.W, "A"), (uraw, g.up, "u")):
                    sp.dma_start(d[n][:], s[bass.ds(c, 1)].rearrange("o p k -> (o p) k")).then_inc(sem(f"ld_{name}{n}"), 16)

            load(0, 0)
            load(1, 1)

            def loads(i):
                for n in range(2):
                    sp.wait_ge(sem("C_lo"), START + 2 * i + (n + 1))
                    load(2 * i + (n + 2), n)

            loads(0)
            for t in range(TT):
                sp.dma_start(y[:, t, :], g.x1[t * P:(t + 1) * P, :]).then_inc(sem("ld_y"), 16)
            with sp.Fori(1, NCH // 2 - 1) as i:
                loads(i)
            sp.wait_ge(sem("C_lo"), START + NCH)
            for d, s in ((araw[0], g.ln2_gain), (araw[1], g.ln2_bias)):
                sp.dma_start(d[:], s.partition_broadcast(P)).then_inc(sem("ld_ln"), 16)
            for t in range(TT):
                if t < TT - 1:
                    sp.wait_ge(sem("final"), START + t + 1)
                else:
                    sp.wait_ge(sem("final_last"), START + 1)
                sp.dma_start(g.out[t * P:(t + 1) * P, :], y[:, t, :]).then_inc(sem("st_out"), 16)
            sp.wait_ge(sem("st_out"), START + 16 * TT)

        @block.scalar
        def _(act):
            def prepare(r, par, pair):
                for q in range(G):
                    c, n, s = G * r + q, q % 2, par * G + q
                    act.wait_ge(sem(f"ld_u{n}"), START + 16 * (G // 2) * r + 16 * (q // 2 + 1))
                    if q == 0 and pair is not None:
                        act.wait_ge(sem("y_mm"), START + pair)
                    nc.scalar.copy(uh[s][:], uraw[n][:]).then_inc(sem("u_hi"), 1)
                    act.wait_ge(sem("weighted"), START + c + 1)
                    nc.scalar.copy(Ch[s][:], araw[n][:]).then_inc(sem("C_hi"), 1)

            prepare(0, 0, None)
            prepare(1, 1, None)
            with act.Fori(0, NR // 2 - 1) as i:
                for par in range(2):
                    prepare(2 * i + (2 + par), par, 32 * i + 16 * (par + 1))

        @block.gpsimd
        def _(pool):
            nc.gpsimd.memset(power[:], -0.5).then_inc(sem("power"), 1)
            with pool.Fori(0, NCH // 2) as i:
                for n in range(2):
                    pool.wait_ge(sem(f"ld_A{n}"), START + 32 * i + 32)
                    nc.gpsimd.tensor_tensor(araw[n][:], araw[n][:], Wt[n][:], ALU.mult).then_inc(sem("weighted"), 1)
            pool.wait_ge(sem("power"), START + 1)
            pool.wait_ge(sem("ld_ln"), START + 32)
            for t in range(TT):
                pool.wait_ge(sem("var"), START + t + 1)
                nc.gpsimd.tensor_tensor(rstd[t % 2][:], mv[t % 2][:, 1:2], power[:], ALU.pow).then_inc(sem("rstd"), 1)
                if t >= 1:
                    affine(nc.gpsimd, pool, t - 1, "final")

        @block.vector
        def _(dve):
            def low(r, par, q):
                c, n, s = G * r + q, q % 2, par * G + q
                dve.wait_ge(sem("u_hi"), START + c + 1)
                nc.vector.tensor_tensor(ul[s][:], uraw[n][:], uh[s][:].bitcast(F32), ALU.subtract)
                dve.wait_ge(sem("C_hi"), START + c + 1)
                nc.vector.tensor_tensor(Cl[s][:], araw[n][:], Ch[s][:].bitcast(F32), ALU.subtract).then_inc(sem("C_lo"), 1)

            def add(r, b):
                dve.wait_ge(sem("y_mm"), START + 16 * r + (b + 1))
                o = y[:, b // 2, b % 2 * HALF:(b % 2 + 1) * HALF]
                nc.vector.tensor_tensor(o, o, psy[b % NB][:], ALU.add).then_inc(sem("y_add"), 1)

            for q in range(G):
                low(0, 0, q)
            for t in range(TT):
                dve.wait_ge(sem("ld_y"), START + 16 * TT)
                nc.vector.tensor_scalar(y[:, t, :], y[:, t, :], ALPHA, None, ALU.mult).then_inc(sem("y_init"), 1)
            dve.wait_ge(sem("y_init"), START + TT)
            for b in range(NB):
                add(0, b)
            for q in range(G):
                low(1, 1, q)
            for b in range(NB, 2 * TT):
                add(0, b)
            for q in range(G):
                low(2, 0, q)
            for b in range(2 * TT):
                add(1, b)
            for q in range(G):
                low(3, 1, q)
            with dve.Fori(1, NR // 2 - 1) as i:
                for par in range(2):
                    for b in range(2 * TT):
                        add(2 * i + par, b)
                    for q in range(G):
                        low(2 * i + (2 + par), par, q)
            for r in (NR - 2, NR - 1):
                for b in range(2 * TT):
                    add(r, b)
                    if r == NR - 1 and b % 2:
                        stats_of(dve, b // 2)
                    if r == NR - 1 and b % 2 == 0 and b > 0:
                        norm(dve, b // 2 - 1)
            norm(dve, TT - 1)
            dve.wait_ge(sem("ld_ln"), START + 32)
            affine(nc.vector, dve, TT - 1, "final_last")

        @block.tensor
        def _(pe):
            def up(r, par, first=False):
                def add_chunk(b, q):
                    t, h, s = b // 2, b % 2, G * par + q
                    for m, (a, v) in enumerate(float32r_products(Ch, Cl, uh, ul)):
                        ins = nc.tensor.matmul(psy[b % NB][:], a[s][:, t * P:(t + 1) * P], v[s][:, h * HALF:(h + 1) * HALF],
                                               start=(q == 0 and m == 0), stop=(q == G - 1 and m == 2))
                    if q == G - 1:
                        ins.then_inc(sem("y_mm"), 1)

                if first:
                    for q in range(G):
                        pe.wait_ge(sem("C_lo"), START + q + 1)
                        for b in range(NB):
                            add_chunk(b, q)
                pe.wait_ge(sem("C_lo"), START + G * r + G)
                for b in range(NB if first else 0, 2 * TT):
                    pe.wait_ge(sem("y_add"), START + 16 * r + (b - NB + 1))
                    for q in range(G):
                        add_chunk(b, q)

            up(0, 0, first=True)
            up(1, 1)
            with pe.Fori(1, NR // 2) as i:
                for par in range(2):
                    up(2 * i + par, par)


def build_program(nc, g):
    def dram(name, shape):
        return nc.dram_tensor(name, shape, F32, kind="Internal").ap()

    g.hT = dram("hT", (N_IN, P, T))
    g.ba = dram("ba", (P, TT, 2 * DH))
    g.y = dram("y", (2 * AT, P, T))
    g.x1 = dram("x1", (T, D))
    g.s = dram("s", (TT, P, 2 * PH, PK))
    g.act = dram("act", (PK, P, T))
    g.W = dram("W", (PK, P, T))
    stage_project(nc, g)
    stage_attention(nc, g)
    stage_deltanet(nc, g)
    with nc.sbuf_tensor("x1h", [P, KD, T], F32R) as g.x1h, nc.sbuf_tensor("x1l", [P, KD, T], F32R) as g.x1l:
        with nc.sbuf_tensor("merged", [P, KD, T], F32) as g.merged:
            stage_merge(nc, g)
            stage_out_norm(nc, g)
        stage_scores(nc, g)
        stage_down_and_route(nc, g)
    stage_up(nc, g)


def host_constants():
    inv = (np.float32(10000.0) ** (-np.arange(0, AD, 2, dtype=np.float32) / np.float32(AD))).astype(np.float32)
    ang = (np.arange(T, dtype=np.float32)[:, None] * inv[None, :]).astype(np.float32)
    c, s = np.cos(ang).T, np.sin(ang).T
    d = np.arange(P)[:, None] - np.arange(T)[None, :] + (T - P)
    n = np.zeros(d.shape, np.float64)
    for window, r in ((128, 1), (512, 4), (2048, 16)):
        n += (d >= 0) & (d % r == 0) & (d <= window)
    bias = np.where(n > 0, np.log(np.maximum(n, 1.0)) * AD ** 0.5, NEG)
    i = np.arange(P)
    later = (i[None, :] >= i[:, None])
    level = np.zeros((P, 7, P), np.float32)
    for n in range(7):
        b = 1 << n
        same = (i[None, :] // (2 * b)) == (i[:, None] // (2 * b))
        level[:, n, :] = same & (i[:, None] // b % 2 == 0) & (i[None, :] // b % 2 == 1)
    return {
        "ident": np.eye(P, dtype=np.float32),
        "cos": np.ascontiguousarray(np.concatenate([c] * 4).astype(np.float32)),
        "sin": np.ascontiguousarray(np.concatenate([-s, s] * 2).astype(np.float32)),
        "bias": bias.astype(np.float32),
        "upto": later.astype(np.float32),
        "notlater": np.where(later, 0.0, NEG).astype(np.float32),
        "level": level,
        "iota": np.tile(np.arange(P, dtype=np.float32), (P, 1)),
    }


class Arrays:
    pass


def kernel(**inputs):
    import concourse.bacc as bacc
    from concourse.bass_utils import run_bass_kernel_spmd

    a = {k: np.asarray(v) for k, v in inputs.items()}
    w_in = a["w_in"][0]
    ba0 = 3 * AW + 3 * DW
    cols = np.r_[0:ba0, ba0 + 2 * DH:w_in.shape[1]]
    arrays = {
        "x": a["x"][0],
        "xT": a["x"][0].T,
        "w_in": w_in[:, cols].reshape(KD, P, N_IN, P).transpose(2, 1, 0, 3),
        "w_ba": w_in[:, ba0:ba0 + 2 * DH],
        "conv": a["dn_conv"][0].reshape(CONV, N_DN, P).transpose(2, 1, 0),
        "a_log": a["dn_A_log"][0],
        "dt_bias": a["dn_dt_bias"][0],
        "norm_gain": a["dn_norm_gain"][0][:, None],
        "w_branch": np.concatenate([a["w_branch_attn"][0], a["w_branch_delta"][0]]).reshape(2 * AT, P, KD, P).transpose(2, 1, 0, 3),
        "w_out": a["w_out"][0],
        "ln1_gain": a["ln1_gain"][0],
        "ln1_bias": a["ln1_bias"][0],
        "w_query": a["peer_w_query"][0].reshape(KD, P, 2 * PH, P).transpose(2, 1, 0, 3),
        "keys": a["peer_sub_keys"][0].reshape(2 * PH, PK, P).transpose(0, 2, 1),
        "down": a["peer_expert_down"][0].reshape(PK, PK, KD, P).transpose(1, 3, 2, 0),
        "up": a["peer_expert_up"][0].reshape(PK, PK, D).transpose(1, 0, 2),
        "ln2_gain": a["ln2_gain"][0],
        "ln2_bias": a["ln2_bias"][0],
        **host_constants(),
    }
    nc = bacc.Bacc("TRN2", target_bir_lowering=False, num_devices=1)
    g = Arrays()
    given = {}
    for name, v in arrays.items():
        v = np.ascontiguousarray(v)
        given[f"in_{name}"] = v
        g.__dict__[name] = nc.dram_tensor(f"in_{name}", v.shape, mybir.dt.from_np(v.dtype), kind="ExternalInput").ap()
    g.out = nc.dram_tensor("out", (T, D), F32, kind="ExternalOutput").ap()
    build_program(nc, g)
    r = run_bass_kernel_spmd(nc, [given], core_ids=[0])
    return r.results[0]["out"].reshape(1, T, D)
```
